# Optimizing a Trainium2 kernel written in Bass

```python
import jax
import jax.numpy as jnp
from jax import lax
import numpy as np
import math
import jax, jax.numpy as jnp

D_MODEL = 2048
BATCH = 1
SEQ = 256
DEPTH = 1

HEAD_DIM = 128
BRANCH_WIDTH = D_MODEL // 2
N_BRANCH = 3
PLE_DIM = 256
NORM_EPS = 1e-6

LRU_BLOCK = 64
LRU_BLOCKS = BRANCH_WIDTH // LRU_BLOCK
CONV_WIDTH = 4
LRU_C = 8.0

NSA_HEADS = BRANCH_WIDTH // HEAD_DIM
NSA_KV_HEADS = 2
NSA_GROUP = NSA_HEADS // NSA_KV_HEADS
NSA_KV_WIDTH = NSA_KV_HEADS * HEAD_DIM
CMP_BLOCK = 32
CMP_STRIDE = 16
CMP_HIDDEN = 256
SEL_BLOCK = 64
SEL_TOPK = 16
WINDOW = 512
NSA_Q_BLOCK = 32

FOX_HEADS = BRANCH_WIDTH // HEAD_DIM
FOX_Q_BLOCK = 128
FORGET_BIAS = 3.0

IN_SPLITS = (
    ('lru_x', BRANCH_WIDTH), ('lru_gate', BRANCH_WIDTH),
    ('nsa_q', BRANCH_WIDTH),
    ('nsa_k_cmp', NSA_KV_WIDTH), ('nsa_v_cmp', NSA_KV_WIDTH),
    ('nsa_k_slc', NSA_KV_WIDTH), ('nsa_v_slc', NSA_KV_WIDTH),
    ('nsa_k_win', NSA_KV_WIDTH), ('nsa_v_win', NSA_KV_WIDTH),
    ('nsa_bgate', NSA_HEADS * 3), ('nsa_gate', BRANCH_WIDTH),
    ('fox_q', BRANCH_WIDTH), ('fox_k', BRANCH_WIDTH), ('fox_v', BRANCH_WIDTH),
    ('fox_f', FOX_HEADS), ('fox_gate', BRANCH_WIDTH),
    ('merge', N_BRANCH * D_MODEL),
)
N_IN = sum(size for _, size in IN_SPLITS)


def column_offsets():
    offs, start = {}, 0
    for name, size in IN_SPLITS:
        offs[name] = (start, size)
        start += size
    return offs

def split_columns(z):
    return {name: z[..., s:s + n] for name, (s, n) in column_offsets().items()}

def split_heads(t, n_heads):
    b, s, _ = t.shape
    return t.reshape(b, s, n_heads, HEAD_DIM)

def rms_norm(x, gain):
    xf = x.astype(jnp.float32)
    y = xf * lax.rsqrt(jnp.mean(xf * xf, axis=-1, keepdims=True) + NORM_EPS)
    return (y * gain.astype(jnp.float32)).astype(x.dtype)

def masked_softmax(logits, mask):
    logits = jnp.where(mask, logits.astype(jnp.float32), -jnp.inf)
    m = jnp.max(logits, axis=-1, keepdims=True)
    m = jnp.where(jnp.isfinite(m), m, 0.0)
    e = jnp.exp(logits - m)
    return e / jnp.maximum(jnp.sum(e, axis=-1, keepdims=True), 1e-30)

def linear_combine(left, right):
    a_l, b_l = left
    a_r, b_r = right
    return a_l * a_r, a_r * b_l + b_r

def rglru_branch(u, conv_w, conv_b, wa, ba, wx, bx, lam):
    b, s, w = u.shape
    taps = conv_w[:, None, :].astype(u.dtype)
    uc = lax.conv_general_dilated(u, taps, (1,), ((CONV_WIDTH - 1, 0),),
                                  dimension_numbers=('NWC', 'WIO', 'NWC'),
                                  feature_group_count=w) + conv_b
    ub = uc.reshape(b, s, LRU_BLOCKS, LRU_BLOCK)
    rec = jax.nn.sigmoid((jnp.einsum('bsnk,nkj->bsnj', ub, wa).reshape(b, s, w) + ba).astype(jnp.float32))
    inp = jax.nn.sigmoid((jnp.einsum('bsnk,nkj->bsnj', ub, wx).reshape(b, s, w) + bx).astype(jnp.float32))
    log_a = -LRU_C * rec * jax.nn.softplus(-lam.astype(jnp.float32))
    a = jnp.exp(log_a)
    drive = jnp.sqrt(-jnp.expm1(2.0 * log_a)) * (inp * uc.astype(jnp.float32))
    _, hseq = lax.associative_scan(linear_combine, (a, drive), axis=1)
    return hseq.astype(u.dtype)

def compress(t, pos, w1, w2):
    b, s, hk, dk = t.shape
    n_chunk = s // CMP_STRIDE
    ratio = CMP_BLOCK // CMP_STRIDE
    n_cmp = n_chunk - ratio + 1
    chunks = t.reshape(b, n_chunk, CMP_STRIDE, hk, dk)
    blocks = jnp.concatenate([chunks[:, r:r + n_cmp] for r in range(ratio)], axis=2)
    blocks = blocks + pos[:, None, :]
    flat = blocks.transpose(0, 1, 3, 2, 4).reshape(b, n_cmp, hk, CMP_BLOCK * dk)
    return jax.nn.silu(flat @ w1) @ w2

def nsa_branch(q, kc, vc, ks, vs, kw, vw, gates):
    b, s, h, dk = q.shape
    scale = dk ** -0.5
    n_cmp = kc.shape[1]
    n_sel = s // SEL_BLOCK
    n_top = min(SEL_TOPK, n_sel)
    nb = s // NSA_Q_BLOCK
    cmp_start = jnp.arange(n_cmp) * CMP_STRIDE
    cmp_end = cmp_start + CMP_BLOCK - 1
    sel_ids = jnp.arange(n_sel)
    sel_start = sel_ids * SEL_BLOCK
    overlap = ((cmp_start[:, None] < sel_start[None, :] + SEL_BLOCK)
               & (cmp_start[:, None] + CMP_BLOCK > sel_start[None, :])).astype(jnp.float32)
    ks_blk = ks.reshape(b, n_sel, SEL_BLOCK, NSA_KV_HEADS, dk).transpose(0, 3, 1, 2, 4)
    vs_blk = vs.reshape(b, n_sel, SEL_BLOCK, NSA_KV_HEADS, dk).transpose(0, 3, 1, 2, 4)
    bi = jnp.arange(b)[:, None, None, None]
    gi = jnp.arange(NSA_KV_HEADS)[None, None, :, None]
    pad = ((0, 0), (WINDOW, 0), (0, 0), (0, 0))
    kw_pad = jnp.pad(kw, pad)
    vw_pad = jnp.pad(vw, pad)
    win_off = jnp.arange(WINDOW + NSA_Q_BLOCK) - WINDOW
    q_blocks = q.reshape(b, nb, NSA_Q_BLOCK, NSA_KV_HEADS, NSA_GROUP, dk).swapaxes(0, 1)
    g_blocks = gates.reshape(b, nb, NSA_Q_BLOCK, NSA_KV_HEADS, NSA_GROUP, 3).swapaxes(0, 1)
    t0s = jnp.arange(nb, dtype=jnp.int32) * NSA_Q_BLOCK
    flat_sel = n_top * SEL_BLOCK

    def block(args):
        qb, gb, t0 = args
        tq = t0 + jnp.arange(NSA_Q_BLOCK)
        s_c = jnp.einsum('btgqd,bcgd->btgqc', qb, kc) * scale
        m_c = (cmp_end[None, :] <= tq[:, None])[None, :, None, None, :]
        p_c = masked_softmax(s_c, m_c)
        o_c = jnp.einsum('btgqc,bcgd->btgqd', p_c.astype(vc.dtype), vc)
        imp = jnp.einsum('btgqc,cj->btgj', p_c, overlap)
        cur = (tq // SEL_BLOCK)[:, None]
        valid = sel_ids[None, :] <= cur
        forced = (sel_ids[None, :] == 0) | (sel_ids[None, :] == cur) | (sel_ids[None, :] == cur - 1)
        score = jnp.where(forced[None, :, None, :], jnp.inf,
                          jnp.where(valid[None, :, None, :], imp, -jnp.inf))
        _, idx = lax.top_k(score, n_top)
        k_sel = ks_blk[bi, gi, idx]
        v_sel = vs_blk[bi, gi, idx]
        s_s = jnp.einsum('btgqd,btgnkd->btgqnk', qb, k_sel) * scale
        kpos = idx[..., None] * SEL_BLOCK + jnp.arange(SEL_BLOCK)
        m_s = kpos <= tq[None, :, None, None, None]
        p_s = masked_softmax(s_s.reshape(b, NSA_Q_BLOCK, NSA_KV_HEADS, NSA_GROUP, flat_sel),
                             m_s.reshape(b, NSA_Q_BLOCK, NSA_KV_HEADS, 1, flat_sel))
        o_s = jnp.einsum('btgqm,btgmd->btgqd', p_s.astype(vs.dtype),
                         v_sel.reshape(b, NSA_Q_BLOCK, NSA_KV_HEADS, flat_sel, dk))
        k_w = lax.dynamic_slice_in_dim(kw_pad, t0, WINDOW + NSA_Q_BLOCK, axis=1)
        v_w = lax.dynamic_slice_in_dim(vw_pad, t0, WINDOW + NSA_Q_BLOCK, axis=1)
        wpos = t0 + win_off
        m_w = ((wpos[None, :] >= 0) & (wpos[None, :] <= tq[:, None])
               & (wpos[None, :] > tq[:, None] - WINDOW))[None, :, None, None, :]
        s_w = jnp.einsum('btgqd,bkgd->btgqk', qb, k_w) * scale
        p_w = masked_softmax(s_w, m_w)
        o_w = jnp.einsum('btgqk,bkgd->btgqd', p_w.astype(vw.dtype), v_w)
        return gb[..., 0:1] * o_c + gb[..., 1:2] * o_s + gb[..., 2:3] * o_w

    out = lax.map(block, (q_blocks, g_blocks, t0s))
    return out.swapaxes(0, 1).reshape(b, s, h * dk)

def fox_branch(q, k, v, log_f):
    b, s, h, dk = q.shape
    scale = dk ** -0.5
    nb = s // FOX_Q_BLOCK
    c = jnp.cumsum(log_f, axis=1)
    ck = c.transpose(0, 2, 1)
    kpos = jnp.arange(s)
    q_blocks = q.reshape(b, nb, FOX_Q_BLOCK, h, dk).swapaxes(0, 1)
    c_blocks = c.reshape(b, nb, FOX_Q_BLOCK, h).swapaxes(0, 1)
    t0s = jnp.arange(nb, dtype=jnp.int32) * FOX_Q_BLOCK

    def block(args):
        qb, cb, t0 = args
        tq = t0 + jnp.arange(FOX_Q_BLOCK)
        logits = jnp.einsum('bqhd,bkhd->bhqk', qb, k).astype(jnp.float32) * scale
        logits = logits + (cb.transpose(0, 2, 1)[..., None] - ck[:, :, None, :])
        p_att = masked_softmax(logits, kpos[None, :] <= tq[:, None])
        return jnp.einsum('bhqk,bkhd->bqhd', p_att.astype(v.dtype), v)

    out = lax.map(block, (q_blocks, c_blocks, t0s))
    return out.swapaxes(0, 1).reshape(b, s, h * dk)

def first_inputs(seed: int = 0) -> dict:
    key = jax.random.key(seed)
    ks = jax.random.split(key, 26)
    f32 = jnp.float32

    def nrm(k, shape, fan_in):
        return jax.random.normal(k, shape, f32) * (fan_in ** -0.5)

    def gain(k, shape):
        return 1.0 + 0.05 * jax.random.normal(k, shape, f32)

    def small(k, shape):
        return 0.02 * jax.random.normal(k, shape, f32)

    x = jax.random.normal(ks[0], (BATCH, SEQ, D_MODEL), f32)
    p = jax.random.normal(ks[1], (DEPTH, BATCH, SEQ, PLE_DIM), f32)
    ln_gain = gain(ks[2], (DEPTH, D_MODEL))
    w_in = nrm(ks[3], (DEPTH, D_MODEL, N_IN), D_MODEL)
    f_off = column_offsets()['fox_f'][0]
    b_in = small(ks[4], (DEPTH, N_IN)).at[:, f_off:f_off + FOX_HEADS].add(FORGET_BIAS)
    conv_w = nrm(ks[5], (DEPTH, CONV_WIDTH, BRANCH_WIDTH), CONV_WIDTH)
    conv_b = small(ks[6], (DEPTH, BRANCH_WIDTH))
    lru_wa = nrm(ks[7], (DEPTH, LRU_BLOCKS, LRU_BLOCK, LRU_BLOCK), LRU_BLOCK)
    lru_ba = small(ks[8], (DEPTH, BRANCH_WIDTH))
    lru_wx = nrm(ks[9], (DEPTH, LRU_BLOCKS, LRU_BLOCK, LRU_BLOCK), LRU_BLOCK)
    lru_bx = small(ks[10], (DEPTH, BRANCH_WIDTH))
    a0 = jax.random.uniform(ks[11], (DEPTH, BRANCH_WIDTH), f32, minval=0.9, maxval=0.999)
    root = a0 ** (1.0 / LRU_C)
    lru_lambda = jnp.log(root) - jnp.log1p(-root)
    cmp_w1 = nrm(ks[12], (DEPTH, 2, CMP_BLOCK * HEAD_DIM, CMP_HIDDEN), CMP_BLOCK * HEAD_DIM)
    cmp_w2 = nrm(ks[13], (DEPTH, 2, CMP_HIDDEN, HEAD_DIM), CMP_HIDDEN)
    cmp_pos = small(ks[14], (DEPTH, 2, CMP_BLOCK, HEAD_DIM))
    nsa_q_gain = gain(ks[15], (DEPTH, HEAD_DIM))
    nsa_k_gain = gain(ks[16], (DEPTH, HEAD_DIM))
    fox_q_gain = gain(ks[17], (DEPTH, HEAD_DIM))
    fox_k_gain = gain(ks[18], (DEPTH, HEAD_DIM))
    w_branch = nrm(ks[19], (DEPTH, N_BRANCH, BRANCH_WIDTH, D_MODEL), BRANCH_WIDTH)
    w_out = nrm(ks[20], (DEPTH, D_MODEL, D_MODEL), D_MODEL)
    w_ple = nrm(ks[21], (DEPTH, PLE_DIM, D_MODEL), PLE_DIM)
    ple_gain = gain(ks[22], (DEPTH, D_MODEL))
    w_ple_gate = nrm(ks[23], (DEPTH, D_MODEL, D_MODEL), D_MODEL)
    return {'x': x, 'p': p, 'ln_gain': ln_gain, 'w_in': w_in, 'b_in': b_in,
            'conv_w': conv_w, 'conv_b': conv_b, 'lru_wa': lru_wa, 'lru_ba': lru_ba,
            'lru_wx': lru_wx, 'lru_bx': lru_bx, 'lru_lambda': lru_lambda,
            'cmp_w1': cmp_w1, 'cmp_w2': cmp_w2, 'cmp_pos': cmp_pos,
            'nsa_q_gain': nsa_q_gain, 'nsa_k_gain': nsa_k_gain,
            'fox_q_gain': fox_q_gain, 'fox_k_gain': fox_k_gain,
            'w_branch': w_branch, 'w_out': w_out, 'w_ple': w_ple,
            'ple_gain': ple_gain, 'w_ple_gate': w_ple_gate}

def first_block(x, p, ln_gain, w_in, b_in, conv_w, conv_b, lru_wa, lru_ba, lru_wx, lru_bx,
              lru_lambda, cmp_w1, cmp_w2, cmp_pos, nsa_q_gain, nsa_k_gain, fox_q_gain,
              fox_k_gain, w_branch, w_out, w_ple, ple_gain, w_ple_gate):
    b, s, _ = x.shape
    h = x
    for l in range(DEPTH):
        hn = rms_norm(h, ln_gain[l])
        z = split_columns(hn @ w_in[l] + b_in[l])
        y_a = rglru_branch(z['lru_x'], conv_w[l], conv_b[l], lru_wa[l], lru_ba[l],
                           lru_wx[l], lru_bx[l], lru_lambda[l]) * jax.nn.silu(z['lru_gate'])
        q_b = rms_norm(split_heads(z['nsa_q'], NSA_HEADS), nsa_q_gain[l])
        k_c = rms_norm(compress(split_heads(z['nsa_k_cmp'], NSA_KV_HEADS), cmp_pos[l, 0],
                                cmp_w1[l, 0], cmp_w2[l, 0]), nsa_k_gain[l])
        v_c = compress(split_heads(z['nsa_v_cmp'], NSA_KV_HEADS), cmp_pos[l, 1],
                       cmp_w1[l, 1], cmp_w2[l, 1])
        k_s = rms_norm(split_heads(z['nsa_k_slc'], NSA_KV_HEADS), nsa_k_gain[l])
        v_s = split_heads(z['nsa_v_slc'], NSA_KV_HEADS)
        k_w = rms_norm(split_heads(z['nsa_k_win'], NSA_KV_HEADS), nsa_k_gain[l])
        v_w = split_heads(z['nsa_v_win'], NSA_KV_HEADS)
        g_b = jax.nn.sigmoid(z['nsa_bgate']).reshape(b, s, NSA_HEADS, 3)
        y_b = nsa_branch(q_b, k_c, v_c, k_s, v_s, k_w, v_w, g_b) * jax.nn.silu(z['nsa_gate'])
        log_f = jax.nn.log_sigmoid(z['fox_f'].astype(jnp.float32))
        y_c = fox_branch(rms_norm(split_heads(z['fox_q'], FOX_HEADS), fox_q_gain[l]),
                         rms_norm(split_heads(z['fox_k'], FOX_HEADS), fox_k_gain[l]),
                         split_heads(z['fox_v'], FOX_HEADS), log_f) * jax.nn.silu(z['fox_gate'])
        mg = jax.nn.sigmoid(z['merge']).reshape(b, s, N_BRANCH, D_MODEL)
        merged = (mg[:, :, 0] * (y_a @ w_branch[l, 0])
                  + mg[:, :, 1] * (y_b @ w_branch[l, 1])
                  + mg[:, :, 2] * (y_c @ w_branch[l, 2]))
        h = h + merged @ w_out[l]
        e = rms_norm(p[l] @ w_ple[l], ple_gain[l])
        h = h + jax.nn.sigmoid(h @ w_ple_gate[l]) * e
    return h


CTX_LEN = 256
GRID_W = 64
EPS = 1e-6

MLA_HEADS = 8
MLA_Q_RANK = 512
MLA_KV_RANK = 256
MLA_NOPE = 128
MLA_ROPE = 64
MLA_V = 128
MLA_SCALE = (MLA_NOPE + MLA_ROPE) ** -0.5
ROPE_BASE = 10000.0
Q_BLOCK = 128

DN_HEADS = 8
DN_DK = 128
DN_DV = 128
DN_QKV = DN_HEADS * (2 * DN_DK + DN_DV)
CONV_W = 5
CHUNK = 64

PEER_HEADS = 8
PEER_KEYS = 128
PEER_EXPERTS = PEER_KEYS * PEER_KEYS
PEER_QDIM = 256
PEER_TOPK = 16
PEER_BLOCK = 64

IN_SIZES = (MLA_Q_RANK, MLA_KV_RANK, MLA_ROPE, DN_QKV, DN_HEADS * DN_DV,
            DN_HEADS, DN_HEADS, DN_HEADS, DN_HEADS, D_MODEL, D_MODEL)
D_IN = sum(IN_SIZES)
IN_POINTS = tuple(int(p) for p in np.cumsum(IN_SIZES)[:-1])


def rmsnorm(x, w):
    xf = x.astype(jnp.float32)
    y = xf * lax.rsqrt(jnp.mean(xf * xf, axis=-1, keepdims=True) + EPS)
    return (y * w.astype(jnp.float32)).astype(x.dtype)

def modulate(x, w, shift, scale):
    return rmsnorm(x, w) * (1 + scale) + shift

def l2norm(x):
    xf = x.astype(jnp.float32)
    return xf * lax.rsqrt(jnp.sum(xf * xf, axis=-1, keepdims=True) + EPS)

def grid_angles(n):
    n_rows = n // GRID_W
    rows = jnp.repeat(jnp.arange(n_rows, dtype=jnp.float32), GRID_W)
    cols = jnp.tile(jnp.arange(GRID_W, dtype=jnp.float32), n_rows)
    axis_dim = MLA_ROPE // 2
    inv_freq = ROPE_BASE ** (-jnp.arange(0, axis_dim, 2, dtype=jnp.float32) / axis_dim)
    return rows[:, None] * inv_freq, cols[:, None] * inv_freq

def rotate(x, ang):
    x1, x2 = jnp.split(x.astype(jnp.float32), 2, axis=-1)
    cos, sin = jnp.cos(ang), jnp.sin(ang)
    return jnp.concatenate([x1 * cos - x2 * sin, x1 * sin + x2 * cos], axis=-1).astype(x.dtype)

def axial_rope(x, ang_r, ang_c):
    xr, xc = jnp.split(x, 2, axis=-1)
    return jnp.concatenate([rotate(xr, ang_r), rotate(xc, ang_c)], axis=-1)

def mla_heads(c_q, c_kv, q_norm_w, kv_norm_w, w_uq, w_ukv):
    b, n = c_q.shape[:2]
    q = (rmsnorm(c_q, q_norm_w) @ w_uq).reshape(b, n, MLA_HEADS, MLA_NOPE + MLA_ROPE)
    kv = (rmsnorm(c_kv, kv_norm_w) @ w_ukv).reshape(b, n, MLA_HEADS, MLA_NOPE + MLA_V)
    return q[..., :MLA_NOPE], q[..., MLA_NOPE:], kv[..., :MLA_NOPE], kv[..., MLA_NOPE:]

def mla_attend(q_nope, q_rope, k_nope, k_rope, v):
    s = (jnp.einsum('bthd,blhd->bhtl', q_nope, k_nope)
         + jnp.einsum('bthr,blr->bhtl', q_rope, k_rope))
    p = jax.nn.softmax(s.astype(jnp.float32) * MLA_SCALE, axis=-1).astype(v.dtype)
    o = jnp.einsum('bhtl,blhd->bthd', p, v)
    return o.reshape(o.shape[0], o.shape[1], MLA_HEADS * MLA_V)

def short_conv(x, w):
    c = x.shape[-1]
    return lax.conv_general_dilated(
        x, w[:, None, :].astype(x.dtype), window_strides=(1,),
        padding=[(CONV_W // 2, CONV_W // 2)],
        dimension_numbers=('NWC', 'WIO', 'NWC'), feature_group_count=c)

def dn_qkv(qkv, conv_w):
    b, n = qkv.shape[:2]
    y = jax.nn.silu(short_conv(qkv, conv_w))
    q, k, v = jnp.split(y, [DN_HEADS * DN_DK, 2 * DN_HEADS * DN_DK], axis=-1)
    q = l2norm(q.reshape(b, n, DN_HEADS, DN_DK)) * DN_DK ** -0.5
    k = l2norm(k.reshape(b, n, DN_HEADS, DN_DK))
    v = v.reshape(b, n, DN_HEADS, DN_DV).astype(jnp.float32)
    return q, k, v

def dn_decay(a, beta_logit, a_log, dt_bias):
    g = -jnp.exp(a_log.astype(jnp.float32)) * jax.nn.softplus(a.astype(jnp.float32) + dt_bias.astype(jnp.float32))
    return g, jax.nn.sigmoid(beta_logit.astype(jnp.float32))

def gated_delta_chunked(q, k, v, g, beta, s0):
    b, n, h, _ = q.shape
    dv = v.shape[-1]
    nc = n // CHUNK

    def chunks(t):
        return t.reshape(b, nc, CHUNK, h, -1).transpose(0, 3, 1, 2, 4)

    q, k, v = chunks(q), chunks(k), chunks(v)
    g = g.reshape(b, nc, CHUNK, h).transpose(0, 3, 1, 2)
    beta = beta.reshape(b, nc, CHUNK, h).transpose(0, 3, 1, 2)
    gc = jnp.cumsum(g, axis=-1)
    incl = jnp.tril(jnp.ones((CHUNK, CHUNK), dtype=bool))
    strict = jnp.tril(jnp.ones((CHUNK, CHUNK), dtype=bool), -1)
    decay = jnp.exp(jnp.where(incl, gc[..., :, None] - gc[..., None, :], -jnp.inf))
    kb = k * beta[..., None]
    m = jnp.where(strict, jnp.einsum('bhnid,bhnjd->bhnij', kb, k) * decay, 0.0)
    rhs = jnp.concatenate([v * beta[..., None], kb * jnp.exp(gc)[..., None]], axis=-1)
    sol = lax.linalg.triangular_solve(m + jnp.eye(CHUNK, dtype=m.dtype), rhs,
                                      left_side=True, lower=True, unit_diagonal=True)
    u, w = sol[..., :dv], sol[..., dv:]
    attn = jnp.where(incl, jnp.einsum('bhnid,bhnjd->bhnij', q, k) * decay, 0.0)
    g_last = gc[..., -1]

    def step(state, xs):
        q_i, k_i, u_i, w_i, a_i, gc_i, gl_i = xs
        v_new = u_i - jnp.einsum('bhck,bhkv->bhcv', w_i, state)
        o_i = (jnp.einsum('bhck,bhkv->bhcv', q_i * jnp.exp(gc_i)[..., None], state)
               + jnp.einsum('bhij,bhjv->bhiv', a_i, v_new))
        k_dec = k_i * jnp.exp(gl_i[..., None] - gc_i)[..., None]
        state = state * jnp.exp(gl_i)[..., None, None] + jnp.einsum('bhck,bhcv->bhkv', k_dec, v_new)
        return state, o_i

    xs = tuple(jnp.moveaxis(t, 2, 0) for t in (q, k, u, w, attn, gc, g_last))
    state, o = lax.scan(step, s0, xs)
    o = o.transpose(1, 0, 3, 2, 4).reshape(b, n, h, dv)
    return o, state

def flip(t):
    return t[:, ::-1]

def dn_gated_out(o, z, norm_w):
    b, n = z.shape[:2]
    o = rmsnorm(o, norm_w) * jax.nn.silu(z.reshape(b, n, DN_HEADS, DN_DV).astype(jnp.float32))
    return o.reshape(b, n, DN_HEADS * DN_DV).astype(z.dtype)

def token_mixer(h, hc, w_in, q_norm_w, kv_norm_w, w_uq, w_ukv, conv_w, a_log, dt_bias,
                dn_norm_w, w_branch_a, w_branch_b, w_out, with_ctx_out):
    b, n, _ = h.shape
    (cq, ckv, kr, qkv, z, a_f, a_b, b_f, b_b, gate_a, gate_b) = jnp.split(h @ w_in, IN_POINTS, axis=-1)
    (cq_c, ckv_c, kr_c, qkv_c, z_c, a_f_c, a_b_c, b_f_c, b_b_c,
     gate_a_c, gate_b_c) = jnp.split(hc @ w_in, IN_POINTS, axis=-1)

    ang_r, ang_c = grid_angles(n)
    qn, qr, kn, v = mla_heads(cq, ckv, q_norm_w, kv_norm_w, w_uq, w_ukv)
    qr = axial_rope(qr, ang_r[:, None, :], ang_c[:, None, :])
    kr = axial_rope(kr, ang_r, ang_c)
    qn_c, qr_c, kn_c, v_c = mla_heads(cq_c, ckv_c, q_norm_w, kv_norm_w, w_uq, w_ukv)
    kn_all = jnp.concatenate([kn_c, kn], axis=1)
    kr_all = jnp.concatenate([kr_c, kr], axis=1)
    v_all = jnp.concatenate([v_c, v], axis=1)
    nb = n // Q_BLOCK

    def to_blocks(t):
        return jnp.swapaxes(t.reshape(b, nb, Q_BLOCK, *t.shape[2:]), 0, 1)

    y_a = lax.map(lambda qs: mla_attend(qs[0], qs[1], kn_all, kr_all, v_all), (to_blocks(qn), to_blocks(qr)))
    y_a = jnp.swapaxes(y_a, 0, 1).reshape(b, n, MLA_HEADS * MLA_V)

    ql, kl, vl = dn_qkv(qkv, conv_w)
    qc, kc, vc = dn_qkv(qkv_c, conv_w)
    g_lf, be_lf = dn_decay(a_f, b_f, a_log[0], dt_bias[0])
    g_lb, be_lb = dn_decay(a_b, b_b, a_log[1], dt_bias[1])
    g_cf, be_cf = dn_decay(a_f_c, b_f_c, a_log[0], dt_bias[0])
    g_cb, be_cb = dn_decay(a_b_c, b_b_c, a_log[1], dt_bias[1])
    s0 = jnp.zeros((b, DN_HEADS, DN_DK, DN_DV), jnp.float32)
    o_cf, s_cf = gated_delta_chunked(qc, kc, vc, g_cf, be_cf, s0)
    o_lf, _ = gated_delta_chunked(ql, kl, vl, g_lf, be_lf, s_cf)
    o_cb, s_cb = gated_delta_chunked(flip(qc), flip(kc), flip(vc), flip(g_cb), flip(be_cb), s0)
    o_lb, _ = gated_delta_chunked(flip(ql), flip(kl), flip(vl), flip(g_lb), flip(be_lb), s_cb)
    y_b = dn_gated_out(o_lf + flip(o_lb), z, dn_norm_w)

    def merge(ya, yb, ga, gb):
        return (jax.nn.sigmoid(ga) * (ya @ w_branch_a) + jax.nn.sigmoid(gb) * (yb @ w_branch_b)) @ w_out

    y = merge(y_a, y_b, gate_a, gate_b)
    if not with_ctx_out:
        return y, None
    y_a_c = mla_attend(qn_c, qr_c, kn_c, kr_c, v_c)
    y_b_c = dn_gated_out(o_cf + flip(o_cb), z_c, dn_norm_w)
    return y, merge(y_a_c, y_b_c, gate_a_c, gate_b_c)

def peer_ffn(h, w_q, sub_keys, u, v):
    b, n, d = h.shape
    nb = (b * n) // PEER_BLOCK
    hb = h.reshape(nb, PEER_BLOCK, d)

    def block(hx):
        t = hx.shape[0]
        q = (hx @ w_q).reshape(t, PEER_HEADS, 2, PEER_QDIM // 2).astype(jnp.float32)
        s = jnp.einsum('thpd,pkd->thpk', q, sub_keys.astype(jnp.float32))
        top_s, top_i = lax.top_k(s, PEER_TOPK)
        cand = top_s[:, :, 0, :, None] + top_s[:, :, 1, None, :]
        cand_idx = top_i[:, :, 0, :, None] * PEER_KEYS + top_i[:, :, 1, None, :]
        best_s, best_pos = lax.top_k(cand.reshape(t, PEER_HEADS, -1), PEER_TOPK)
        idx = jnp.take_along_axis(cand_idx.reshape(t, PEER_HEADS, -1), best_pos, axis=-1)
        wts = jax.nn.softmax(best_s, axis=-1).astype(hx.dtype)
        act = jax.nn.gelu(jnp.einsum('td,thkd->thk', hx, u[idx]), approximate=False)
        return jnp.einsum('thk,thkd->td', wts * act, v[idx])

    return lax.map(block, hb).reshape(b, n, d)

def second_inputs(seed: int = 0) -> dict:
    key = jax.random.key(seed)
    ks = jax.random.split(key, 26)
    f32 = jnp.float32
    L, D = DEPTH, D_MODEL

    def nrm(k, shape, scale=1.0):
        return jax.random.normal(k, shape, f32) * scale

    dt = jnp.exp(jax.random.uniform(ks[14], (L, 2, DN_HEADS), f32, math.log(1e-3), math.log(1e-1)))
    return {
        'x': nrm(ks[0], (BATCH, SEQ, D)),
        'c': nrm(ks[1], (BATCH, D)),
        'ctx': nrm(ks[2], (BATCH, CTX_LEN, D)),
        'c_ctx': nrm(ks[3], (D,)),
        'w_mod': nrm(ks[4], (L, D, 6 * D), 0.5 * D ** -0.5),
        'b_mod': nrm(ks[5], (L, 6 * D), 0.02),
        'norm1_w': 1.0 + nrm(ks[6], (L, D), 0.1),
        'w_in': nrm(ks[7], (L, D, D_IN), D ** -0.5),
        'mla_q_norm_w': 1.0 + nrm(ks[8], (L, MLA_Q_RANK), 0.1),
        'mla_kv_norm_w': 1.0 + nrm(ks[9], (L, MLA_KV_RANK), 0.1),
        'w_uq': nrm(ks[10], (L, MLA_Q_RANK, MLA_HEADS * (MLA_NOPE + MLA_ROPE)), MLA_Q_RANK ** -0.5),
        'w_ukv': nrm(ks[11], (L, MLA_KV_RANK, MLA_HEADS * (MLA_NOPE + MLA_V)), MLA_KV_RANK ** -0.5),
        'dn_conv_w': nrm(ks[12], (L, CONV_W, DN_QKV), CONV_W ** -0.5),
        'dn_a_log': jnp.log(jax.random.uniform(ks[13], (L, 2, DN_HEADS), f32, 1.0, 16.0)),
        'dn_dt_bias': dt + jnp.log(-jnp.expm1(-dt)),
        'dn_norm_w': 1.0 + nrm(ks[15], (L, DN_DV), 0.1),
        'w_branch_a': nrm(ks[16], (L, MLA_HEADS * MLA_V, D), (MLA_HEADS * MLA_V) ** -0.5),
        'w_branch_b': nrm(ks[17], (L, DN_HEADS * DN_DV, D), (DN_HEADS * DN_DV) ** -0.5),
        'w_out': nrm(ks[18], (L, D, D), D ** -0.5),
        'norm2_w': 1.0 + nrm(ks[19], (L, D), 0.1),
        'peer_w_q': nrm(ks[20], (L, D, PEER_HEADS * PEER_QDIM), D ** -0.5),
        'peer_sub_keys': nrm(ks[21], (L, 2, PEER_KEYS, PEER_QDIM // 2), (PEER_QDIM // 2) ** -0.5),
        'peer_u': nrm(ks[22], (L, PEER_EXPERTS, D), D ** -0.5),
        'peer_v': nrm(ks[23], (L, PEER_EXPERTS, D), PEER_HEADS ** -0.5),
        'final_norm_w': 1.0 + nrm(ks[24], (D,), 0.1),
    }

def second_block(x, c, ctx, c_ctx, w_mod, b_mod, norm1_w, w_in, mla_q_norm_w, mla_kv_norm_w,
              w_uq, w_ukv, dn_conv_w, dn_a_log, dn_dt_bias, dn_norm_w, w_branch_a, w_branch_b,
              w_out, norm2_w, peer_w_q, peer_sub_keys, peer_u, peer_v, final_norm_w):
    silu_c = jax.nn.silu(c)
    silu_cc = jax.nn.silu(c_ctx)
    for i in range(DEPTH):
        last = i == DEPTH - 1
        mod = (silu_c @ w_mod[i] + b_mod[i])[:, None, :]
        sh1, sc1, g1, sh2, sc2, g2 = jnp.split(mod, 6, axis=-1)
        mod_c = silu_cc @ w_mod[i] + b_mod[i]
        shc1, scc1, gc1, shc2, scc2, gc2 = jnp.split(mod_c, 6, axis=-1)
        h = modulate(x, norm1_w[i], sh1, sc1)
        hc = modulate(ctx, norm1_w[i], shc1, scc1)
        y, yc = token_mixer(h, hc, w_in[i], mla_q_norm_w[i], mla_kv_norm_w[i], w_uq[i], w_ukv[i],
                            dn_conv_w[i], dn_a_log[i], dn_dt_bias[i], dn_norm_w[i],
                            w_branch_a[i], w_branch_b[i], w_out[i], not last)
        x = x + g1 * y
        x = x + g2 * peer_ffn(modulate(x, norm2_w[i], sh2, sc2), peer_w_q[i], peer_sub_keys[i], peer_u[i], peer_v[i])
        if not last:
            ctx = ctx + gc1 * yc
            ctx = ctx + gc2 * peer_ffn(modulate(ctx, norm2_w[i], shc2, scc2), peer_w_q[i], peer_sub_keys[i], peer_u[i], peer_v[i])
    return rmsnorm(x, final_norm_w)


def setup_inputs(seed=0):
    out = dict(first_inputs(seed))
    for name, value in second_inputs(seed + 1).items():
        if name != "x":
            out[name + "_2"] = value
    return out


def reference(
    x, p, ln_gain, w_in, b_in, conv_w, conv_b, lru_wa, lru_ba, lru_wx, lru_bx, lru_lambda,
    cmp_w1, cmp_w2, cmp_pos, nsa_q_gain, nsa_k_gain, fox_q_gain, fox_k_gain, w_branch, w_out,
    w_ple, ple_gain, w_ple_gate, c_2, ctx_2, c_ctx_2, w_mod_2, b_mod_2, norm1_w_2, w_in_2,
    mla_q_norm_w_2, mla_kv_norm_w_2, w_uq_2, w_ukv_2, dn_conv_w_2, dn_a_log_2, dn_dt_bias_2,
    dn_norm_w_2, w_branch_a_2, w_branch_b_2, w_out_2, norm2_w_2, peer_w_q_2, peer_sub_keys_2,
    peer_u_2, peer_v_2, final_norm_w_2,
):
    x = first_block(
        x, p, ln_gain, w_in, b_in, conv_w, conv_b, lru_wa, lru_ba, lru_wx, lru_bx, lru_lambda,
        cmp_w1, cmp_w2, cmp_pos, nsa_q_gain, nsa_k_gain, fox_q_gain, fox_k_gain, w_branch,
        w_out, w_ple, ple_gain, w_ple_gate,
    )
    return second_block(
        x, c_2, ctx_2, c_ctx_2, w_mod_2, b_mod_2, norm1_w_2, w_in_2, mla_q_norm_w_2,
        mla_kv_norm_w_2, w_uq_2, w_ukv_2, dn_conv_w_2, dn_a_log_2, dn_dt_bias_2, dn_norm_w_2,
        w_branch_a_2, w_branch_b_2, w_out_2, norm2_w_2, peer_w_q_2, peer_sub_keys_2, peer_u_2,
        peer_v_2, final_norm_w_2,
    )


_drawn_inputs = setup_inputs


def setup_inputs(seed=0):
    import zlib

    import numpy as np

    out = dict(_drawn_inputs(seed))
    spreads = {}
    factors = {'ln_gain': 3.172,
     'lru_ba': 8.0,
     'lru_bx': 8.0,
     'cmp_pos': 8.0,
     'nsa_q_gain': 8.0,
     'nsa_k_gain': 8.0,
     'fox_q_gain': 8.0,
     'fox_k_gain': 8.0,
     'ctx_2': 4.276,
     'c_ctx_2': 2.815,
     'b_mod_2': 4.635,
     'norm1_w_2': 3.545,
     'mla_q_norm_w_2': 8.0,
     'mla_kv_norm_w_2': 8.0,
     'w_uq_2': 4.117,
     'dn_a_log_2': 2.78,
     'dn_norm_w_2': 6.657,
     'norm2_w_2': 15.319,
     'ple_gain': 3.44}
    for name, (base, spread) in spreads.items():
        noise = np.random.default_rng([zlib.crc32(name.encode()), seed]).standard_normal(out[name].shape)
        drawn = base * np.exp(spread * noise) if base else spread * noise
        out[name] = jnp.asarray(drawn.astype(out[name].dtype))
    for name, factor in factors.items():
        out[name] = (out[name] * factor).astype(out[name].dtype)
    return out
```

```python
from contextlib import ExitStack

import numpy as np

import concourse.bass as bass
from concourse import mybir

F32 = mybir.dt.float32
U32 = mybir.dt.uint32
ACT = mybir.ActivationFunctionType
ALU = mybir.AluOpType
AX_X = mybir.AxisListType.X

P = 128
T = 256
NT = T // P
D = 2048
DC = D // P
BW = 1024
BC = BW // P
EPS = 1e-6
BIG = 1e30
GUARD = 1e20
SCALE = P ** -0.5
MLA_SCALE = 192 ** -0.5
NCMP = 15
KEYS = 128
TOPK = 16
SLOTS = 4
SLOTW = 3072
GROUP = 4
SOFTPLUS_TERMS = 8

(Z_LRU, Z_NQ, Z_KS, Z_KW, Z_FQ, Z_FK, Z_VS, Z_VW, Z_FV, Z_KC, Z_VC, Z_GB, Z_LG, Z_NG, Z_FG, N_Z) = (
    0, 8, 16, 18, 20, 28, 36, 38, 40, 48, 50, 52, 53, 61, 69, 77)
N_QK = Z_VS - Z_NQ

(Y_KV, Y_K, Y_V, Y_KR, Y_AB, N_Y) = (0, 2, 10, 18, 19, 20)
(L_CQ, L_Q, L_Z, N_L) = (0, 4, 12, 20)


def layout(*sizes):
    at, out = 0, {}
    for name, n in sizes:
        out[name] = (at, n)
        at += n
    return out, at


PARAMS, N_PARAMS = layout(
    ("b_merge", 48), ("lru_ba", 8), ("lru_bx", 8), ("eps", 1), ("ln_gain", 16), ("b_in", N_Z), ("conv_w", 32),
    ("conv_b", 8), ("lam", 8), ("pos", 64), ("qk_gain", N_QK), ("cmp_gain", 1), ("ple_gain", 16), ("b_mod", 96),
    ("norm1", 16), ("q_norm", 4), ("kv_norm", 2), ("conv2_w", 120), ("a_log", 1), ("dt_bias", 1), ("dn_norm", 1),
    ("norm2", 16), ("final_norm", 16), ("cond", 32))
CONSTS, N_CONSTS = layout(
    ("ident", 128), ("ones", 128), ("causal", 384), ("cmp_mask", 32), ("upto", 128), ("cos", 256), ("sin", 256),
    ("rot", 128), ("dup", 128), ("duprot", 128))
DN_CONSTS, N_DN_CONSTS = layout(
    ("le", 128), ("ge", 128), ("lt", 128), ("gt", 128), ("chunk", 128), ("half0", 128), ("half1", 128),
    ("level", 6 * 128), ("level_t", 6 * 128))
PEER_CONSTS, N_PEER_CONSTS = layout(("iota", 128), ("same_head", 128))
MISC, N_MISC = layout(("cmp_w2", 512), ("sub_keys", 256))

N_MOD = 96
STREAMS = (("z", 2 * N_Z, 2048), ("lru", 8, 256), ("cmp", 8, 2048), ("merge", 48, 3072),
           ("out", 16, 2048), ("ple", 2, 2048), ("ple_gate", 16, 2048), ("y", N_Y + N_MOD - N_Z, 2048), ("l", N_L, 2048),
           ("mla", 8, 1280), ("merge2", 32, 3072), ("out2", 16, 2048), ("peer_q", 16, 2048))


class Steps:

    def __init__(self, sem, names):
        self.sem, self.names = sem, names
        assert len(set(names)) == len(names), names

    def at(self, name, it=0):
        return it * len(self.names) + (self.names.index(name) + 1)


class Stage:

    def __init__(self, new_sem, name, rounds, **names):
        self.rounds = rounds
        self.steps = {e: Steps(new_sem(f"{name}_{e}_steps"), n.split()) for e, n in names.items() if n}

    def finished(self, eng):
        for s in self.steps.values():
            eng.wait_ge(s.sem, self.rounds * len(s.names))


class Do:

    def __init__(self, eng, stage, who, it=0):
        self.eng, self.stage, self.mine, self.it, self.n = eng, stage, stage.steps[who], it, 0

    def __call__(self, name, instruction):
        assert self.mine.names[self.n] == name, (self.mine.names[self.n], name)
        self.n += 1
        instruction.then_inc(self.mine.sem, 1)

    def wait(self, who, name, it=None):
        s = self.stage.steps[who]
        self.eng.wait_ge(s.sem, s.at(name, self.it if it is None else it))

    def own(self):
        self.eng.wait_ge(self.mine.sem, self.it * len(self.mine.names) + self.n)

    def end(self):
        assert self.n == len(self.mine.names), self.mine.names[self.n:]


def rounds(eng, count, body):
    body(0)
    if count == 2:
        body(1)
    elif count > 2:
        with eng.Fori(1, count) as i:
            body(i)


class Stream:

    def __init__(self, first, count, cols):
        self.first, self.count, self.cols = first, count, cols

    def each(self, eng, body, step=SLOTS):
        per = step // SLOTS

        def blocks(i, us):
            for u in us:
                b = self.first + u
                body(i * step + u, b % SLOTS, i * per + (b // SLOTS + 1), i, u)

        whole = self.count // step
        if whole:
            blocks(0, range(step))
        if whole == 2:
            blocks(1, range(step))
        elif whole > 2:
            with eng.Fori(1, whole) as i:
                blocks(i, range(step))
        blocks(whole, range(self.count - whole * step))


def build(nc: bass.Bass, a: dict):
    with ExitStack() as ctx:
        def new_sem(name):
            return ctx.enter_context(nc.semaphore(name))

        def sb(name, cols):
            return ctx.enter_context(nc.sbuf_tensor(name, [P, cols], F32))

        ps = ctx.enter_context(nc.psum_tensor("ps", [P, 8, 512], F32))
        ring = ctx.enter_context(nc.sbuf_tensor("ring", [P, SLOTS, SLOTW], F32))
        params = sb("params", N_PARAMS)
        halves = sb("halves", 64)
        pT = sb("p", 2 * T)[:, :].rearrange("p (k t) -> p k t", t=T)
        consts = sb("consts", N_CONSTS)
        misc = sb("misc", N_MISC)
        x = sb("x", D * T // P)
        mod = sb("mod", 192)
        gains = sb("gains", 80)
        AREA = 32600
        area = sb("area", AREA)

        def par(name, c=0, n=1):
            o, k = PARAMS[name]
            return params[:, bass.ds(c + o, n)]

        def half(name, c=0):
            o, k = PARAMS[name]
            return halves[:, bass.ds(c + o, 1)]

        def con(name):
            o, k = CONSTS[name]
            return consts[:, o:o + k]

        def cut(at, *shape):
            n = 1
            for s in shape:
                n *= s
            v = area[:, at:at + n]
            assert at + n <= AREA, (at, n)
            if len(shape) == 2:
                return v.rearrange("p (a b) -> p a b", b=shape[1])
            if len(shape) == 3:
                return v.rearrange("p (a b c) -> p a b c", b=shape[1], c=shape[2])
            return v

        ident, ones, causal, upto_mask = con("ident"), con("ones"), con("causal"), con("upto")
        xc = x[:, :].rearrange("p (c t) -> p c t", t=T)
        modv = mod[:, :].rearrange("p (c s) -> p c s", s=2)

        def bank(b, lo=0, n=512):
            return ps[:, b, lo:lo + n]

        streams, first = {}, 0
        for name, count, cols in STREAMS:
            streams[name] = Stream(first, count, cols)
            first += count
        landed = [new_sem(f"weights_landed_{s}") for s in range(SLOTS)]
        weights_used = new_sem("weights_used")
        evacuated = {name: new_sem(f"evacuated_{name}") for name, _, _ in STREAMS}
        inputs_loaded = new_sem("inputs_loaded")
        N_INPUTS = 5

        def gemm_block(pe, name, idx, slot, loads, ktiles, rhs, n, out=None, col=0, start=True, wait_bank=True):
            pe.wait_ge(landed[slot], loads * 16)
            if wait_bank and not (isinstance(idx, int) and idx < SLOTS):
                pe.wait_ge(evacuated[name], idx - (SLOTS - 1))
            for k in range(ktiles):
                last = nc.tensor.matmul(bank(slot, 0, n) if out is None else out, ring[:, slot, col + k * P:col + (k + 1) * P],
                                        rhs(k), start=(k == 0), stop=(k == ktiles - 1))
            return last

        S = {}

        def stage(name, rounds, **names):
            S[name] = Stage(new_sem, name, rounds, **names)
            return S[name]

        def norm_stage(name, rounds, chunks, extra_act=""):
            return stage(name, rounds, act="squares root", pe="sums", dve="inverse " + " ".join(
                f"scaled{c}" for c in range(chunks)))

        def norm_act(act, st, it, src, squares, root, sums, width, scale=1.0):
            do = Do(act, st, "act", it)
            do("squares", nc.scalar.activation(squares, src, ACT.Square))
            do.wait("pe", "sums")
            do("root", nc.scalar.activation(root, sums, ACT.Sqrt, bias=par("eps"), scale=scale))
            do.end()

        def norm_pe(pe, st, it, squares, sums, chunks):
            do = Do(pe, st, "pe", it)
            do.wait("act", "squares")
            for c in range(chunks):
                last = nc.tensor.matmul(sums, ones, squares[:, c, :], start=(c == 0), stop=(c == chunks - 1))
            do("sums", last)
            do.end()

        def norm_dve(dve, st, it, src, dst, root, gain, chunks):
            do = Do(dve, st, "dve", it)
            do.wait("act", "root")
            do("inverse", nc.vector.reciprocal(root, root))
            do.own()
            for c in range(chunks):
                do(f"scaled{c}", nc.vector.scalar_tensor_tensor(
                    out=dst(c), in0=src(c), scalar=gain(c), in1=root, op0=ALU.mult, op1=ALU.mult))
            do.end()

        SP_DVE = "sp_negated sp_plus2 sp_recip sp_s sp_s2 sp_q0 " + " ".join(
            f"sp_q{k}" for k in range(1, SOFTPLUS_TERMS - 1)) + " sp_last sp_top sp_out"
        SP_ACT = "sp_exp"

        def softplus_dve(do, v, t1, t2, t3, out):
            do("sp_negated", nc.vector.scalar_tensor_tensor(out=t1, in0=v, scalar=-1.0, in1=v, op0=ALU.mult, op1=ALU.min))
            do.wait("act", "sp_exp")
            do("sp_plus2", nc.vector.tensor_scalar(t2, t1, 2.0, None, ALU.add))
            do.own()
            do("sp_recip", nc.vector.reciprocal(t2, t2))
            do.own()
            do("sp_s", nc.vector.tensor_tensor(t1, t1, t2, ALU.mult))
            do.own()
            do("sp_s2", nc.vector.tensor_tensor(t2, t1, t1, ALU.mult))
            do.own()
            do("sp_q0", nc.vector.tensor_scalar(t3, t2, 1.0 / (2 * SOFTPLUS_TERMS - 1), None, ALU.mult))
            for k in range(1, SOFTPLUS_TERMS - 1):
                do.own()
                do(f"sp_q{k}", nc.vector.scalar_tensor_tensor(
                    out=t3, in0=t3, scalar=1.0 / (2 * (SOFTPLUS_TERMS - k) - 1), in1=t2, op0=ALU.add, op1=ALU.mult))
            do.own()
            do("sp_last", nc.vector.scalar_tensor_tensor(out=t3, in0=t3, scalar=1.0, in1=t1, op0=ALU.add, op1=ALU.mult))
            do("sp_top", nc.vector.tensor_scalar(out, v, 0.0, None, ALU.max))
            do.own()
            do("sp_out", nc.vector.scalar_tensor_tensor(out=out, in0=t3, scalar=2.0, in1=out, op0=ALU.mult, op1=ALU.add))

        def softplus_act(do, t1):
            do.wait("dve", "sp_negated")
            do("sp_exp", nc.scalar.activation(t1, t1, ACT.Exp))

        HN, ZAT = 0, 4096
        TMP = ZAT + N_Z * T
        hn = cut(HN, DC, T)
        z = cut(ZAT, N_Z, T)

        st_pre = stage("pre", 1, dve="halved cond_silu", act="cond_tanh")
        cond = par("cond", 0, 32)
        cond_silu = gains[:, 48:80]

        st_n1 = norm_stage("norm_x", 1, DC)
        sq = cut(TMP + 64, DC, T)
        root = cut(TMP + 64 + DC * T, T)

        A_AT, M_AT = TMP, TMP + 2048
        lru_a = cut(A_AT, BC, T)
        lru_m = cut(M_AT, BC, T)
        LT = M_AT + 2048
        uc, la, th, den, tx = (cut(LT + k * T, T) for k in range(5))
        lt1, lt2, lt3, lt4, nsp = (cut(LT + 5 * T + 8 * k, 8) for k in range(5))
        st_lam = stage("lam", 1, dve="neg " + SP_DVE + " scaled", act=SP_ACT)
        st_lru = stage("lru", BC, dve="lag0 lag1 lag2 lag3 log_a den inv m gated", act="tanh_a tanh_x a th")
        st_lru2 = stage("lru2", 1, act="root tanh_gate", dve="drive " + " ".join(f"scan{c}" for c in range(BC)) + " silu out")

        st_qk = stage("qk", N_QK // 4, act="squares root", pe="sums0 sums1", dve="inverse " + " ".join(f"scaled{c}" for c in range(4)))
        qk_sq = cut(TMP, 1024)
        qk_root = cut(TMP + 1024, 1024)

        VT_N = 12
        vt = cut(TMP, VT_N * NT, P)
        VT_END = TMP + VT_N * NT * P
        gb = cut(VT_END, NT, P)
        logf = cut(VT_END + 256, NT, BC)
        ft = [cut(VT_END + 256 + 16 * k, NT, BC) for k in range(1, 5)]
        cum = cut(VT_END + 256 + 16 * 5, NT, BC)
        G_END = VT_END + 256 + 96
        st_tr = stage("turn", 1, pe=" ".join(f"turned{k}" for k in range(7)) + " cum0 cum1", act=" ".join(f"kept{k}" for k in range(7))
                      + " gate_tanh " + SP_ACT, dve="gate neg " + SP_DVE + " logf cumkept")

        blk = cut(G_END, 2, 32 * 30)
        C_AT = G_END + 1920
        cth = cut(C_AT, 2, 30)
        chid = cut(C_AT + 60, 2 * 2, 30)
        kc = cut(C_AT + 180, 30)
        kcs = cut(C_AT + 210, 30)
        kcr = cut(C_AT + 240, 30)
        vc = cut(C_AT + 270, 2, P)
        C_END = C_AT + 270 + 256
        st_cmp = stage("cmp", 2, dve="b0 b1 silu halved", act="tanh")
        st_cmp2 = stage("cmp2", 1, pe="kc vc0 vc1 sums", act="copied squares root vck0 vck1", dve="inv out")

        N_AT = C_END
        nq = cut(N_AT, T)
        nst = cut(N_AT + 256, 2, 384)
        nex = cut(N_AT + 1024, 2, 384)
        ncs = cut(N_AT + 1792, 2, 16)
        nce = cut(N_AT + 1824, 2, 16)
        nmx = cut(N_AT + 1856, 2, 3)
        nsm = cut(N_AT + 1862, 2, 3)
        net = nst
        nct = cut(N_AT + 1868, 2, P)
        BR = [(b, t) for t in range(NT) for b in range(3)]
        st_nsa = stage(
            "nsa", BC,
            act="q " + " ".join(f"e{b}{t}" for b, t in BR) + " et0 et1 ctk",
            pe="s turned o",
            dve="ss sw sc max0 max1 maxc guard floor inv gates " + " ".join(f"w{b}{t}" for b, t in BR) + " y")

        fq = cut(N_AT, T)
        fv = cut(N_AT + 256, NT, P)
        fr = cut(N_AT + 512, NT, P)
        fb = cut(N_AT + 768, 384)
        fs = cut(N_AT + 1152, 384)
        fe = cut(N_AT + 1536, 384)
        fet = cut(N_AT + 1920, 384)
        fmx = cut(N_AT + 2304, 2)
        fsm = cut(N_AT + 2306, 2)
        st_fox = stage("fox", BC, act="q v e0 e1 etk", pe="s c turned o",
                       dve="r0 r1 b0 b1 s max0 max1 inv w0 w1 y")
        st_gate = stage("gates1", 2, act="tanh", dve="silu halved")

        merged = cut(TMP, DC, T)
        mth = cut(TMP + 4096, 2, T)
        mtm = cut(TMP + 4096 + 2 * T, 2, T)
        mlt = cut(TMP + 4096 + 4 * T, 2, T)
        st_merge = stage("merge", 48, act="gate y", dve="scaled summed")
        e_at = ZAT + 512
        e = cut(e_at, DC, T)
        e_sq = cut(e_at + 4096, DC, T)
        e_root = cut(e_at + 8192, T)
        gth = cut(e_at + 8192 + T, SLOTS, T)
        x2 = cut(TMP, DC, T)
        st_e = norm_stage("norm_e", 1, DC)
        st_ple = stage("ple", 2, act="e0 e1", pe="p0")
        st_pg = stage("pg", 16, dve="mixed added")
        st_x2 = stage("x2", 1, dve="moved")

        zg_tanh = cut(LT + 5 * T + 64, BC, T)
        gates_tmp = cut(TMP, BC, T)
        zflat = cut(ZAT, N_Z * T)
        vtf = cut(TMP, VT_N * NT * P)
        blkf = cut(G_END, 2 * 960)
        cthf, chidf = cut(C_AT, 60), cut(C_AT + 60, 120)
        bank45 = ps[:, 4:6, :]
        tick = cut(TMP + 4096 + 6 * T, 1)

        CTX_AT, Y_AT, L_AT, MY_AT, T2 = 4096, 8192, 18432, 23552, 25600
        hcat = cut(0, 2, DC * T)[:, :, :].rearrange("p s (c t) -> p s c t", t=T)
        yv = cut(Y_AT, N_Y, 2 * T)
        lv = cut(L_AT, N_L, T)
        my = cut(MY_AT, BC, T)
        gain1v = gains[:, 0:32].rearrange("p (c s) -> p c s", s=2)
        gain2v = gains[:, 32:48]
        sq2 = cut(T2, DC, T)
        root2 = cut(T2 + 4096, T)
        st_gain = stage("gain", 1, dve="first second")
        st_n2 = [norm_stage(f"norm2_{s}", 1, DC) for s in range(2)]
        st_shift = stage("shift", 1, act=" ".join(f"shift{c}" for c in range(2 * DC)))
        ctx_loaded = new_sem("ctx_loaded")
        st_cq = norm_stage("norm_cq", 1, 4)
        st_ckv = norm_stage("norm_ckv", 1, 2)
        msq = cut(T2, 1024)
        mroot = cut(T2 + 1024, 512)
        krd = cut(T2 + 1536, 2 * T)
        krt = cut(T2 + 2048, T)
        st_kr = stage("kr", 1, pe="dup rot", act="ctx", dve="cos sin sum")
        mq = cut(T2 + 2304, T)
        mqr = cut(T2 + 2560, T)
        mqt = cut(T2 + 2816, T)
        mk = cut(T2 + 3072, 2 * T)
        mv = cut(T2 + 3584, 4, P)
        me = cut(T2 + 4096, 2, 2 * T)
        met = cut(T2 + 5120, 2, 2 * T)
        mmx = cut(T2 + 6144, 2)
        msm = cut(T2 + 6146, 2)
        st_mla = stage("mla", BC, act="qn qr kn v e0 e1 et0 et1", pe="rot s turned0 turned1 o",
                       dve="cos sin sum max neg inv w0 w1 y")
        ctmp, cth2 = cut(T2, 2, T), cut(T2 + 512, 2, T)
        st_ckvv = stage("conv_kv", 16, dve="mid lm2 lm1 lp1 lp2 out", act="tanh")
        st_cvq = stage("conv_q", 8, dve="mid lm2 lm1 lp1 lp2 out", act="tanh")
        st_lk = stage("l2_k", 8, act="squares root", pe="sums", dve="inv out")
        st_lq = stage("l2_q", 8, act="squares root", pe="sums", dve="inv out")
        dnc_loaded = new_sem("dn_consts_loaded")
        DNC_AT = CTX_AT
        R2 = DNC_AT + N_DN_CONSTS
        dnc = cut(DNC_AT, N_DN_CONSTS)

        def dcon(name, k=0):
            o, _ = DN_CONSTS[name]
            return dnc[:, o + k * P:o + (k + 1) * P]

        gsp, gt1, gt2, gt3, gv = (cut(T2 + 512 * k, 2 * T) for k in range(5))
        ea = cut(T2 + 2560, 1)
        S13 = T2 + 6656
        AB_AT = Y_AT + Y_AB * 512
        gT, bT, gcum, eg, egl = (cut(S13 + 64 * k, 64) for k in range(5))
        beg, egls, gl = cut(AB_AT, 64), cut(AB_AT + 64, 128), cut(AB_AT + 192, 64)
        st_dec = stage("decay", 1, dve="shifted " + SP_DVE + " scale half_b beta sub beg", act=SP_ACT + " ea tanh_b gk bk cumk glk egl_exp eg_exp chunk_exp",
                       pe="turned cums")
        NU = 8
        B = [T2 + 1024 * k for k in range(6)]
        rg = cut(B[0], NU, P)
        pbuf = rg
        dec = cut(B[1], NU, P)
        xb = dec
        ub = dec
        mb = cut(B[2], NU, P)
        kbe = mb
        mt = cut(B[3], NU, P)
        kdec = mt
        xt = cut(B[4], NU, P)
        atl = cut(B[5], NU, P)
        wt = atl
        state = cut(T2 + 6144, 2, P)
        vnew = cut(T2 + 6400, 2, P)
        vb = cut(R2, NU, P)
        att = cut(R2 + 1024, 4, P)
        kst = cut(R2 + 1536, 2 * T)
        vst = cut(R2 + 2048, 2 * T)
        assert R2 + 2560 <= Y_AT + 1024
        qst = cut(L_AT, T)
        ktm = cut(L_AT + 256, 4, P)
        ob0 = cut(L_AT + 768, NT, P)
        vtm = cut(Y_AT + Y_KR * 512, 4, P)
        ob1 = cut(AB_AT + 256, NT, P)
        LV = range(1, 6)
        INNER = range(1, 5)
        SC = [(s, d) for s in range(8) for d in range(2)]
        st_dn = stage(
            "dn", BC,
            act="k v q ktm vtm relu_t relu dec dec_t mt " + " ".join(f"p{l}" for l in LV) + " u",
            pe="turned rows gram mt " + " ".join(f"p{l} " + (f"x{l} " if l in INNER else "") + f"xt{l}" for l in LV) + " u w "
               + " ".join(f"ws{s}0 ws{s}1 " + " ".join((f"oa{s}{d} " if s >= 4 else "") + f"su{s}{d}" for d in range(2)) for s in range(8)) + " ot",
            dve="rg0 rg1 diff0 diff1 tmask0 tmask1 att0 att1 smask0 smask1 gb0 gb1 m l00 l01 x l0t0 l0t1 xt "
                + " ".join(f"a{l}0 a{l}1 " + (f"x{l} " if l in INNER else "") + f"xt{l}" for l in LV) + " vb0 vb1 ke0 ke1 kd0 kd1 w s0 "
                + " ".join(f"vn{s}{d} " + (f"oi{s}{d} o{s}{d} " if s >= 4 else "") + f"st{s}{d}" for s, d in SC) + " osum ot")
        st_on = stage("dn_out", 2, act="squares root", pe="sums0 sums1", dve="inv " + " ".join(f"scaled{c}" for c in range(4)))
        st_og = stage("dn_gate", 1, act="tanh", dve="silu out")
        osq, oroot = cut(T2, 1024), cut(T2 + 1024, 1024)
        og = cut(T2 + 2048, BC, T)
        merged2 = cut(T2, DC, T)
        m2th, m2tm = cut(T2 + 4096, 2, T), cut(T2 + 4608, 2, T)
        st_merge2 = stage("merge2", 32, act="gate y", dve="scaled summed")

        HP_AT, MTR_AT, W_AT, IDX_AT, PB_AT, PC_AT = 0, 4096, 8192, 24576, 25088, 32256
        hp = cut(HP_AT, DC, T)
        psq, proot = cut(W_AT, DC, T), cut(W_AT + 4096, T)
        pq = cut(MTR_AT, DC, T)
        scores = cut(W_AT, 2 * DC, P)
        topv = cut(W_AT + 4096, 2 * DC, TOPK)
        topi = cut(W_AT + 4608, 2 * DC, TOPK)
        gated = cut(W_AT + 6208, 1)
        krow, kval, kidx = cut(W_AT + 6048, P), cut(W_AT + 6176, TOPK), cut(W_AT + 6192, TOPK).bitcast(U32)
        krest = cut(W_AT + 5120, P)
        cand, crest, cexp = (cut(W_AT + 5248 + 256 * k, 256) for k in range(3))
        c8, csum = cut(W_AT + 6016, 2, 8), cut(W_AT + 6032, 2)
        mix = cut(W_AT + 8192, NT, TOPK, P)
        mix5 = mix.rearrange("p t a (h b) -> p t a h b", b=TOPK)
        idxp = cut(W_AT + 12288, 4, P)
        idxt = cut(IDX_AT, 2, T)
        mixt = cut(MTR_AT, TOPK, T)
        st_np = norm_stage("norm_p", 1, DC)
        st_sh2 = stage("shift2", 1, act=" ".join(f"shift{c}" for c in range(DC)))
        st_sc = stage("scores", 1, pe=" ".join(f"s{b}" for b in range(8)), act=" ".join(f"k{b}" for b in range(8)))
        st_top = stage("top", 2 * DC, dve="row gate0 m0 gate1 i0 rest gate2 m1 gate3 i1 values indices")
        st_cand = stage("cand", DC, dve="sum gate0 m0 gate1 r0 gate2 m1 gate3 r1 chosen neg masked total inv out", act="exp")
        st_mt = stage("mix", 1, dve="idx0 idx1", pe="idx " + " ".join(f"m{b}" for b in range(8)), act="idx " + " ".join(f"m{b}" for b in range(8)))
        NB4 = 4
        NR = T // NB4
        hots = [[cut(PB_AT + 512 * (3 * k + j), NB4, P) for j in range(3)] for k in range(4)]
        rbuf = [cut(PB_AT + 512 * (12 + k), NB4, P) for k in range(2)]
        iota, same_head = cut(PC_AT, P), cut(PC_AT + P, P)
        ew = [cut(W_AT + 8192 * k, P, 64) for k in range(2)]
        hot_made, spread_made, spread_kept, weights_made, weights_kept = (new_sem(n) for n in (
            "hot_made", "spread_made", "spread_kept", "weights_made", "weights_kept"))
        peer_loaded, w_stored = new_sem("peer_consts_loaded"), [new_sem(f"expert_weights_stored_{k}") for k in range(2)]
        NG = KEYS // GROUP
        V_AT, YA_AT, EW_AT, G_AT, GEL_AT = 4096, 20480, 24576, 26624, 28672
        vslots = cut(V_AT, 2 * GROUP, D)
        yacc = cut(YA_AT, DC, T)
        wexp = [cut(EW_AT + 1024 * k, 4, GROUP, 64) for k in range(2)]
        gact = [cut(G_AT + 1024 * k, GROUP, T) for k in range(2)]
        gel = cut(GEL_AT, GROUP, T)
        u_landed = [new_sem(f"u_landed_{k}") for k in range(GROUP)]
        v_landed = [new_sem(f"v_landed_{k}") for k in range(2 * GROUP)]
        wexp_landed = [new_sem(f"expert_weights_landed_{k}") for k in range(2)]
        hidden_made, hidden_taken, hidden_weighted, products_made, products_added = (new_sem(n) for n in (
            "hidden_made", "hidden_taken", "hidden_weighted", "products_made", "products_added"))
        st_res = stage("residual", 1, dve=" ".join(f"r{c}" for c in range(DC)))
        st_nf = norm_stage("norm_f", 1, DC)
        fsq, froot = cut(V_AT, DC, T), cut(V_AT + 4096, T)
        stored = new_sem("stored")

        mixtf = cut(MTR_AT, TOPK * T)
        ewf = [cut(W_AT + 8192 * k, P * 64) for k in range(2)]
        zeroed = new_sem("zeroed")

        def barrier(eng, *names):
            for n in names:
                if n in S:
                    S[n].finished(eng)
                else:
                    eng.wait_ge(evacuated[n], streams[n].count)

        block = ctx.enter_context(nc.Block())

        def evacuate(act, name, out, bias, n=T, func=ACT.Identity, scale=1.0):
            def take(idx, slot, loads, i, u):
                act.wait_ge(weights_used, idx + (streams[name].first + 1))
                nc.scalar.activation(out(idx), bank(slot, 0, n), func, bias=bias(idx), scale=scale).then_inc(evacuated[name], 1)
            streams[name].each(act, take)

        def gemm(pe, name, ktiles, rhs, n=T):
            def product(idx, slot, loads, i, u):
                gemm_block(pe, name, idx, slot, loads, ktiles, rhs, n).then_inc(weights_used, 1)
            streams[name].each(pe, product)

        cs = cond_silu.rearrange("p (k s) -> p k s", s=2)

        def product_pairs(pe, name, rhs, n, out=None):
            def product(idx, slot, loads, i, u):
                if u % 2:
                    gemm_block(pe, name, idx, slot, loads, DC, lambda k: cs[:, k, :], 2).then_inc(weights_used, 1)
                else:
                    gemm_block(pe, name, idx, slot, loads, DC, rhs, n, out=None if out is None else out(slot)).then_inc(weights_used, 1)
            streams[name].each(pe, product)

        def take_pairs(act, name, kept, n, first_mod):
            def take(idx, slot, loads, i, u):
                act.wait_ge(weights_used, idx + (streams[name].first + 1))
                k = i * 2 + u // 2
                if u % 2:
                    nc.scalar.activation(modv[:, k + first_mod, :], bank(slot, 0, 2), ACT.Identity,
                                         bias=par("b_mod", k + first_mod), scale=0.5).then_inc(evacuated[name], 1)
                    return
                out, bias = kept(k)
                if bias is None:
                    nc.scalar.activation(out, bank(slot, 0, n), ACT.Copy).then_inc(evacuated[name], 1)
                else:
                    nc.scalar.activation(out, bank(slot, 0, n), ACT.Identity, bias=bias).then_inc(evacuated[name], 1)
            streams[name].each(act, take)

        def pre_dve(dve):
            dve.wait_ge(inputs_loaded, N_INPUTS * 16)
            do = Do(dve, st_pre, "dve")
            do("halved", nc.vector.tensor_scalar(halves[:, :], params[:, 0:64], 0.5, None, ALU.mult))
            do.wait("act", "cond_tanh")
            do("cond_silu", nc.vector.scalar_tensor_tensor(out=cond_silu, in0=cond_silu, scalar=1.0, in1=cond, op0=ALU.add, op1=ALU.mult))
            do.end()

        def pre_act(act):
            act.wait_ge(inputs_loaded, N_INPUTS * 16)
            do = Do(act, st_pre, "act")
            do("cond_tanh", nc.scalar.activation(cond_silu, cond, ACT.Tanh, scale=0.5))
            do.end()

        def pre_pe(pe):
            pe.wait_ge(inputs_loaded, N_INPUTS * 16)
            barrier(pe, "pre")

        def n1_act(act):
            norm_act(act, st_n1, 0, xc, sq, root, bank(4, 0, T), T, 1.0 / D)
            take_pairs(act, "z", lambda i: (z[:, i, :], par("b_in", i)), T, 0)

        def n1_pe(pe):
            norm_pe(pe, st_n1, 0, sq, bank(4, 0, T), DC)
            barrier(pe, "norm_x")
            product_pairs(pe, "z", lambda k: hn[:, k, :], T)

        def n1_dve(dve):
            norm_dve(dve, st_n1, 0, lambda c: xc[:, c, :], lambda c: hn[:, c, :], root, lambda c: par("ln_gain", c), DC)

        def lru_dve(dve):
            do = Do(dve, st_lam, "dve")
            do("neg", nc.vector.tensor_scalar(lt3, par("lam", 0, 8), -1.0, None, ALU.mult))
            do.own()
            softplus_dve(do, lt3, lt1, lt2, lt4, nsp)
            do.own()
            do("scaled", nc.vector.tensor_scalar(nsp, nsp, -4.0, None, ALU.mult))
            do.end()
            barrier(dve, "z")

            def chunk(c):
                do = Do(dve, st_lru, "dve", c)
                u = z[:, Z_LRU + c, :]
                do("lag0", nc.vector.tensor_scalar(uc, u, par("conv_w", c + 24), par("conv_b", c), ALU.mult, ALU.add))
                for lag in range(1, 4):
                    do.own()
                    do(f"lag{lag}", nc.vector.scalar_tensor_tensor(
                        out=uc[:, lag:], in0=u[:, 0:T - lag], scalar=par("conv_w", c + (3 - lag) * 8), in1=uc[:, lag:], op0=ALU.mult, op1=ALU.add))
                do.wait("act", "tanh_a")
                do("log_a", nc.vector.tensor_scalar(la, la, 1.0, nsp[:, bass.ds(c, 1)], ALU.add, ALU.mult))
                do.wait("act", "th")
                do("den", nc.vector.tensor_scalar(den, th, -1.0, 1.0, ALU.mult, ALU.add))
                do.own()
                do("inv", nc.vector.reciprocal(den, den))
                do.own()
                do("m", nc.vector.scalar_tensor_tensor(out=lru_m[:, c, :], in0=th, scalar=-2.0, in1=den, op0=ALU.mult, op1=ALU.mult))
                do("gated", nc.vector.scalar_tensor_tensor(out=z[:, Z_LRU + c, :], in0=tx, scalar=1.0, in1=uc, op0=ALU.add, op1=ALU.mult))
                do.own()
                do.end()

            rounds(dve, BC, chunk)
            do = Do(dve, st_lru2, "dve")
            do.wait("act", "root")
            zu = z[:, Z_LRU:Z_LRU + BC, :]
            zg = z[:, Z_LG:Z_LG + BC, :]
            do("drive", nc.vector.scalar_tensor_tensor(out=zu, in0=lru_m, scalar=0.5, in1=zu, op0=ALU.mult, op1=ALU.mult))
            do.own()
            for c in range(BC):
                do(f"scan{c}", nc.vector.tensor_tensor_scan(
                    out=lru_m[:, c, :], data0=lru_a[:, c, :], data1=z[:, Z_LRU + c, :], initial=0.0, op0=ALU.mult, op1=ALU.add))
            do.wait("act", "tanh_gate")
            do("silu", nc.vector.scalar_tensor_tensor(out=zg, in0=zg_tanh, scalar=1.0, in1=zg, op0=ALU.add, op1=ALU.mult))
            do.own()
            do("out", nc.vector.scalar_tensor_tensor(out=zg, in0=lru_m, scalar=0.5, in1=zg, op0=ALU.mult, op1=ALU.mult))
            do.end()

        def lru_act(act):
            do = Do(act, st_lam, "act")
            softplus_act(do, lt1)

            def chunk(idx, slot, loads, i, u):
                do = Do(act, st_lru, "act", idx)
                act.wait_ge(weights_used, idx + (streams["lru"].first + 1))
                if not (isinstance(idx, int) and idx == 0):
                    do.wait("dve", "gated", idx - 1)
                do("tanh_a", nc.scalar.activation(la, bank(slot, 0, T), ACT.Tanh, bias=half("lru_ba", idx), scale=0.5))
                do("tanh_x", nc.scalar.activation(tx, bank(slot, T, T), ACT.Tanh, bias=half("lru_bx", idx), scale=0.5))
                do.wait("dve", "log_a")
                do("a", nc.scalar.activation(lru_a[:, idx, :], la, ACT.Exp))
                do("th", nc.scalar.activation(th, la, ACT.Tanh))
                do.end()

            streams["lru"].each(act, chunk)
            do = Do(act, st_lru2, "act")
            S["lru"].finished(act)
            do("root", nc.scalar.activation(lru_m, lru_m, ACT.Sqrt))
            do.wait("dve", "drive")
            do("tanh_gate", nc.scalar.activation(zg_tanh, z[:, Z_LG:Z_LG + BC, :], ACT.Tanh, scale=0.5))
            do.end()

        def lru_pe(pe):
            barrier(pe, "z")

            def chunk(idx, slot, loads, i, u):
                pe.wait_ge(landed[slot], loads * 16)
                pe.wait_ge(st_lru.steps["dve"].sem, st_lru.steps["dve"].at("lag3", idx))
                nc.tensor.matmul(bank(slot, 0, T), ring[:, slot, 0:P], uc, start=True, stop=True)
                nc.tensor.matmul(bank(slot, T, T), ring[:, slot, P:2 * P], uc, start=True, stop=True).then_inc(weights_used, 1)

            streams["lru"].each(pe, chunk)

        def qk_act(act):
            barrier(act, "lru2", "gates1")

            def part(it):
                do = Do(act, st_qk, "act", it)
                do("squares", nc.scalar.activation(qk_sq, zflat[:, bass.ds(it * 1024 + Z_NQ * T, 1024)], ACT.Square))
                do.wait("pe", "sums1")
                if not isinstance(it, int) or it > 0:
                    do.wait("dve", "scaled3", it - 1)
                do("root", nc.scalar.activation(qk_root, ps[:, 4:6, :].rearrange("p b n -> p (b n)"), ACT.Sqrt, bias=par("eps"), scale=1.0 / P))
                do.end()
            rounds(act, N_QK // 4, part)

        def qk_pe(pe):
            barrier(pe, "lru2")

            def part(it):
                do = Do(pe, st_qk, "pe", it)
                do.wait("act", "squares")
                do("sums0", nc.tensor.matmul(bank(4), ones, qk_sq[:, 0:512], start=True, stop=True))
                do("sums1", nc.tensor.matmul(bank(5), ones, qk_sq[:, 512:1024], start=True, stop=True))
                do.end()
            rounds(pe, N_QK // 4, part)

        def qk_dve(dve):
            def part(it):
                do = Do(dve, st_qk, "dve", it)
                do.wait("act", "root")
                do("inverse", nc.vector.reciprocal(qk_root, qk_root))
                do.own()
                for c in range(4):
                    v = z[:, it * 4 + (Z_NQ + c), :]
                    do(f"scaled{c}", nc.vector.scalar_tensor_tensor(
                        out=v, in0=v, scalar=par("qk_gain", it * 4 + c), in1=qk_root[:, c * T:(c + 1) * T], op0=ALU.mult, op1=ALU.mult))
                do.end()
            rounds(dve, N_QK // 4, part)

        TURNS = [[(c, t) for c in (2 * k, 2 * k + 1) for t in range(NT)] for k in range(VT_N // 2)] + [[(None, 0), (None, 1)]]

        def turn_pe(pe):
            barrier(pe, "qk")
            do = Do(pe, st_tr, "pe")
            for k, parts in enumerate(TURNS):
                if k >= 2:
                    do.wait("act", f"kept{k - 2}")
                for j, (c, t) in enumerate(parts):
                    src = z[:, Z_GB if c is None else Z_VS + c, t * P:(t + 1) * P]
                    last = nc.tensor.transpose(bank(4 + k % 2, j * P, P), src, ident)
                do(f"turned{k}", last)
            do.wait("dve", "logf")
            do("cum0", nc.tensor.matmul(bank(6, 0, BC), upto_mask, logf[:, 0, :], start=True, stop=True))
            nc.tensor.matmul(bank(7, 0, BC), upto_mask, logf[:, 1, :], start=True, stop=False)
            do("cum1", nc.tensor.matmul(bank(7, 0, BC), ones, logf[:, 0, :], start=False, stop=True))
            do.end()

        def turn_act(act):
            barrier(act, "qk")
            do = Do(act, st_tr, "act")
            for k, parts in enumerate(TURNS):
                do.wait("pe", f"turned{k}")
                dst = vt[:, 4 * k:4 * k + 4, :] if k < len(TURNS) - 1 else gb
                do(f"kept{k}", nc.scalar.activation(dst, bank(4 + k % 2, 0, len(parts) * P).rearrange("p (a b) -> p a b", b=P), ACT.Copy))
            do.own()
            do("gate_tanh", nc.scalar.activation(gb[:, :, 32:56], gb[:, :, 0:24], ACT.Tanh, scale=0.5))
            softplus_act(do, ft[0])
            do.end()

        def turn_dve(dve):
            do = Do(dve, st_tr, "dve")
            do.wait("act", "gate_tanh")
            do("gate", nc.vector.tensor_scalar(gb[:, :, 0:24], gb[:, :, 32:56], 1.0, 0.5, ALU.add, ALU.mult))
            do("neg", nc.vector.tensor_scalar(ft[1], gb[:, :, 24:32], -1.0, None, ALU.mult))
            do.own()
            softplus_dve(do, ft[1], ft[0], ft[2], ft[3], logf)
            do.own()
            do("logf", nc.vector.tensor_scalar(logf, logf, -1.0, None, ALU.mult))
            do.wait("pe", "cum1")
            do("cumkept", nc.vector.tensor_copy(cum, ps[:, 6:8, 0:BC]))
            do.end()

        def cmp_dve(dve):
            barrier(dve, "turn")

            def kv(it):
                do = Do(dve, st_cmp, "dve", it)
                zk = [z[:, it * 2 + (Z_KC + g), :].rearrange("p (n r) -> p r n", r=16) for g in range(2)]
                b4 = blkf[:, bass.ds(it * 960, 960)].rearrange("p (h r g n) -> p h r g n", h=2, r=16, g=2)
                for h in range(2):
                    for g in range(2):
                        last = nc.vector.tensor_tensor(
                            b4[:, h, :, g, :], zk[g][:, :, h:h + NCMP],
                            par("pos", it * 32 + h * 16, 16)[:, :, None].to_broadcast([P, 16, NCMP]), ALU.add)
                        if g == 1:
                            do(f"b{h}", last)
                do.wait("act", "tanh")
                hv = bank45[:, :, 0:30]
                do("silu", nc.vector.scalar_tensor_tensor(out=cth, in0=cth, scalar=1.0, in1=hv, op0=ALU.add, op1=ALU.mult))
                do.own()
                do("halved", nc.vector.tensor_scalar(chidf[:, bass.ds(it * 60, 60)], cthf, 0.5, None, ALU.mult))
                do.own()
                do.end()
            rounds(dve, 2, kv)
            do = Do(dve, st_cmp2, "dve")
            do.wait("act", "root")
            do("inv", nc.vector.reciprocal(kcr, kcr))
            do.own()
            do("out", nc.vector.scalar_tensor_tensor(out=kc, in0=kc, scalar=par("cmp_gain"), in1=kcr, op0=ALU.mult, op1=ALU.mult))
            do.end()

        def cmp_pe(pe):
            barrier(pe, "turn")

            def part(idx, slot, loads, i, u):
                pe.wait_ge(landed[slot], loads * 16)
                if u == 0:
                    pe.wait_ge(st_cmp.steps["dve"].sem, st_cmp.steps["dve"].at("b1", i))
                bk = blkf[:, bass.ds(i * 960, 960)].rearrange("p (r n) -> p r n", n=30)
                for r in range(8):
                    for h in range(2):
                        last = nc.tensor.matmul(bank(4 + h, 0, 30), ring[:, slot, r * T + h * P:r * T + (h + 1) * P], bk[:, u * 8 + r, :],
                                                start=(u == 0 and r == 0), stop=(u == 3 and r == 7))
                last.then_inc(weights_used, 1)

            streams["cmp"].each(pe, part)
            do = Do(pe, st_cmp2, "pe")
            S["cmp"].finished(pe)
            w2 = misc[:, 0:512].rearrange("p (a n) -> p a n", n=P)
            for h in range(2):
                last = nc.tensor.matmul(bank(6, 0, 30), w2[:, h, :], chid[:, h, :], start=(h == 0), stop=(h == 1))
            do("kc", last)
            for g in range(2):
                for h in range(2):
                    last = nc.tensor.matmul(bank(4 + g, 0, P)[0:NCMP, :], chid[:, 2 + h, g * NCMP:(g + 1) * NCMP], w2[:, 2 + h, :],
                                            start=(h == 0), stop=(h == 1))
                do(f"vc{g}", last)
            do.wait("act", "squares")
            do("sums", nc.tensor.matmul(bank(7, 0, 30), ones, kcs, start=True, stop=True))
            do.end()

        def cmp_act(act):
            barrier(act, "turn")

            def kv(it):
                do = Do(act, st_cmp, "act", it)
                act.wait_ge(weights_used, it * 4 + (streams["cmp"].first + 4))
                do("tanh", nc.scalar.activation(cth, bank45[:, :, 0:30], ACT.Tanh, scale=0.5))
                do.end()
            rounds(act, 2, kv)
            do = Do(act, st_cmp2, "act")
            do.wait("pe", "kc")
            do("copied", nc.scalar.activation(kc, bank(6, 0, 30), ACT.Copy))
            do("squares", nc.scalar.activation(kcs, bank(6, 0, 30), ACT.Square))
            do.wait("pe", "sums")
            do("root", nc.scalar.activation(kcr, bank(7, 0, 30), ACT.Sqrt, bias=par("eps"), scale=1.0 / P))
            for g in range(2):
                do(f"vck{g}", nc.scalar.activation(vc[0:NCMP, g, :], bank(4 + g, 0, P)[0:NCMP, :], ACT.Copy))
            do.end()

        SPAN = ((0, 128), (128, 256))

        def nsa_head(g, fn):
            def run(eng):
                with eng.Fori(4 * g, 4 * g + 4) as h:
                    fn(h, g)
            return run

        def nsa_act(act):
            barrier(act, "cmp2")

            def head(h, g):
                do = Do(act, st_nsa, "act", h)
                do("q", nc.scalar.activation(nq, z[:, h + Z_NQ, :], ACT.Copy))
                do.wait("dve", "guard")
                for b, t in BR:
                    lo, n = SPAN[t]
                    src, dst = (ncs[:, t, 0:NCMP], nce[:, t, 0:NCMP]) if b == 2 else (nst[:, b, lo:lo + n], nex[:, b, lo:lo + n])
                    do(f"e{b}{t}", nc.scalar.activation(dst, src, ACT.Exp, bias=nmx[:, t, b:b + 1], accum_out=nsm[:, t, b:b + 1]))
                do.wait("pe", "turned")
                do("et0", nc.scalar.activation(net[:, 0, :], bank(5, 0, 384), ACT.Copy))
                do("et1", nc.scalar.activation(net[:, 1, :], bank(6, 0, 384), ACT.Copy))
                do("ctk", nc.scalar.activation(nct[0:NCMP, :, :], bank(7, 0, 256)[0:NCMP, :].rearrange("p (a b) -> p a b", b=P), ACT.Copy))
                do.end()
            for g in range(2):
                nsa_head(g, head)(act)

        def nsa_pe(pe):
            barrier(pe, "cmp2")

            def head(h, g):
                do = Do(pe, st_nsa, "pe", h)
                do.wait("act", "q")
                for t in range(NT):
                    lo, n = SPAN[t]
                    q = nq[:, t * P:(t + 1) * P]
                    nc.tensor.matmul(bank(0, lo, n), q, z[:, Z_KS + g, 0:n], start=True, stop=True)
                    nc.tensor.matmul(bank(1, lo, n), q, z[:, Z_KW + g, 0:n], start=True, stop=True)
                    last = nc.tensor.matmul(bank(2, t * 16, NCMP), q, kc[:, g * NCMP:(g + 1) * NCMP], start=True, stop=True)
                do("s", last)
                do.wait("dve", "w21")
                for b in range(2):
                    for j in range(3):
                        nc.tensor.transpose(bank(5 + b, j * P, P), nex[:, b, j * P:(j + 1) * P], ident)
                for t in range(NT):
                    last = nc.tensor.transpose(bank(7, t * P, P)[0:NCMP, :], nce[:, t, 0:NCMP], ident)
                do("turned", last)
                do.wait("act", "ctk")
                for t in range(NT):
                    out = bank(4, t * P, P)
                    keys = (0,) if t == 0 else (1, 2)
                    for b in range(2):
                        for n, j in enumerate(keys):
                            nc.tensor.matmul(out, vt[:, (2 * b + g) * NT + n, :], net[:, b, j * P:(j + 1) * P],
                                             start=(b == 0 and n == 0), stop=False)
                    last = nc.tensor.matmul(out, vc[0:NCMP, g, :], nct[0:NCMP, t, :], start=False, stop=True)
                do("o", last)
                do.end()
            for g in range(2):
                nsa_head(g, head)(pe)

        def nsa_dve(dve):
            barrier(dve, "cmp2", "gates1")

            def head(h, g):
                do = Do(dve, st_nsa, "dve", h)
                do.wait("pe", "s")
                for b, name in enumerate(("ss", "sw")):
                    do(name, nc.vector.scalar_tensor_tensor(out=nst[:, b, :], in0=bank(b, 0, 384), scalar=SCALE, in1=causal,
                                                            op0=ALU.mult, op1=ALU.subtract))
                cm = con("cmp_mask").rearrange("p (t n) -> p t n", n=16)[:, :, 0:NCMP]
                do("sc", nc.vector.scalar_tensor_tensor(out=ncs[:, :, 0:NCMP], in0=bank(2, 0, 32).rearrange("p (t n) -> p t n", n=16)[:, :, 0:NCMP],
                                                        scalar=SCALE, in1=cm, op0=ALU.mult, op1=ALU.subtract))
                do.own()
                for t in range(NT):
                    lo, n = SPAN[t]
                    do(f"max{t}", nc.vector.tensor_reduce(nmx[:, t, 0:2], nst[:, :, lo:lo + n], AX_X, ALU.max, negate=True))
                do("maxc", nc.vector.tensor_reduce(nmx[:, :, 2], ncs[:, :, 0:NCMP], AX_X, ALU.max, negate=True))
                do.own()
                do("guard", nc.vector.tensor_scalar(nmx, nmx, GUARD, None, ALU.min))
                do.wait("act", "e21")
                do("floor", nc.vector.tensor_scalar(nsm, nsm, 1e-30, None, ALU.max))
                do.own()
                do("inv", nc.vector.reciprocal(nsm, nsm))
                do.own()
                do("gates", nc.vector.tensor_tensor(nsm, nsm, gb[:, :, bass.ds(h * 3, 3)], ALU.mult))
                do.own()
                for b, t in BR:
                    lo, n = SPAN[t]
                    v = nce[:, t, 0:NCMP] if b == 2 else nex[:, b, lo:lo + n]
                    do(f"w{b}{t}", nc.vector.tensor_scalar(v, v, nsm[:, t, b:b + 1], None, ALU.mult))
                do.wait("pe", "o")
                y = z[:, h + Z_NG, :]
                do("y", nc.vector.tensor_tensor(y, y, bank(4, 0, T), ALU.mult))
                do.end()
            for g in range(2):
                nsa_head(g, head)(dve)

        GATES = (Z_NG, Z_FG)

        def gates_act(act):
            barrier(act, "lru2")
            for it, c in enumerate(GATES):
                do = Do(act, st_gate, "act", it)
                if it:
                    do.wait("dve", "silu", it - 1)
                do("tanh", nc.scalar.activation(gates_tmp, z[:, c:c + BC, :], ACT.Tanh, scale=0.5))
                do.end()

        def gates_dve(dve):
            for it, c in enumerate(GATES):
                do = Do(dve, st_gate, "dve", it)
                do.wait("act", "tanh")
                v = z[:, c:c + BC, :]
                do("silu", nc.vector.scalar_tensor_tensor(out=v, in0=gates_tmp, scalar=1.0, in1=v, op0=ALU.add, op1=ALU.mult))
                do.own()
                do("halved", nc.vector.tensor_scalar(v, v, 0.5, None, ALU.mult))
                do.end()

        def fox_act(act):
            barrier(act, "nsa")

            def head(h):
                do = Do(act, st_fox, "act", h)
                do("q", nc.scalar.activation(fq, z[:, h + Z_FQ, :], ACT.Copy))
                if not isinstance(h, int) or h > 0:
                    do.wait("pe", "o", h - 1)
                do("v", nc.scalar.activation(fv, vtf[:, bass.ds(h * (NT * P) + 4 * NT * P, NT * P)].rearrange("p (a b) -> p a b", b=P), ACT.Copy))
                for t in range(NT):
                    lo, n = SPAN[t]
                    do.wait("dve", f"max{t}")
                    do(f"e{t}", nc.scalar.activation(fe[:, lo:lo + n], fs[:, lo:lo + n], ACT.Exp, bias=fmx[:, t:t + 1], accum_out=fsm[:, t:t + 1]))
                do.wait("pe", "turned")
                do("etk", nc.scalar.activation(fet, bank(2, 0, 384), ACT.Copy))
                do.end()
            rounds(act, BC, head)

        def fox_pe(pe):
            barrier(pe, "nsa")

            def head(h):
                do = Do(pe, st_fox, "pe", h)
                do.wait("act", "q")
                if not isinstance(h, int) or h > 0:
                    do.wait("dve", "y", h - 1)
                for t in range(NT):
                    lo, n = SPAN[t]
                    last = nc.tensor.matmul(bank(0, lo, n), fq[:, t * P:(t + 1) * P], z[:, h + Z_FK, 0:n], start=True, stop=True)
                do("s", last)
                do.wait("dve", "r1")
                nc.tensor.matmul(bank(1, 0, P), ones, fr[:, 0, :], start=True, stop=True)
                nc.tensor.matmul(bank(1, P, P), ones, fr[:, 1, :], start=True, stop=False)
                do("c", nc.tensor.matmul(bank(1, P, P), ones, logf[:, 0, bass.ds(h, 1)].to_broadcast([P, P]), start=False, stop=True))
                do.wait("dve", "w1")
                for j in range(3):
                    last = nc.tensor.transpose(bank(2, j * P, P), fe[:, j * P:(j + 1) * P], ident)
                do("turned", last)
                do.wait("act", "etk")
                nc.tensor.matmul(bank(3, 0, P), fv[:, 0, :], fet[:, 0:P], start=True, stop=True)
                nc.tensor.matmul(bank(3, P, P), fv[:, 0, :], fet[:, P:2 * P], start=True, stop=False)
                do("o", nc.tensor.matmul(bank(3, P, P), fv[:, 1, :], fet[:, 2 * P:3 * P], start=False, stop=True))
                do.end()
            rounds(pe, BC, head)

        def fox_dve(dve):
            barrier(dve, "nsa")

            def head(h):
                do = Do(dve, st_fox, "dve", h)
                for t in range(NT):
                    do(f"r{t}", nc.vector.tensor_scalar(fr[:, t, :], upto_mask, logf[:, t, bass.ds(h, 1)], None, ALU.mult))
                do.wait("pe", "c")
                for t in range(NT):
                    lo, n = SPAN[t]
                    do(f"b{t}", nc.vector.scalar_tensor_tensor(out=fb[:, lo:lo + n], in0=bank(1, 0, n), scalar=cum[:, t, bass.ds(h, 1)],
                                                               in1=causal[:, lo:lo + n], op0=ALU.subtract, op1=ALU.add))
                do.own()
                do.wait("pe", "s")
                do("s", nc.vector.scalar_tensor_tensor(out=fs, in0=bank(0, 0, 384), scalar=SCALE, in1=fb, op0=ALU.mult, op1=ALU.subtract))
                do.own()
                for t in range(NT):
                    lo, n = SPAN[t]
                    do(f"max{t}", nc.vector.tensor_reduce(fmx[:, t:t + 1], fs[:, lo:lo + n], AX_X, ALU.max, negate=True))
                do.wait("act", "e1")
                do("inv", nc.vector.reciprocal(fsm, fsm))
                do.own()
                for t in range(NT):
                    lo, n = SPAN[t]
                    do(f"w{t}", nc.vector.tensor_scalar(fe[:, lo:lo + n], fe[:, lo:lo + n], fsm[:, t:t + 1], None, ALU.mult))
                do.wait("pe", "o")
                y = z[:, h + Z_FG, :]
                do("y", nc.vector.tensor_tensor(y, y, bank(3, 0, T), ALU.mult))
                do.end()
            rounds(dve, BC, head)

        YAT = (Z_LG, Z_NG, Z_FG)

        def merge_pe(pe):
            barrier(pe, "fox")

            def part(idx, slot, loads, i, u):
                y = YAT[u % 3]
                pe.wait_ge(landed[slot], loads * 16)
                if not (isinstance(idx, int) and idx < SLOTS):
                    pe.wait_ge(st_merge.steps["act"].sem, st_merge.steps["act"].at("y", idx - SLOTS))
                for k in range(DC):
                    nc.tensor.matmul(bank(slot, 0, T), ring[:, slot, k * P:(k + 1) * P], hn[:, k, :], start=(k == 0), stop=(k == DC - 1))
                for k in range(BC):
                    last = nc.tensor.matmul(bank(4 + slot, 0, T), ring[:, slot, D + k * P:D + (k + 1) * P], z[:, y + k, :],
                                            start=(k == 0), stop=(k == BC - 1))
                last.then_inc(weights_used, 1)
            streams["merge"].each(pe, part, step=12)

        def merge_act(act):
            def part(idx, slot, loads, i, u):
                do = Do(act, st_merge, "act", idx)
                act.wait_ge(weights_used, idx + (streams["merge"].first + 1))
                if not (isinstance(idx, int) and idx < 2):
                    do.wait("dve", "summed", idx - 2)
                do("gate", nc.scalar.activation(mth[:, u % 2, :], bank(slot, 0, T), ACT.Tanh, bias=half("b_merge", idx), scale=0.5))
                do("y", nc.scalar.activation(mtm[:, u % 2, :], bank(4 + slot, 0, T), ACT.Copy, scale=0.5))
                do.end()
            streams["merge"].each(act, part, step=12)

        def merge_dve(dve):
            barrier(dve, "fox")

            def part(idx, slot, loads, i, u):
                do = Do(dve, st_merge, "dve", idx)
                do.wait("act", "y")
                d = merged[:, i * 4 + u // 3, :]
                dst = d if u % 3 == 0 else mtm[:, u % 2, :]
                do("scaled", nc.vector.scalar_tensor_tensor(out=dst, in0=mth[:, u % 2, :], scalar=1.0, in1=mtm[:, u % 2, :], op0=ALU.add, op1=ALU.mult))
                do.own()
                if u % 3 == 0:
                    ins = nc.vector.tensor_copy(tick, par("eps"))
                else:
                    ins = nc.vector.tensor_tensor(d, d, dst, ALU.add)
                do("summed", ins)
                do.end()
            streams["merge"].each(dve, part, step=12)

        def add_block(dve, name, out, scalar=None):
            def take(idx, slot, loads, i, u):
                dve.wait_ge(weights_used, idx + (streams[name].first + 1))
                o = out(idx)
                if scalar is None:
                    ins = nc.vector.tensor_tensor(o, o, bank(slot, 0, T), ALU.add)
                else:
                    ins = nc.vector.scalar_tensor_tensor(out=o, in0=bank(slot, 0, T), scalar=scalar(idx), in1=o, op0=ALU.mult, op1=ALU.add)
                ins.then_inc(evacuated[name], 1)
            streams[name].each(dve, take)

        def out_pe(pe):
            barrier(pe, "merge")
            gemm(pe, "out", DC, lambda k: merged[:, k, :])

            def ple(idx, slot, loads, i, u):
                pe.wait_ge(landed[slot], loads * 16)
                do = Do(pe, st_ple, "pe", idx)
                for half_ in range(2):
                    if idx or half_:
                        do.wait("act", "e0" if half_ else "e1", idx if half_ else idx - 1)
                    for c in range(4):
                        n = half_ * 4 + c
                        for k in range(2):
                            last = nc.tensor.matmul(bank(4 + c // 2, (c % 2) * T, T), ring[:, slot, k * 1024 + n * P:k * 1024 + (n + 1) * P],
                                                    pT[:, k, :], start=(k == 0), stop=(k == 1))
                    if half_ == 0:
                        do("p0", last)
                    else:
                        last.then_inc(weights_used, 1)
                do.end()
            streams["ple"].each(pe, ple)
            barrier(pe, "ple")
            norm_pe(pe, st_e, 0, e_sq, bank(6, 0, T), DC)
            barrier(pe, "out", "norm_e")
            gemm(pe, "ple_gate", DC, lambda k: xc[:, k, :])

        def out_act(act):
            barrier(act, "fox", "merge")
            for idx in range(2):
                do = Do(act, st_ple, "act", idx)
                for half_ in range(2):
                    if half_ == 0:
                        do.wait("pe", "p0")
                    else:
                        act.wait_ge(weights_used, streams["ple"].first + idx + 1)
                    do(f"e{half_}", nc.scalar.activation(e[:, idx * 8 + half_ * 4:idx * 8 + half_ * 4 + 4, :],
                                                         ps[:, 4:6, :].rearrange("p b (c t) -> p (b c) t", t=T), ACT.Copy))
                do.own()
            norm_act(act, st_e, 0, e, e_sq, e_root, bank(6, 0, T), T, 1.0 / D)

            def gate(idx, slot, loads, i, u):
                do = Do(act, st_pg, "dve", idx)
                act.wait_ge(weights_used, idx + (streams["ple_gate"].first + 1))
                if not (isinstance(idx, int) and idx < SLOTS):
                    do.wait("dve", "mixed", idx - SLOTS)
                nc.scalar.activation(gth[:, u, :], bank(slot, 0, T), ACT.Tanh, scale=0.5).then_inc(evacuated["ple_gate"], 1)
            streams["ple_gate"].each(act, gate)

        def out_dve(dve):
            add_block(dve, "out", lambda i: xc[:, i, :])
            norm_dve(dve, st_e, 0, lambda c: e[:, c, :], lambda c: e[:, c, :], e_root, lambda c: par("ple_gain", c), DC)
            barrier(dve, "norm_e", "out")

            def gate(idx, slot, loads, i, u):
                do = Do(dve, st_pg, "dve", idx)
                dve.wait_ge(evacuated["ple_gate"], idx + 1)
                v = e[:, idx, :]
                do("mixed", nc.vector.scalar_tensor_tensor(out=v, in0=gth[:, u, :], scalar=1.0, in1=v, op0=ALU.add, op1=ALU.mult))
                do.own()
                do("added", nc.vector.scalar_tensor_tensor(out=x2[:, idx, :], in0=v, scalar=0.5, in1=xc[:, idx, :], op0=ALU.mult, op1=ALU.add))
                do.end()
            streams["ple_gate"].each(dve, gate)
            barrier(dve, "ple_gate", "pg")
            do = Do(dve, st_x2, "dve")
            do("moved", nc.vector.tensor_copy(xc, x2))
            do.end()

        def n2_act(act):
            barrier(act, "x2")
            norm_act(act, st_n2[0], 0, xc, sq2, root2, bank(4, 0, T), T, 1.0 / D)
            act.wait_ge(ctx_loaded, 16)
            barrier(act, "norm2_0")
            norm_act(act, st_n2[1], 0, hcat[:, 1, :, :], sq2, root2, bank(5, 0, T), T, 1.0 / D)
            barrier(act, "norm2_1")
            do = Do(act, st_shift, "act")
            for c in range(2 * DC):
                s, k = c // DC, c % DC
                v = hcat[:, s, k, :]
                do(f"shift{c}", nc.scalar.activation(v, v, ACT.Identity, bias=modv[:, k, s:s + 1]))
            do.end()
            take_pairs(act, "y", lambda i: (yv[:, i, :], None), 2 * T, N_Z)
            copy_out(act, "l", lambda i: lv[:, i, :], T)

        def copy_out(act, name, out, n):
            def take(idx, slot, loads, i, u):
                act.wait_ge(weights_used, idx + (streams[name].first + 1))
                nc.scalar.activation(out(idx), bank(slot, 0, n), ACT.Copy).then_inc(evacuated[name], 1)
            streams[name].each(act, take)

        def n2_pe(pe):
            barrier(pe, "x2")
            norm_pe(pe, st_n2[0], 0, sq2, bank(4, 0, T), DC)
            norm_pe(pe, st_n2[1], 0, sq2, bank(5, 0, T), DC)
            barrier(pe, "norm2_1", "shift")

            product_pairs(pe, "y", lambda k: hcat[:, :, k, :], 2 * T, lambda slot: bank(slot).rearrange("p (s t) -> p s t", s=2))
            barrier(pe, "y")
            gemm(pe, "l", DC, lambda k: hcat[:, 0, k, :])

        def n2_dve(dve):
            do = Do(dve, st_gain, "dve")
            barrier(dve, "z")
            do("first", nc.vector.scalar_tensor_tensor(
                out=gain1v, in0=modv[:, DC:2 * DC, :], scalar=1.0, in1=par("norm1", 0, DC)[:, :, None].to_broadcast([P, DC, 2]),
                op0=ALU.add, op1=ALU.mult))
            do.own()
            norm_dve(dve, st_n2[0], 0, lambda c: xc[:, c, :], lambda c: hcat[:, 0, c, :], root2, lambda c: gain1v[:, c, 0:1], DC)
            dve.wait_ge(ctx_loaded, 16)
            norm_dve(dve, st_n2[1], 0, lambda c: hcat[:, 1, c, :], lambda c: hcat[:, 1, c, :], root2, lambda c: gain1v[:, c, 1:2], DC)
            barrier(dve, "y")
            do("second", nc.vector.scalar_tensor_tensor(
                out=gain2v, in0=modv[:, 4 * DC:5 * DC, 0], scalar=1.0, in1=par("norm2", 0, DC), op0=ALU.add, op1=ALU.mult))

        def mla_act(act):
            barrier(act, "y", "l")
            sq4 = msq.rearrange("p (c t) -> p c t", t=T)
            norm_act(act, st_cq, 0, lv[:, L_CQ:L_CQ + 4, :], sq4, mroot[:, 0:T], bank(4, 0, T), T, 1.0 / 512)
            barrier(act, "norm_cq")
            norm_act(act, st_ckv, 0, yv[:, Y_KV:Y_KV + 2, :], msq.rearrange("p (c t) -> p c t", t=2 * T), mroot, bank(5), 2 * T, 1.0 / 256)
            do = Do(act, st_kr, "act")
            do.wait("pe", "dup")
            do("ctx", nc.scalar.activation(krd[:, T:2 * T], bank(6, T, T), ACT.Copy))
            do.end()

            def head(idx, slot, loads, i, u):
                do = Do(act, st_mla, "act", idx)
                act.wait_ge(weights_used, idx + (streams["mla"].first + 1))
                do("qn", nc.scalar.activation(mq, bank(0, 0, T), ACT.Copy))
                do("qr", nc.scalar.activation(mqr[0:64, :], bank(0, T, T)[0:64, :], ACT.Copy))
                do("kn", nc.scalar.activation(mk, bank(1), ACT.Copy))
                do("v", nc.scalar.activation(mv, bank(2).rearrange("p (a b) -> p a b", b=P), ACT.Copy))
                do.wait("dve", "neg")
                for t in range(NT):
                    do(f"e{t}", nc.scalar.activation(me[:, t, :], bank(4 + t), ACT.Exp, bias=mmx[:, t:t + 1], scale=MLA_SCALE, accum_out=msm[:, t:t + 1]))
                for t in range(NT):
                    do.wait("pe", f"turned{t}")
                    do(f"et{t}", nc.scalar.activation(met[:, t, :], bank(6 + t), ACT.Copy))
                do.end()
            streams["mla"].each(act, head)

        def mla_pe(pe):
            barrier(pe, "y", "l")
            norm_pe(pe, st_cq, 0, msq.rearrange("p (c t) -> p c t", t=T), bank(4, 0, T), 4)
            norm_pe(pe, st_ckv, 0, msq.rearrange("p (c t) -> p c t", t=2 * T), bank(5), 2)
            do = Do(pe, st_kr, "pe")
            do("dup", nc.tensor.matmul(bank(6), con("dup"), yv[:, Y_KR, :], start=True, stop=True))
            do("rot", nc.tensor.matmul(bank(7, 0, T), con("duprot"), yv[:, Y_KR, 0:T], start=True, stop=True))
            do.end()
            barrier(pe, "norm_cq", "norm_ckv", "kr")

            def head(idx, slot, loads, i, u):
                do = Do(pe, st_mla, "pe", idx)
                pe.wait_ge(landed[slot], loads * 16)
                if not (isinstance(idx, int) and idx == 0):
                    do.wait("dve", "y", idx - 1)
                w = ring[:, slot, :]
                for k in range(4):
                    nc.tensor.matmul(bank(0, 0, T), w[:, k * 192:k * 192 + P], lv[:, L_CQ + k, :], start=(k == 0), stop=(k == 3))
                for k in range(4):
                    nc.tensor.matmul(bank(0, T, T)[0:64, :], w[:, k * 192 + P:k * 192 + 192], lv[:, L_CQ + k, :], start=(k == 0), stop=(k == 3))
                for k in range(2):
                    nc.tensor.matmul(bank(1), w[:, 768 + k * 256:768 + k * 256 + P], yv[:, Y_KV + k, :], start=(k == 0), stop=(k == 1))
                for j in range(4):
                    for k in range(2):
                        last = nc.tensor.matmul(bank(2, j * P, P), yv[:, Y_KV + k, j * P:(j + 1) * P],
                                                w[:, 768 + k * 256 + P:768 + (k + 1) * 256], start=(k == 0), stop=(k == 1))
                last.then_inc(weights_used, 1)
                do.wait("act", "qr")
                do("rot", nc.tensor.matmul(bank(3, 0, T)[0:64, :], con("rot")[0:64, 0:64], mqr[0:64, :], start=True, stop=True))
                do.wait("act", "kn")
                do.wait("dve", "sum")
                for t in range(NT):
                    nc.tensor.matmul(bank(4 + t), mq[:, t * P:(t + 1) * P], mk, start=True, stop=False)
                    last = nc.tensor.matmul(bank(4 + t), mqt[0:64, t * P:(t + 1) * P], krd[0:64, :], start=False, stop=True)
                do("s", last)
                for t in range(NT):
                    do.wait("dve", f"w{t}")
                    for j in range(4):
                        last = nc.tensor.transpose(bank(6 + t, j * P, P), me[:, t, j * P:(j + 1) * P], ident)
                    do(f"turned{t}", last)
                do.wait("act", "et1")
                for t in range(NT):
                    for j in range(4):
                        last = nc.tensor.matmul(bank(3, T + t * P, P), mv[:, j, :], met[:, t, j * P:(j + 1) * P], start=(j == 0), stop=(j == 3))
                do("o", last)
                do.end()
            streams["mla"].each(pe, head)

        def mla_dve(dve):
            norm_dve(dve, st_cq, 0, lambda c: lv[:, L_CQ + c, :], lambda c: lv[:, L_CQ + c, :], mroot[:, 0:T], lambda c: par("q_norm", c), 4)
            norm_dve(dve, st_ckv, 0, lambda c: yv[:, Y_KV + c, :], lambda c: yv[:, Y_KV + c, :], mroot, lambda c: par("kv_norm", c), 2)
            do = Do(dve, st_kr, "dve")
            do.wait("pe", "rot")
            do.wait("act", "ctx")
            do("cos", nc.vector.tensor_tensor(krd[:, 0:T], bank(6, 0, T), con("cos"), ALU.mult))
            do("sin", nc.vector.tensor_tensor(krt, bank(7, 0, T), con("sin"), ALU.mult))
            do.own()
            do("sum", nc.vector.tensor_tensor(krd[:, 0:T], krd[:, 0:T], krt, ALU.add))
            do.end()

            def head(idx, slot, loads, i, u):
                do = Do(dve, st_mla, "dve", idx)
                do.wait("act", "qr")
                do("cos", nc.vector.tensor_tensor(mqt[0:64, :], mqr[0:64, :], con("cos")[0:64, :], ALU.mult))
                do.wait("pe", "rot")
                do.own()
                do("sin", nc.vector.tensor_tensor(mqr[0:64, :], bank(3, 0, T)[0:64, :], con("sin")[0:64, :], ALU.mult))
                do.own()
                do("sum", nc.vector.tensor_tensor(mqt[0:64, :], mqt[0:64, :], mqr[0:64, :], ALU.add))
                do.wait("pe", "s")
                do("max", nc.vector.tensor_reduce(mmx, ps[:, 4:6, :], AX_X, ALU.max, negate=True))
                do.own()
                do("neg", nc.vector.tensor_scalar(mmx, mmx, MLA_SCALE, None, ALU.mult))
                do.wait("act", "e1")
                do("inv", nc.vector.reciprocal(msm, msm))
                do.own()
                for t in range(NT):
                    do(f"w{t}", nc.vector.tensor_scalar(me[:, t, :], me[:, t, :], msm[:, t:t + 1], None, ALU.mult))
                do.wait("pe", "o")
                do("y", nc.vector.tensor_copy(my[:, idx, :], bank(3, T, T)))
                do.end()
            streams["mla"].each(dve, head)

        def conv_stages():
            return ((st_ckvv, 16, lambda c: yv[:, c + Y_K, :].rearrange("p (s t) -> p s t", t=T), 8, 2),
                    (st_cvq, 8, lambda c: lv[:, bass.ds(c + L_Q, 1), :], 0, 1))

        def conv_dve(dve):
            barrier(dve, "mla")
            for st, n, chunk, first_w, seqs in conv_stages():
                def part(c, st=st, chunk=chunk, first_w=first_w, seqs=seqs):
                    do = Do(dve, st, "dve", c)
                    u, out = chunk(c), ctmp[:, 0:seqs, :]
                    do("mid", nc.vector.tensor_scalar(out, u, par("conv2_w", c + (2 * 24 + first_w)), None, ALU.mult))
                    for name, k in (("lm2", -2), ("lm1", -1), ("lp1", 1), ("lp2", 2)):
                        do.own()
                        lo, hi = max(0, -k), T - max(0, k)
                        o = out[:, :, lo:hi]
                        do(name, nc.vector.scalar_tensor_tensor(out=o, in0=u[:, :, lo + k:hi + k], scalar=par("conv2_w", c + ((2 + k) * 24 + first_w)),
                                                                in1=o, op0=ALU.mult, op1=ALU.add))
                    do.wait("act", "tanh")
                    do("out", nc.vector.scalar_tensor_tensor(out=u, in0=cth2[:, 0:seqs, :], scalar=1.0, in1=out, op0=ALU.add, op1=ALU.mult))
                    do.own()
                    do.end()
                rounds(dve, n, part)
            for st, n, chunk, w in l2_stages():
                def norm(c, st=st, chunk=chunk, w=w):
                    do = Do(dve, st, "dve", c)
                    do.wait("act", "root")
                    do("inv", nc.vector.reciprocal(mroot[:, 0:w], mroot[:, 0:w]))
                    do.own()
                    do("out", nc.vector.scalar_tensor_tensor(out=chunk(c), in0=chunk(c), scalar=0.5 if w == 2 * T else 0.5 * SCALE,
                                                             in1=mroot[:, 0:w], op0=ALU.mult, op1=ALU.mult))
                    do.end()
                rounds(dve, n, norm)

        def l2_stages():
            return ((st_lk, 8, lambda c: yv[:, c + Y_K, :], 2 * T), (st_lq, 8, lambda c: lv[:, c + L_Q, :], T))

        def conv_act(act):
            for st, n, chunk, first_w, seqs in conv_stages():
                def part(c, st=st, seqs=seqs):
                    do = Do(act, st, "act", c)
                    do.wait("dve", "lp2")
                    do("tanh", nc.scalar.activation(cth2[:, 0:seqs, :], ctmp[:, 0:seqs, :], ACT.Tanh, scale=0.5))
                    do.end()
                rounds(act, n, part)
            barrier(act, "conv_kv", "conv_q")
            for st, n, chunk, w in l2_stages():
                def norm(c, st=st, chunk=chunk, w=w):
                    do = Do(act, st, "act", c)
                    do("squares", nc.scalar.activation(msq[:, 0:w], chunk(c), ACT.Square, scale=0.5))
                    do.wait("pe", "sums")
                    if not (isinstance(c, int) and c == 0):
                        do.wait("dve", "out", c - 1)
                    do("root", nc.scalar.activation(mroot[:, 0:w], bank(4, 0, w), ACT.Sqrt, bias=par("eps")))
                    do.end()
                rounds(act, n, norm)
                S["l2_k"].finished(act)

        def conv_pe(pe):
            barrier(pe, "mla", "conv_kv", "conv_q")
            for st, n, chunk, w in l2_stages():
                def norm(c, st=st, w=w):
                    do = Do(pe, st, "pe", c)
                    do.wait("act", "squares")
                    if not (isinstance(c, int) and c == 0):
                        do.wait("act", "root", c - 1)
                    do("sums", nc.tensor.matmul(bank(4, 0, w), ones, msq[:, 0:w], start=True, stop=True))
                    do.end()
                rounds(pe, n, norm)
                S["l2_k"].finished(pe)

        ab = yv[:, Y_AB, :]
        LO, HI = slice(64, 96), slice(96, 128)

        def decay_dve(dve):
            barrier(dve, "l2_q")
            dve.wait_ge(dnc_loaded, 16)
            do = Do(dve, st_dec, "dve")
            do("shifted", nc.vector.tensor_scalar(gv, ab, par("dt_bias"), None, ALU.add))
            do.own()
            softplus_dve(do, gv, gt1, gt2, gt3, gsp)
            do.own()
            do.wait("act", "ea")
            do("scale", nc.vector.tensor_scalar(gsp, gsp, ea, -1.0, ALU.mult, ALU.mult))
            do.wait("act", "tanh_b")
            do.own()
            do("half_b", nc.vector.tensor_scalar(gt3[HI, :], gt3[HI, :], 1.0, 0.5, ALU.add, ALU.mult))
            do.own()
            do("beta", nc.vector.tensor_copy(gsp[HI, :], gt3[HI, :]))
            do.wait("act", "glk")
            d4 = lambda v: v.rearrange("p (t d h) -> p d t h", t=4, d=2)
            c4 = lambda v: v.rearrange("p (d t h) -> p d t h", t=4, d=2)
            do("sub", nc.vector.tensor_tensor(c4(egl), d4(gl), c4(gcum), ALU.subtract))
            do.wait("act", "eg_exp")
            do("beg", nc.vector.tensor_tensor(c4(beg), d4(bT), c4(eg), ALU.mult))
            do.end()

        def decay_act(act):
            barrier(act, "l2_q")
            do = Do(act, st_dec, "act")
            softplus_act(do, gt1)
            do("ea", nc.scalar.activation(ea, par("a_log"), ACT.Exp))
            do.wait("dve", "sp_out")
            do("tanh_b", nc.scalar.activation(gt3[HI, :], ab[HI, :], ACT.Tanh, scale=0.5))
            do.wait("pe", "turned")
            tv = bank(4).rearrange("p (t n) -> p t n", n=P)
            g16 = lambda v: v.rearrange("p (t n) -> p t n", n=16)
            do("gk", nc.scalar.activation(g16(gT), tv[:, :, 64:80], ACT.Copy))
            do("bk", nc.scalar.activation(g16(bT), tv[:, :, 96:112], ACT.Copy))
            do.wait("pe", "cums")
            do("cumk", nc.scalar.activation(gcum, bank(5, 0, 64), ACT.Copy))
            do("glk", nc.scalar.activation(gl, bank(5, 64, 64), ACT.Copy))
            do.wait("dve", "sub")
            do("egl_exp", nc.scalar.activation(egl, egl, ACT.Exp))
            do("eg_exp", nc.scalar.activation(eg, bank(5, 0, 64), ACT.Exp))
            do("chunk_exp", nc.scalar.activation(egls, bank(5, 128, 128), ACT.Exp))
            do.end()

        def decay_pe(pe):
            do = Do(pe, st_dec, "pe")
            do.wait("dve", "beta")
            for t in range(4):
                last = nc.tensor.transpose(bank(4, t * P, P), gsp[:, t * P:(t + 1) * P], ident)
            do("turned", last)
            do.wait("act", "gk")
            g4 = gT.rearrange("p (t d h) -> p d t h", t=4, d=2)
            for d, m in enumerate(("le", "ge")):
                nc.tensor.matmul(bank(5, 32 * d, 32).rearrange("p (t h) -> p t h", t=4), dcon(m), g4[:, d, :, :], start=True, stop=True)
            nc.tensor.matmul(bank(5, 64, 64), dcon("chunk"), gT, start=True, stop=True)
            nc.tensor.matmul(bank(5, 128, 64), dcon("half0"), gT, start=True, stop=True)
            do("cums", nc.tensor.matmul(bank(5, 192, 64), dcon("half1"), gT, start=True, stop=True))
            do.end()

        def of_head(v, h):
            return v.rearrange("p (u h) -> p u h", h=BC)[:, :, bass.ds(h, 1)]

        def spread(v, d, n=4):
            return v[:, d * n:(d + 1) * n, :].to_broadcast([P, n, P])

        def over_tiles(m, n=4):
            return m[:, None, :].to_broadcast([P, n, P])

        def where(s, d):
            base, r = (2, s) if s < 4 else (0, s - 4)
            r = r if d == 0 else 3 - r
            t = base + r // 2
            return d * 4 + t, t, 64 * (r % 2)

        def two(b):
            return ps[:, b:b + 2, :].rearrange("p b (u n) -> p (b u) n", n=P)

        def dn_dve(dve):
            barrier(dve, "decay")

            def head(h):
                do = Do(dve, st_dn, "dve", h)
                g3 = gT.rearrange("p (t n) -> p t n", n=16)
                b3 = bT.rearrange("p (t n) -> p t n", n=16)
                gsel = lambda v, d: v[:, :, bass.ds(h + d * 8, 1)].to_broadcast([P, 4, P])
                gc = of_head(gcum, h)
                for d, m in enumerate(("le", "ge")):
                    do(f"rg{d}", nc.vector.tensor_tensor(rg[:, 4 * d:4 * d + 4, :], over_tiles(dcon(m)), gsel(g3, d), ALU.mult))
                do.wait("pe", "rows")
                for d in range(2):
                    do(f"diff{d}", nc.vector.tensor_tensor(dec[:, 4 * d:4 * d + 4, :], bank(2 + d).rearrange("p (t n) -> p t n", n=P), spread(gc, d), ALU.subtract))
                do.wait("act", "dec_t")
                for d, m in enumerate(("le", "ge")):
                    do(f"tmask{d}", nc.vector.tensor_tensor(att[:, 2 * d:2 * d + 2, :], att[:, 2 * d:2 * d + 2, :], over_tiles(dcon(m), 2), ALU.mult))
                do.wait("pe", "gram")
                do.own()
                for d in range(2):
                    do(f"att{d}", nc.vector.tensor_tensor(att[:, 2 * d:2 * d + 2, :], att[:, 2 * d:2 * d + 2, :],
                                                          bank(5, 0, 256).rearrange("p (t n) -> p t n", n=P), ALU.mult))
                do.wait("act", "dec")
                for d, m in enumerate(("gt", "lt")):
                    do(f"smask{d}", nc.vector.tensor_tensor(dec[:, 4 * d:4 * d + 4, :], dec[:, 4 * d:4 * d + 4, :], over_tiles(dcon(m)), ALU.mult))
                for d in range(2):
                    do(f"gb{d}", nc.vector.tensor_tensor(mb[:, 4 * d:4 * d + 4, :], bank(4).rearrange("p (t n) -> p t n", n=P), gsel(b3, d), ALU.mult))
                do.own()
                do("m", nc.vector.tensor_tensor(mb, mb, dec, ALU.mult))
                do.own()
                for d, m in enumerate(("level", "level_t")):
                    do(f"l0{d}", nc.vector.tensor_tensor(xb[:, 4 * d:4 * d + 4, :], mb[:, 4 * d:4 * d + 4, :], over_tiles(dcon(m)), ALU.mult))
                do.own()
                do("x", nc.vector.scalar_tensor_tensor(out=xb, in0=xb, scalar=-1.0, in1=over_tiles(ident, NU), op0=ALU.mult, op1=ALU.add))
                do.wait("act", "mt")
                for d, m in enumerate(("level_t", "level")):
                    do(f"l0t{d}", nc.vector.tensor_tensor(xt[:, 4 * d:4 * d + 4, :], mt[:, 4 * d:4 * d + 4, :], over_tiles(dcon(m)), ALU.mult))
                do.own()
                do("xt", nc.vector.scalar_tensor_tensor(out=xt, in0=xt, scalar=-1.0, in1=over_tiles(ident, NU), op0=ALU.mult, op1=ALU.add))
                for l in LV:
                    if l > 1:
                        do.wait("pe", f"p{l - 1}")
                    for d, m in enumerate(("level_t", "level")):
                        do(f"a{l}{d}", nc.vector.tensor_tensor(atl[:, 4 * d:4 * d + 4, :], mt[:, 4 * d:4 * d + 4, :], over_tiles(dcon(m, l)), ALU.mult))
                    do.wait("pe", f"xt{l}")
                    if l in INNER:
                        do(f"x{l}", nc.vector.tensor_tensor(xb, xb, two(2), ALU.subtract))
                    do(f"xt{l}", nc.vector.tensor_tensor(xt, xt, two(6), ALU.subtract))
                do.own()
                for d in range(2):
                    do(f"vb{d}", nc.vector.tensor_tensor(vb[:, 4 * d:4 * d + 4, :], vtm, gsel(b3, d), ALU.mult))
                for d in range(2):
                    do(f"ke{d}", nc.vector.tensor_tensor(kbe[:, 4 * d:4 * d + 4, :], ktm, spread(of_head(beg, h), d), ALU.mult))
                for d in range(2):
                    do(f"kd{d}", nc.vector.tensor_tensor(kdec[:, 4 * d:4 * d + 4, :], ktm, spread(of_head(egl, h), d), ALU.mult))
                do.wait("pe", "w")
                do("w", nc.vector.tensor_copy(wt, two(6)))
                do("s0", nc.vector.memset(state, 0.0))
                do.wait("act", "u")
                ego = of_head(eg, h)
                e5 = egls.rearrange("p (f t d h) -> p f t d h", f=2, t=4, d=2)
                for s, d in SC:
                    u, t, p0 = where(s, d)
                    rows = slice(p0, p0 + 64)
                    do.wait("pe", f"ws{s}{d}")
                    do(f"vn{s}{d}", nc.vector.tensor_tensor(vnew[rows, d, :], ub[rows, u, :], ps[rows, 2 + d, 0:P], ALU.subtract))
                    do.wait("pe", f"su{s}{d}")
                    if s >= 4:
                        ob = (ob0, ob1)[d]
                        do(f"oi{s}{d}", nc.vector.tensor_scalar(ob[rows, t, :], ps[rows, 2 + d, P:2 * P], ego[rows, u, :], None, ALU.mult))
                        do.own()
                        do(f"o{s}{d}", nc.vector.tensor_tensor(ob[rows, t, :], ob[rows, t, :], ps[rows, 2 + d, 2 * P:3 * P], ALU.add))
                    do(f"st{s}{d}", nc.vector.scalar_tensor_tensor(
                        out=state[:, d, :], in0=state[:, d, :], scalar=e5[:, p0 // 64, t, d, bass.ds(h, 1)], in1=bank(4 + d, 0, P), op0=ALU.mult, op1=ALU.add))
                do.own()
                do("osum", nc.vector.tensor_tensor(ob0, ob0, ob1, ALU.add))
                do.wait("pe", "ot")
                do("ot", nc.vector.tensor_scalar(lv[:, h + L_Q, :], bank(6, 0, T), 1.0, None, ALU.mult))
                do.end()
            rounds(dve, BC, head)

        def dn_act(act):
            barrier(act, "decay")

            def head(h):
                do = Do(act, st_dn, "act", h)
                if not (isinstance(h, int) and h == 0):
                    do.wait("pe", "ot", h - 1)
                do("k", nc.scalar.activation(kst, yv[:, h + Y_K, :], ACT.Copy))
                do("v", nc.scalar.activation(vst, yv[:, h + Y_V, :], ACT.Copy, scale=0.5))
                do("q", nc.scalar.activation(qst, lv[:, h + L_Q, :], ACT.Copy))
                do.wait("pe", "turned")
                do("ktm", nc.scalar.activation(ktm, bank(0).rearrange("p (t n) -> p t n", n=P), ACT.Copy))
                do("vtm", nc.scalar.activation(vtm, bank(1).rearrange("p (t n) -> p t n", n=P), ACT.Copy))
                do.wait("dve", "diff1")
                att4 = att.rearrange("p (d t) n -> p d t n", d=2)
                lat = dec.rearrange("p (d t) n -> p d t n", d=2)[:, :, 0:2, :]
                do("relu_t", nc.scalar.activation(att4, lat, ACT.Relu, scale=-1.0))
                do("relu", nc.scalar.activation(mt, dec, ACT.Relu))
                do.own()
                do("dec", nc.scalar.activation(dec, mt, ACT.Exp, scale=-1.0))
                do("dec_t", nc.scalar.activation(att, att, ACT.Exp, scale=-1.0))
                do.wait("pe", "mt")
                do("mt", nc.scalar.activation(mt, two(6), ACT.Copy))
                for l in LV:
                    do.wait("pe", f"p{l}")
                    do(f"p{l}", nc.scalar.activation(pbuf, two(0), ACT.Copy))
                do.wait("pe", "u")
                do("u", nc.scalar.activation(ub, two(0), ACT.Copy))
                do.end()
            rounds(act, BC, head)

        def dn_pe(pe):
            barrier(pe, "decay")

            def head(h):
                do = Do(pe, st_dn, "pe", h)
                do.wait("act", "q")
                for t in range(4):
                    nc.tensor.transpose(bank(0, t * P, P), kst[:, t * P:(t + 1) * P], ident)
                for t in range(4):
                    last = nc.tensor.transpose(bank(1, t * P, P), vst[:, t * P:(t + 1) * P], ident)
                do("turned", last)
                do.wait("dve", "rg1")
                for d in range(2):
                    last = nc.tensor.matmul(bank(2 + d), ones, rg[:, 4 * d:4 * d + 4, :].rearrange("p u n -> p (u n)"), start=True, stop=True)
                do("rows", last)
                for t in range(4):
                    nc.tensor.matmul(bank(4, t * P, P), kst[:, t * P:(t + 1) * P], kst[:, t * P:(t + 1) * P], start=True, stop=True)
                for t in range(2):
                    last = nc.tensor.matmul(bank(5, t * P, P), kst[:, t * P:(t + 1) * P], qst[:, t * P:(t + 1) * P], start=True, stop=True)
                do("gram", last)
                do.wait("dve", "m")
                for u in range(NU):
                    last = nc.tensor.transpose(two(6)[:, u, :], mb[:, u, :], ident)
                do("mt", last)
                for l in LV:
                    do.wait("dve", f"a{l}1")
                    for u in range(NU):
                        last = nc.tensor.matmul(two(0)[:, u, :], atl[:, u, :], xb[:, u, :], start=True, stop=True)
                    do(f"p{l}", last)
                    do.wait("act", f"p{l}")
                    if l in INNER:
                        for u in range(NU):
                            last = nc.tensor.matmul(two(2)[:, u, :], xt[:, u, :], pbuf[:, u, :], start=True, stop=True)
                        do(f"x{l}", last)
                    for u in range(NU):
                        last = nc.tensor.matmul(two(6)[:, u, :], pbuf[:, u, :], xt[:, u, :], start=True, stop=True)
                    do(f"xt{l}", last)
                    do.wait("dve", f"xt{l}")
                do.wait("dve", "ke1")
                for u in range(NU):
                    last = nc.tensor.matmul(two(0)[:, u, :], xt[:, u, :], vb[:, u, :], start=True, stop=True)
                do("u", last)
                for u in range(NU):
                    last = nc.tensor.matmul(two(6)[:, u, :], kbe[:, u, :], xt[:, u, :], start=True, stop=True)
                do("w", last)
                do.wait("dve", "s0")
                do.wait("act", "u")

                def reads_state(s, d):
                    u, t, p0 = where(s, d)
                    rows = slice(p0, p0 + 64)
                    if s:
                        do.wait("dve", f"st{s - 1}{d}")
                    last = nc.tensor.matmul(ps[rows, 2 + d, 0:P], wt[:, u, rows], state[:, d, :], start=True, stop=True)
                    do(f"ws{s}{d}", last)

                def from_new(s, d):
                    u, t, p0 = where(s, d)
                    rows = slice(p0, p0 + 64)
                    do.wait("dve", f"vn{s}{d}")
                    if s >= 4:
                        nc.tensor.matmul(ps[rows, 2 + d, P:2 * P], qst[:, t * P + p0:t * P + p0 + 64], state[:, d, :], start=True, stop=True)
                        do(f"oa{s}{d}", nc.tensor.matmul(ps[rows, 2 + d, 2 * P:3 * P], att[rows, 2 * d + t, rows], vnew[rows, d, :], start=True, stop=True))
                    do(f"su{s}{d}", nc.tensor.matmul(bank(4 + d, 0, P), kdec[rows, u, :], vnew[rows, d, :], start=True, stop=True))
                for s in range(8):
                    for d in range(2):
                        reads_state(s, d)
                    for d in range(2):
                        from_new(s, d)
                do.wait("dve", "osum")
                for t in range(NT):
                    last = nc.tensor.transpose(bank(6, t * P, P), ob0[:, t, :], ident)
                do("ot", last)
                do.end()
            rounds(pe, BC, head)

        oflat = cut(L_AT + L_Q * T, BC * T)
        ov = lv[:, L_Q:L_Q + BC, :]
        zv = lv[:, L_Z:L_Z + BC, :]

        def dno_act(act):
            barrier(act, "dn")
            for it in range(2):
                do = Do(act, st_on, "act", it)
                do("squares", nc.scalar.activation(osq, oflat[:, it * 1024:(it + 1) * 1024], ACT.Square))
                do.wait("pe", "sums1")
                if it:
                    do.wait("dve", "scaled3", it - 1)
                do("root", nc.scalar.activation(oroot, ps[:, 4:6, :].rearrange("p b n -> p (b n)"), ACT.Sqrt, bias=par("eps"), scale=1.0 / P))
                do.end()
            do = Do(act, st_og, "act")
            do("tanh", nc.scalar.activation(og, zv, ACT.Tanh, scale=0.5))
            do.end()

        def dno_pe(pe):
            for it in range(2):
                do = Do(pe, st_on, "pe", it)
                do.wait("act", "squares")
                do("sums0", nc.tensor.matmul(bank(4), ones, osq[:, 0:512], start=True, stop=True))
                do("sums1", nc.tensor.matmul(bank(5), ones, osq[:, 512:1024], start=True, stop=True))
                do.end()

        def dno_dve(dve):
            for it in range(2):
                do = Do(dve, st_on, "dve", it)
                do.wait("act", "root")
                do("inv", nc.vector.reciprocal(oroot, oroot))
                do.own()
                for c in range(4):
                    v = ov[:, it * 4 + c, :]
                    do(f"scaled{c}", nc.vector.scalar_tensor_tensor(out=v, in0=v, scalar=par("dn_norm"), in1=oroot[:, c * T:(c + 1) * T], op0=ALU.mult, op1=ALU.mult))
                do.end()
            do = Do(dve, st_og, "dve")
            do.wait("act", "tanh")
            do("silu", nc.vector.scalar_tensor_tensor(out=og, in0=og, scalar=1.0, in1=zv, op0=ALU.add, op1=ALU.mult))
            do.own()
            barrier(dve, "dn_out")
            do("out", nc.vector.scalar_tensor_tensor(out=ov, in0=og, scalar=0.5, in1=ov, op0=ALU.mult, op1=ALU.mult))
            do.end()

        def merge2_pe(pe):
            barrier(pe, "dn_gate")

            def part(idx, slot, loads, i, u):
                y = (my, ov)[u % 2]
                pe.wait_ge(landed[slot], loads * 16)
                if not (isinstance(idx, int) and idx < SLOTS):
                    pe.wait_ge(st_merge2.steps["act"].sem, st_merge2.steps["act"].at("y", idx - SLOTS))
                for k in range(DC):
                    nc.tensor.matmul(bank(slot, 0, T), ring[:, slot, k * P:(k + 1) * P], hcat[:, 0, k, :], start=(k == 0), stop=(k == DC - 1))
                for k in range(BC):
                    last = nc.tensor.matmul(bank(4 + slot, 0, T), ring[:, slot, D + k * P:D + (k + 1) * P], y[:, k, :],
                                            start=(k == 0), stop=(k == BC - 1))
                last.then_inc(weights_used, 1)
            streams["merge2"].each(pe, part)
            barrier(pe, "merge2")
            gemm(pe, "out2", DC, lambda k: merged2[:, k, :])

        def merge2_act(act):
            barrier(act, "dn_gate")

            def part(idx, slot, loads, i, u):
                do = Do(act, st_merge2, "act", idx)
                act.wait_ge(weights_used, idx + (streams["merge2"].first + 1))
                if not (isinstance(idx, int) and idx < 2):
                    do.wait("dve", "summed", idx - 2)
                do("gate", nc.scalar.activation(m2th[:, u % 2, :], bank(slot, 0, T), ACT.Tanh, scale=0.5))
                do("y", nc.scalar.activation(m2tm[:, u % 2, :], bank(4 + slot, 0, T), ACT.Copy, scale=0.5))
                do.end()
            streams["merge2"].each(act, part)

        def merge2_dve(dve):
            barrier(dve, "dn_gate")

            def part(idx, slot, loads, i, u):
                do = Do(dve, st_merge2, "dve", idx)
                do.wait("act", "y")
                d = merged2[:, i * 2 + u // 2, :]
                dst = d if u % 2 == 0 else m2tm[:, 1, :]
                do("scaled", nc.vector.scalar_tensor_tensor(out=dst, in0=m2th[:, u % 2, :], scalar=1.0, in1=m2tm[:, u % 2, :], op0=ALU.add, op1=ALU.mult))
                do.own()
                do("summed", nc.vector.tensor_copy(gains[:, 48:49], par("eps")) if u % 2 == 0 else nc.vector.tensor_tensor(d, d, dst, ALU.add))
                do.end()
            streams["merge2"].each(dve, part)
            add_block(dve, "out2", lambda i: xc[:, i, :], scalar=lambda i: modv[:, i + 2 * DC, 0:1])

        def choose_act(act):
            barrier(act, "out2")
            norm_act(act, st_np, 0, xc, psq, proot, bank(4, 0, T), T, 1.0 / D)
            barrier(act, "norm_p")
            do = Do(act, st_sh2, "act")
            for c in range(DC):
                do(f"shift{c}", nc.scalar.activation(hp[:, c, :], hp[:, c, :], ACT.Identity, bias=modv[:, 3 * DC + c, 0:1]))
            do.end()
            copy_out(act, "peer_q", lambda i: pq[:, i, :], T)
            do = Do(act, st_sc, "act")
            for b in range(8):
                do.wait("pe", f"s{b}")
                do(f"k{b}", nc.scalar.activation(scores[:, 4 * b:4 * b + 4, :], bank(b).rearrange("p (r n) -> p r n", n=P), ACT.Copy))
            do.end()

            def head(r):
                do = Do(act, st_cand, "act", r)
                do.wait("dve", "neg")
                do("exp", nc.scalar.activation(cexp, cand, ACT.Exp, bias=csum[:, 0:1]))
                do.end()
            rounds(act, DC, head)
            do = Do(act, st_mt, "act")
            do.wait("pe", "idx")
            do("idx", nc.scalar.activation(idxt, bank(0).rearrange("p (a b) -> p a b", b=T), ACT.Copy))
            for b in range(8):
                do.wait("pe", f"m{b}")
                do(f"m{b}", nc.scalar.activation(mixt[:, 2 * b:2 * b + 2, :], bank((b + 1) % 8).rearrange("p (a t) -> p a t", t=T), ACT.Copy))
            do.end()

        def choose_pe(pe):
            barrier(pe, "out2")
            norm_pe(pe, st_np, 0, psq, bank(4, 0, T), DC)
            barrier(pe, "norm_p", "shift2")
            gemm(pe, "peer_q", DC, lambda k: hp[:, k, :])
            barrier(pe, "peer_q")
            do = Do(pe, st_sc, "pe")
            for b in range(8):
                for j in range(4):
                    t, c = divmod(4 * b + j, DC)
                    last = nc.tensor.matmul(bank(b, j * P, P), pq[:, c, t * P:(t + 1) * P], misc[:, 512 + (c % 2) * P:512 + (c % 2 + 1) * P],
                                            start=True, stop=True)
                do(f"s{b}", last)
            do.end()
            barrier(pe, "scores", "cand")
            do = Do(pe, st_mt, "pe")
            do.wait("dve", "idx1")
            for half_ in range(2):
                for t in range(NT):
                    last = nc.tensor.transpose(bank(0, half_ * T + t * P, P), idxp[:, 2 * t + half_, :], ident)
            do("idx", last)
            for b in range(8):
                if b == 7:
                    do.wait("act", "idx")
                for j in range(2):
                    for t in range(NT):
                        last = nc.tensor.transpose(bank((b + 1) % 8, j * T + t * P, P), mix[:, t, 2 * b + j, :], ident)
                do(f"m{b}", last)
            do.end()

        def choose_dve(dve):
            barrier(dve, "out2")
            norm_dve(dve, st_np, 0, lambda c: xc[:, c, :], lambda c: hp[:, c, :], proot, lambda c: gain2v[:, c:c + 1], DC)
            barrier(dve, "scores")

            def top(r):
                do = Do(dve, st_top, "dve", r)
                do("row", nc.vector.tensor_copy(krow, scores[:, r, :]))
                do.own()
                do("gate0", nc.vector.memset(gated, 0.0))
                do("m0", nc.vector.max(kval[:, 0:8], krow))
                do.own()
                do("gate1", nc.vector.memset(gated, 0.0))
                do("i0", nc.vector.max_index(kidx[:, 0:8], kval[:, 0:8], krow))
                do("rest", nc.vector.match_replace(krest, kval[:, 0:8], krow, -BIG))
                do.own()
                do("gate2", nc.vector.memset(gated, 0.0))
                do("m1", nc.vector.max(kval[:, 8:16], krest))
                do.own()
                do("gate3", nc.vector.memset(gated, 0.0))
                do("i1", nc.vector.max_index(kidx[:, 8:16], kval[:, 8:16], krest))
                do("values", nc.vector.tensor_copy(topv[:, r, :], kval))
                do.own()
                do("indices", nc.vector.tensor_copy(topi[:, r, :], kidx))
                do.own()
                do.end()
            rounds(dve, 2 * DC, top)
            S["top"].finished(dve)

            def head(r):
                do = Do(dve, st_cand, "dve", r)
                cv = cand.rearrange("p (a b) -> p a b", b=TOPK)
                do("sum", nc.vector.tensor_tensor(cv, topv[:, bass.ds(r * 2, 1), :].rearrange("p o k -> p k o").to_broadcast([P, TOPK, TOPK]),
                                                  topv[:, bass.ds(r * 2 + 1, 1), :].to_broadcast([P, TOPK, TOPK]), ALU.add))
                do.own()
                do("gate0", nc.vector.memset(gated, 0.0))
                do("m0", nc.vector.max(c8[:, 0, :], cand))
                do.own()
                do("gate1", nc.vector.memset(gated, 0.0))
                do("r0", nc.vector.match_replace(crest, c8[:, 0, :], cand, -BIG))
                do.own()
                do("gate2", nc.vector.memset(gated, 0.0))
                do("m1", nc.vector.max(c8[:, 1, :], crest))
                do.own()
                do("gate3", nc.vector.memset(gated, 0.0))
                do("r1", nc.vector.match_replace(crest, c8[:, 1, :], crest, -BIG))
                do.own()
                do("chosen", nc.vector.tensor_tensor(crest, crest, cand, ALU.is_lt))
                do("neg", nc.vector.tensor_scalar(csum[:, 0:1], c8[:, 0, 0:1], -1.0, None, ALU.mult))
                do.wait("act", "exp")
                do.own()
                do("masked", nc.vector.tensor_tensor(cexp, cexp, crest, ALU.mult))
                do.own()
                do("total", nc.vector.tensor_reduce(csum[:, 1:2], cexp, AX_X, ALU.add))
                do.own()
                do("inv", nc.vector.reciprocal(csum[:, 1:2], csum[:, 1:2]))
                do.own()
                o = mix_out(r)
                do("out", nc.vector.tensor_scalar(o, cexp.rearrange("p (a b) -> p a b", b=TOPK), csum[:, 1:2], None, ALU.mult))
                do.end()

            for t in range(NT):
                if t == 0:
                    head(0)
                with dve.Fori(8 * t + (t == 0), 8 * t + 8) as r:
                    mix_tile[0] = t
                    head(r)
            do = Do(dve, st_mt, "dve")
            for t in range(NT):
                do(f"idx{t}", nc.vector.tensor_copy(
                    idxp[:, 2 * t:2 * t + 2, :].rearrange("p q (h k) -> p q h k", k=TOPK),
                    topi[:, DC * t:DC * t + DC, :].rearrange("p (h q) k -> p q h k", q=2)))
            do.end()

        mix_tile = [0]

        def mix_out(r):
            t = mix_tile[0]
            return mix5[:, t, :, bass.ds(r - 8 * t, 1), :].rearrange("p a o b -> p a (o b)")

        def by_groups(eng, q, body):
            if q == 0:
                body(0)
            with eng.Fori(4 * q + (q == 0), 4 * q + 4) as g:
                body(g)

        def later(r, n):
            return not (isinstance(r, int) and r < n)

        def expw_dve(dve):
            barrier(dve, "mix")
            dve.wait_ge(peer_loaded, 16)

            def group(g):
                for u in range(4):
                    r = g * 4 + u
                    bd, hot1, hot2 = hots[u]
                    if later(r, 4):
                        dve.wait_ge(weights_made, r - 3)
                    mt4 = mixtf.rearrange("p (a t) -> p t a", t=T)[:, bass.ds(r * NB4, NB4), :]
                    nc.vector.tensor_tensor(
                        bd.rearrange("p t (h a) -> p t h a", a=TOPK), same_head.rearrange("p (h a) -> p h a", a=TOPK)[:, None, :, :].to_broadcast([P, NB4, 8, TOPK]),
                        mt4[:, :, None, :].to_broadcast([P, NB4, 8, TOPK]), ALU.mult)
                    for k, hot in enumerate((hot1, hot2)):
                        last = nc.vector.tensor_tensor(hot, iota[:, None, :].to_broadcast([P, NB4, P]),
                                                       idxt[:, k, bass.ds(r * NB4, NB4)].rearrange("p (t o) -> p t o", o=1).to_broadcast([P, NB4, P]), ALU.is_equal)
                    last.then_inc(hot_made, 1)
            for q in range(4):
                by_groups(dve, q, group)

        def expw_pe(pe):
            barrier(pe, "mix")

            def group(g):
                for pair in range(2):
                    for u in (2 * pair, 2 * pair + 1):
                        r = g * 4 + u
                        pe.wait_ge(hot_made, r + 1)
                        if later(r, 2):
                            pe.wait_ge(spread_kept, r - 1)
                        bd, hot1, hot2 = hots[u]
                        for n in range(NB4):
                            last = nc.tensor.matmul(bank(u % 2, n * P, P), bd[:, n, :], hot2[:, n, :], start=True, stop=True)
                        last.then_inc(spread_made, 1)
                    for u in (2 * pair, 2 * pair + 1):
                        r = g * 4 + u
                        pe.wait_ge(spread_kept, r + 1)
                        if later(r, 2):
                            pe.wait_ge(weights_kept, r - 1)
                        for n in range(NB4):
                            last = nc.tensor.matmul(bank(2 + u % 2, n * P, P), rbuf[u % 2][:, n, :], hots[u][1][:, n, :], start=True, stop=True)
                        last.then_inc(weights_made, 1)
            for q in range(4):
                by_groups(pe, q, group)

        def expw_act(act):
            for q in range(4):
                if q >= 2:
                    act.wait_ge(w_stored[q % 2], 16)

                def group(g, q=q):
                    for pair in range(2):
                        for u in (2 * pair, 2 * pair + 1):
                            r = g * 4 + u
                            act.wait_ge(spread_made, r + 1)
                            if later(r, 2):
                                act.wait_ge(weights_made, r - 1)
                            nc.scalar.activation(rbuf[u % 2], bank(u % 2).rearrange("p (t n) -> p t n", n=P), ACT.Copy).then_inc(spread_kept, 1)
                        for u in (2 * pair, 2 * pair + 1):
                            r = g * 4 + u
                            act.wait_ge(weights_made, r + 1)
                            kept_to = ewf[q % 2].rearrange("p (i t) -> p t i", t=64)[:, bass.ds(r * NB4 - 64 * q, NB4), :]
                            quarter_copy(act, kept_to, bank(2 + u % 2).rearrange("p (t i) -> p t i", i=P))
                by_groups(act, q, group)

        def quarter_copy(act, out, src):
            nc.scalar.activation(out, src, ACT.Copy).then_inc(weights_kept, 1)

        def pairs(eng, body):
            for g in range(2):
                body(g, g)
            with eng.Fori(1, NG // 2 - 1) as i:
                for k in range(2):
                    body(i * 2 + k, k)
            for g in range(NG - 2, NG):
                body(g, g % 2)

        def hidden_pe(pe, g, par_):
            for s in range(GROUP):
                pe.wait_ge(u_landed[s], g * 16 + 16)
                if not (isinstance(g, int) and g == 0):
                    pe.wait_ge(hidden_taken, g * GROUP + (s - GROUP + 1))
                for k in range(DC):
                    last = nc.tensor.matmul(bank(s, 0, T), ring[:, s, k * P:(k + 1) * P], hp[:, k, :], start=(k == 0), stop=(k == DC - 1))
                last.then_inc(hidden_made, 1)

        def experts_pe(pe):
            pe.wait_ge(weights_kept, NR)
            hidden_pe(pe, 0, 0)

            def group(g, k):
                if not (isinstance(g, int) and g == NG - 1):
                    hidden_pe(pe, g + 1, 1 - k)
                pe.wait_ge(hidden_weighted, g * GROUP + GROUP)
                for s in range(GROUP):
                    pe.wait_ge(v_landed[k * GROUP + s], (g // 2) * 16 + 16 if isinstance(g, int) else (g - k) * 8 + 16)
                for c in range(DC):
                    if not (isinstance(g, int) and g == 0 and c < 4):
                        pe.wait_ge(products_added, g * DC + (c - 3))
                    for s in range(GROUP):
                        last = nc.tensor.matmul(bank(4 + c % 4, 0, T), vslots[:, k * GROUP + s, c * P:(c + 1) * P], gact[k][:, s, :],
                                                start=(s == 0), stop=(s == GROUP - 1))
                    last.then_inc(products_made, 1)
            pairs(pe, group)

        def experts_act(act):
            def group(g, k):
                for s in range(GROUP):
                    act.wait_ge(hidden_made, g * GROUP + (s + 1))
                    if not (isinstance(g, int) and g == 0):
                        act.wait_ge(hidden_weighted, g * GROUP + (s - GROUP + 1))
                    nc.scalar.activation(gel[:, s, :], bank(s, 0, T), ACT.Gelu).then_inc(hidden_taken, 1)
            pairs(act, group)

        def weigh(dve, g, k):
            dve.wait_ge(wexp_landed[k], (g // 2) * 16 + 16 if isinstance(g, int) else (g - k) * 8 + 16)
            for s in range(GROUP):
                dve.wait_ge(hidden_taken, g * GROUP + (s + 1))
                if not (isinstance(g, int) and g < 2):
                    dve.wait_ge(products_made, g * DC - DC)
                nc.vector.tensor_tensor(gact[k][:, s, :].rearrange("p (q t) -> p q t", t=64), gel[:, s, :].rearrange("p (q t) -> p q t", t=64),
                                        wexp[k][:, :, s, :], ALU.mult).then_inc(hidden_weighted, 1)

        def experts_dve(dve):
            dve.wait_ge(weights_kept, NR)
            for s_ in range(2):
                dve.wait_ge(w_stored[s_], 32)
            zeroed_ins = nc.vector.memset(yacc, 0.0)
            zeroed_ins.then_inc(zeroed, 1)
            dve.wait_ge(zeroed, 1)
            weigh(dve, 0, 0)

            def group(g, k):
                if not (isinstance(g, int) and g == NG - 1):
                    weigh(dve, g + 1, 1 - k)
                for c in range(DC):
                    dve.wait_ge(products_made, g * DC + (c + 1))
                    if not (isinstance(g, int) and g == 0):
                        dve.wait_ge(products_added, g * DC + (c - DC + 1))
                    nc.vector.tensor_tensor(yacc[:, c, :], yacc[:, c, :], bank(4 + c % 4, 0, T), ALU.add).then_inc(products_added, 1)
            pairs(dve, group)

        def last_dve(dve):
            dve.wait_ge(products_added, NG * DC)
            do = Do(dve, st_res, "dve")
            for c in range(DC):
                do(f"r{c}", nc.vector.scalar_tensor_tensor(out=xc[:, c, :], in0=yacc[:, c, :], scalar=modv[:, 5 * DC + c, 0:1], in1=xc[:, c, :], op0=ALU.mult, op1=ALU.add))
            do.end()
            norm_dve(dve, st_nf, 0, lambda c: xc[:, c, :], lambda c: xc[:, c, :], froot, lambda c: par("final_norm", c), DC)

        def last_act(act):
            barrier(act, "residual")
            norm_act(act, st_nf, 0, xc, fsq, froot, bank(0, 0, T), T, 1.0 / D)

        def last_pe(pe):
            norm_pe(pe, st_nf, 0, fsq, bank(0, 0, T), DC)

        def experts_sp(sp):
            barrier(sp, "out2")
            sp.dma_start(cut(PC_AT, N_PEER_CONSTS), a["peer_consts"]).then_inc(peer_loaded, 16)
            for q in range(4):
                sp.wait_ge(weights_kept, 16 * q + 16)
                sp.dma_start(a["experts"][q].rearrange("j i t -> j (i t)"), ewf[q % 2]).then_inc(w_stored[q % 2], 16)
            for k in range(2):
                sp.wait_ge(w_stored[k], 32)

            def group(g, k):
                if not (isinstance(g, int) and g < 2):
                    sp.wait_ge(hidden_weighted, g * GROUP - GROUP)
                sp.dma_start(wexp[k].rearrange("p q i t -> p q (i t)"),
                             a["experts"].rearrange("q j i t -> j q (i t)")[:, :, bass.ds(g * (GROUP * 64), GROUP * 64)]).then_inc(wexp_landed[k], 16)
                for s in range(GROUP):
                    if not (isinstance(g, int) and g == 0):
                        sp.wait_ge(hidden_made, g * GROUP + (s - GROUP + 1))
                    sp.dma_start(ring[:, s, 0:D], a["u"][g * GROUP + s]).then_inc(u_landed[s], 16)
                if not (isinstance(g, int) and g < 2):
                    sp.wait_ge(products_made, g * DC - DC)
                for s in range(GROUP):
                    sp.dma_start(vslots[:, k * GROUP + s, :], a["v"][g * GROUP + s]).then_inc(v_landed[k * GROUP + s], 16)
            pairs(sp, group)

        def store_sp(sp):
            barrier(sp, "norm_f")
            sp.dma_start(a["out"], x[:, :]).then_inc(stored, 16)
            sp.wait_ge(stored, 16)

        @block.sync
        def _(sp):
            for dst, src in ((params[:, :], a["params"]), (consts[:, :], a["consts"]), (misc[:, :], a["misc"]),
                             (x[:, :], a["x"]), (pT, a["p"].rearrange("p (k t) -> p k t", t=T))):
                sp.dma_start(dst, src).then_inc(inputs_loaded, 16)
            for name, count, cols in STREAMS:
                s = streams[name]
                if name == "y":
                    barrier(sp, "x2")
                    sp.dma_start(hcat[:, 1, :, :], a["ctx"].rearrange("p (c t) -> p c t", t=T)).then_inc(ctx_loaded, 16)
                if name == "merge2":
                    barrier(sp, "y")
                    sp.dma_start(dnc, a["dn_consts"]).then_inc(dnc_loaded, 16)

                def load(idx, slot, loads, i, u, name=name, s=s, cols=cols):
                    if not (isinstance(idx, int) and s.first + idx < SLOTS):
                        sp.wait_ge(weights_used, idx + (s.first - SLOTS + 1))
                    sp.dma_start(ring[:, slot, 0:cols], a["w_" + name][idx]).then_inc(landed[slot], 16)
                s.each(sp, load)
            experts_sp(sp)
            store_sp(sp)

        @block.tensor
        def _(pe):
            pre_pe(pe)
            n1_pe(pe)
            lru_pe(pe)
            qk_pe(pe)
            turn_pe(pe)
            cmp_pe(pe)
            nsa_pe(pe)
            fox_pe(pe)
            merge_pe(pe)
            out_pe(pe)
            n2_pe(pe)
            mla_pe(pe)
            conv_pe(pe)
            decay_pe(pe)
            dn_pe(pe)
            dno_pe(pe)
            merge2_pe(pe)
            choose_pe(pe)
            expw_pe(pe)
            experts_pe(pe)
            last_pe(pe)

        @block.scalar
        def _(act):
            pre_act(act)
            n1_act(act)
            lru_act(act)
            gates_act(act)
            qk_act(act)
            turn_act(act)
            cmp_act(act)
            nsa_act(act)
            fox_act(act)
            merge_act(act)
            out_act(act)
            n2_act(act)
            mla_act(act)
            conv_act(act)
            decay_act(act)
            dn_act(act)
            dno_act(act)
            merge2_act(act)
            choose_act(act)
            expw_act(act)
            experts_act(act)
            last_act(act)

        @block.vector
        def _(dve):
            pre_dve(dve)
            n1_dve(dve)
            lru_dve(dve)
            gates_dve(dve)
            qk_dve(dve)
            turn_dve(dve)
            cmp_dve(dve)
            nsa_dve(dve)
            fox_dve(dve)
            merge_dve(dve)
            out_dve(dve)
            n2_dve(dve)
            mla_dve(dve)
            conv_dve(dve)
            decay_dve(dve)
            dn_dve(dve)
            dno_dve(dve)
            merge2_dve(dve)
            choose_dve(dve)
            expw_dve(dve)
            experts_dve(dve)
            last_dve(dve)


def blocks(w):
    k, n = w.shape
    return w.reshape(k // P, P, n // P, P).transpose(2, 1, 0, 3).reshape(n // P, P, k)


def columns(v):
    return v.reshape(-1, P).T


def tokens_last(v):
    t, n = v.shape
    return v.T.reshape(n // P, P, t).transpose(1, 0, 2).reshape(P, -1)


def pad_to(v, n):
    out = np.zeros(v.shape[:-1] + (n,), np.float32)
    out[..., :v.shape[-1]] = v
    return out


def constants():
    i = np.arange(P)
    eye = np.eye(P)
    masked = BIG * (i[None, :] > i[:, None])
    t = np.arange(T)
    end = np.arange(NCMP) * 16 + 31
    cmp_mask = np.zeros((P, NT, 16))
    for tile in range(NT):
        cmp_mask[:, tile, :NCMP] = BIG * (end[None, :] > (i + tile * P)[:, None])
    freq = (10000.0 ** (-np.arange(0, 32, 2, dtype=np.float32) / np.float32(32))).astype(np.float32)
    rows, cols = (t // 64).astype(np.float32), (t % 64).astype(np.float32)
    ang = np.zeros((64, T), np.float32)
    for f in range(64):
        ang[f] = (rows if f < 32 else cols) * freq[f % 16]
    ang = np.concatenate([ang, ang])
    rot = np.zeros((P, P))
    for f in range(P):
        if f % 32 < 16:
            rot[f + 16, f] = -1
        else:
            rot[f - 16, f] = 1
    dup = np.zeros((P, P))
    dup[:64, :64] = dup[:64, 64:] = np.eye(64)
    duprot = np.zeros((P, P))
    duprot[:64, :64] = duprot[:64, 64:] = rot[:64, :64]
    c = np.concatenate([eye, np.ones((P, P)), masked, np.zeros((P, P)), masked, cmp_mask.reshape(P, -1),
                        i[:, None] <= i[None, :], np.cos(ang), np.sin(ang), rot, dup, duprot], 1)
    same = (i[:, None] // 64) == (i[None, :] // 64)
    r, s = i[:, None], i[None, :]
    level = [((r // (2 * b)) == (s // (2 * b))) & ((r // b) % 2 == 1) & ((s // b) % 2 == 0) for b in (1, 2, 4, 8, 16, 32)]
    dn = np.concatenate([same & (r <= s), same & (r >= s), same & (r < s), same & (r > s), same,
                         np.broadcast_to(r < 64, (P, P)), np.broadcast_to(r >= 64, (P, P))] + level + [m.T for m in level], 1)
    peer = np.concatenate([np.broadcast_to(s, (P, P)), (r // 16) == (s // 16)], 1)
    out = [v.astype(np.float32) for v in (c, dn, peer)]
    assert [v.shape[1] for v in out] == [N_CONSTS, N_DN_CONSTS, N_PEER_CONSTS]
    return out


def lay_out(v):
    v = {k: np.asarray(x) for k, x in v.items()}
    out = {}
    w, b = v["w_in"][0], v["b_in"][0]
    order = ("lru_x lru_gate nsa_q k_cmp v_cmp k_slc v_slc k_win v_win bgate nsa_gate fox_q fox_k fox_v fox_f fox_gate merge").split()
    size = (1024, 1024, 1024, 256, 256, 256, 256, 256, 256, 24, 1024, 1024, 1024, 1024, 8, 1024, 6144)
    at = dict(zip(order, np.concatenate([[0], np.cumsum(size)[:-1]]).tolist()))
    size = dict(zip(order, size))

    def col(m, name):
        return m[..., at[name]:at[name] + size[name]]
    z_order = "lru_x nsa_q k_slc k_win fox_q fox_k v_slc v_win fox_v k_cmp v_cmp".split()

    def z_columns(m):
        by_head = col(m, "bgate").reshape(m.shape[:-1] + (8, 3))[..., [1, 2, 0]].reshape(m.shape[:-1] + (24,))
        gates = pad_to(np.concatenate([by_head, col(m, "fox_f")], -1), P)
        return np.concatenate([col(m, n) for n in z_order] + [gates] + [col(m, n) for n in ("lru_gate", "nsa_gate", "fox_gate")], -1)
    w_mod = blocks(v["w_mod_2"][0])
    out["w_z"] = np.stack([blocks(z_columns(w)), w_mod[:N_Z]], 1).reshape(2 * N_Z, P, D)
    bz = z_columns(b)
    mg = blocks(col(w, "merge")).reshape(3, DC, P, D)
    wb = np.stack([blocks(v["w_branch"][0, j]) for j in range(3)])
    out["w_merge"] = np.concatenate([mg, wb], -1).transpose(1, 0, 2, 3).reshape(48, P, 3072)
    b_merge = col(b, "merge").reshape(3, DC, P).transpose(2, 1, 0).reshape(P, 48)
    pair = np.zeros((2, 8, P, P), np.float32)
    for j, name in enumerate(("lru_wa", "lru_wx")):
        m = v[name][0].reshape(8, 2, 64, 64)
        pair[j, :, :64, :64], pair[j, :, 64:, 64:] = m[:, 0], m[:, 1]
    out["w_lru"] = pair.transpose(1, 2, 0, 3).reshape(8, P, 256)
    out["w_cmp"] = v["cmp_w1"][0].reshape(2, 4, 8, P, 256).transpose(0, 1, 3, 2, 4).reshape(8, P, 2048)
    out["w_out"] = blocks(v["w_out"][0])
    out["w_ple"] = v["w_ple"][0].reshape(2, P, 2, 1024).transpose(2, 1, 0, 3).reshape(2, P, 2048)
    out["w_ple_gate"] = blocks(v["w_ple_gate"][0])
    out["misc"] = np.concatenate([v["cmp_w2"][0].reshape(4, P, P).transpose(1, 0, 2).reshape(P, 512),
                                  v["peer_sub_keys_2"][0].transpose(2, 0, 1).reshape(P, 256)], 1)
    out["x"], out["ctx"], out["p"] = tokens_last(v["x"][0]), tokens_last(v["ctx_2"][0]), tokens_last(v["p"][0, 0])

    w = v["w_in_2"][0]
    sizes = (512, 256, 64, 3072, 1024, 8, 8, 8, 8, 2048, 2048)
    cq, ckv, kr, qkv, zz, af, ab, bf, bb, ga, gate_b = np.split(w, np.cumsum(sizes)[:-1], axis=1)
    small = np.zeros((D, P), np.float32)
    small[:, 64:72], small[:, 72:80], small[:, 96:104], small[:, 104:112] = af, ab, bf, bb
    w_y = blocks(np.concatenate([ckv, qkv[:, 1024:], pad_to(kr, P), small], 1))
    n = N_MOD - N_Z
    out["w_y"] = np.concatenate([np.stack([w_y[:n], w_mod[N_Z:]], 1).reshape(2 * n, P, D), w_y[n:]])
    out["w_l"] = blocks(np.concatenate([cq, qkv[:, :1024], zz], 1))
    uq = v["w_uq_2"][0].reshape(4, P, 8, 192).transpose(2, 1, 0, 3).reshape(8, P, 768)
    ukv = v["w_ukv_2"][0].reshape(2, P, 8, 256).transpose(2, 1, 0, 3).reshape(8, P, 512)
    out["w_mla"] = np.concatenate([uq, ukv], -1)
    g2 = np.stack([blocks(ga), blocks(gate_b)])
    b2 = np.stack([blocks(v["w_branch_a_2"][0]), blocks(v["w_branch_b_2"][0])])
    out["w_merge2"] = np.concatenate([g2, b2], -1).transpose(1, 0, 2, 3).reshape(32, P, 3072)
    out["w_out2"] = blocks(v["w_out_2"][0])
    out["w_peer_q"] = blocks(v["peer_w_q_2"][0])
    out["u"] = blocks(v["peer_u_2"][0].T)
    out["v"] = v["peer_v_2"][0].reshape(KEYS, P, D)

    ab_rows = np.zeros((2, P, 1), np.float32)
    ab_rows[0, 64:80, 0] = v["dn_a_log_2"][0].reshape(16)
    ab_rows[1, 64:80, 0] = v["dn_dt_bias_2"][0].reshape(16)
    cond = np.stack([columns(v["c_2"][0]), columns(v["c_ctx_2"])], -1).reshape(P, 32)
    conv = v["conv_w"][0].reshape(4, 8, P).transpose(2, 0, 1).reshape(P, 32)
    conv2 = v["dn_conv_w_2"][0].reshape(5, 24, P).transpose(2, 0, 1).reshape(P, 120)
    gains = np.concatenate([np.repeat(v[n][0][:, None], c, 1) for n, c in
                            (("nsa_q_gain", 8), ("nsa_k_gain", 4), ("fox_q_gain", 8), ("fox_k_gain", 8))], 1)
    p = {"b_merge": b_merge, "lru_ba": columns(v["lru_ba"][0]), "lru_bx": columns(v["lru_bx"][0]),
         "eps": np.full((P, 1), EPS, np.float32), "ln_gain": columns(v["ln_gain"][0]), "b_in": columns(bz),
         "conv_w": conv, "conv_b": columns(v["conv_b"][0]), "lam": columns(v["lru_lambda"][0]),
         "pos": v["cmp_pos"][0].transpose(2, 0, 1).reshape(P, 64), "qk_gain": gains,
         "cmp_gain": v["nsa_k_gain"][0][:, None], "ple_gain": columns(v["ple_gain"][0]), "b_mod": columns(v["b_mod_2"][0]),
         "norm1": columns(v["norm1_w_2"][0]), "q_norm": columns(v["mla_q_norm_w_2"][0]),
         "kv_norm": columns(v["mla_kv_norm_w_2"][0]), "conv2_w": conv2, "a_log": ab_rows[0], "dt_bias": ab_rows[1],
         "dn_norm": v["dn_norm_w_2"][0][:, None], "norm2": columns(v["norm2_w_2"][0]),
         "final_norm": columns(v["final_norm_w_2"]), "cond": cond}
    out["params"] = np.concatenate([p[n] for n in PARAMS], 1)
    out["consts"], out["dn_consts"], out["peer_consts"] = constants()
    return {k: np.ascontiguousarray(x) for k, x in out.items()}


def kernel(**inputs):
    import concourse.bacc as bacc
    from concourse.bass_utils import run_bass_kernel_spmd

    nc = bacc.Bacc("TRN2", target_bir_lowering=False, num_devices=1)
    arrays = lay_out(inputs)
    args = {k: nc.dram_tensor(f"{k}_dram", x.shape, F32, kind="ExternalInput").ap() for k, x in arrays.items()}
    args["out"] = nc.dram_tensor("out_dram", (P, DC * T), F32, kind="ExternalOutput").ap()
    args["experts"] = nc.dram_tensor("experts_dram", (4, P, KEYS, 64), F32, kind="Internal").ap()
    build(nc, args)
    r = run_bass_kernel_spmd(nc, [{f"{k}_dram": x for k, x in arrays.items()}], core_ids=[0])
    out = r.results[0]["out_dram"]
    return out.reshape(P, DC, T).transpose(2, 1, 0).reshape(1, T, D)
```

```python
from contextlib import ExitStack

import numpy as np

import concourse.bass as bass
from concourse import mybir

F32 = mybir.dt.float32
F32R = mybir.dt.float32r
U32 = mybir.dt.uint32
ACT = mybir.ActivationFunctionType
ALU = mybir.AluOpType
AX_X = mybir.AxisListType.X

P = 128
T = 256
NT = T // P
D = 2048
DC = D // P
BW = 1024
BC = BW // P
EPS = 1e-6
BIG = 1e30
GUARD = 1e20
SCALE = P ** -0.5
MLA_SCALE = 192 ** -0.5
NCMP = 15
KEYS = 128
TOPK = 16
SLOTS = 4
SLOTW = 3072
GROUP = 4
SOFTPLUS_TERMS = 8
ROUNDED = 16384

(Z_LRU, Z_NQ, Z_KS, Z_KW, Z_FQ, Z_FK, Z_VS, Z_VW, Z_FV, Z_KC, Z_VC, Z_GB, Z_LG, Z_NG, Z_FG, N_Z) = (
    0, 8, 16, 18, 20, 28, 36, 38, 40, 48, 50, 52, 53, 61, 69, 77)
N_QK = Z_VS - Z_NQ

(Y_KV, Y_K, Y_V, Y_KR, Y_AB, N_Y) = (0, 2, 10, 18, 19, 20)
(L_CQ, L_Q, L_Z, N_L) = (0, 4, 12, 20)


def layout(*sizes):
    at, out = 0, {}
    for name, n in sizes:
        out[name] = (at, n)
        at += n
    return out, at


PARAMS, N_PARAMS = layout(
    ("b_merge", 48), ("lru_ba", 8), ("lru_bx", 8), ("eps", 1), ("ln_gain", 16), ("b_in", N_Z), ("conv_w", 32),
    ("conv_b", 8), ("lam", 8), ("pos", 64), ("qk_gain", N_QK), ("cmp_gain", 1), ("ple_gain", 16), ("b_mod", 96),
    ("norm1", 16), ("q_norm", 4), ("kv_norm", 2), ("conv2_w", 120), ("a_log", 1), ("dt_bias", 1), ("dn_norm", 1),
    ("norm2", 16), ("final_norm", 16))
CONSTS, N_CONSTS = layout(
    ("ident", 128), ("ones", 128), ("causal", 384), ("cmp_mask", 32), ("upto", 128), ("cos", 256), ("sin", 256),
    ("rot", 128), ("dup", 128), ("duprot", 128))
DN_CONSTS, N_DN_CONSTS = layout(
    ("le", 128), ("ge", 128), ("lt", 128), ("gt", 128), ("chunk", 128), ("half0", 128), ("half1", 128),
    ("level", 6 * 128), ("level_t", 6 * 128))
PEER_CONSTS, N_PEER_CONSTS = layout(("iota", 128), ("same_head", 128))
MISC, N_MISC = layout(("cmp_w2", 512), ("sub_keys", 256))

N_MOD = 96
STREAMS = (("z", N_Z, 2048), ("lru", 8, 256), ("cmp", 8, 2048), ("merge", 48, 3072),
           ("out", 16, 2048), ("ple", 2, 2048), ("ple_gate", 16, 2048), ("y", N_Y, 2048), ("l", N_L, 2048),
           ("mla", 8, 1280), ("merge2", 32, 3072), ("out2", 16, 2048), ("peer_q", 16, 2048))


class Steps:

    def __init__(self, sem, names):
        self.sem, self.names = sem, names
        assert len(set(names)) == len(names), names

    def at(self, name, it=0):
        return it * len(self.names) + (self.names.index(name) + 1)


class Stage:

    def __init__(self, new_sem, name, rounds, **names):
        self.rounds = rounds
        self.steps = {e: Steps(new_sem(f"{name}_{e}_steps"), n.split()) for e, n in names.items() if n}

    def finished(self, eng):
        for s in self.steps.values():
            eng.wait_ge(s.sem, self.rounds * len(s.names))


class Do:

    def __init__(self, eng, stage, who, it=0):
        self.eng, self.stage, self.mine, self.it, self.n = eng, stage, stage.steps[who], it, 0

    def __call__(self, name, instruction):
        assert self.mine.names[self.n] == name, (self.mine.names[self.n], name)
        self.n += 1
        instruction.then_inc(self.mine.sem, 1)

    def wait(self, who, name, it=None):
        s = self.stage.steps[who]
        self.eng.wait_ge(s.sem, s.at(name, self.it if it is None else it))

    def own(self):
        self.eng.wait_ge(self.mine.sem, self.it * len(self.mine.names) + self.n)

    def end(self):
        assert self.n == len(self.mine.names), self.mine.names[self.n:]


def rounds(eng, count, body):
    body(0)
    if count == 2:
        body(1)
    elif count > 2:
        with eng.Fori(1, count) as i:
            body(i)


class Stream:

    def __init__(self, first, count, cols):
        self.first, self.count, self.cols = first, count, cols

    def each(self, eng, body, step=SLOTS):
        per = step // SLOTS

        def blocks(i, us):
            for u in us:
                b = self.first + u
                body(i * step + u, b % SLOTS, i * per + (b // SLOTS + 1), i, u)

        whole = self.count // step
        if whole:
            blocks(0, range(step))
        if whole == 2:
            blocks(1, range(step))
        elif whole > 2:
            with eng.Fori(1, whole) as i:
                blocks(i, range(step))
        blocks(whole, range(self.count - whole * step))


def build(nc: bass.Bass, a: dict):
    with ExitStack() as ctx:
        def new_sem(name):
            return ctx.enter_context(nc.semaphore(name))

        def sb(name, cols):
            return ctx.enter_context(nc.sbuf_tensor(name, [P, cols], F32))

        ps = ctx.enter_context(nc.psum_tensor("ps", [P, 8, 512], F32))
        ring = ctx.enter_context(nc.sbuf_tensor("ring", [P, SLOTS, SLOTW], F32))
        params = sb("params", N_PARAMS)
        halves = sb("halves", 64)
        pT = sb("p", 2 * T)[:, :].rearrange("p (k t) -> p k t", t=T)
        consts = sb("consts", N_CONSTS)
        misc = sb("misc", N_MISC)
        x = sb("x", D * T // P)
        mod = sb("mod", 192)
        gains = sb("gains", 49)
        AREA = 32600
        FRONT = AREA - ROUNDED
        with nc.sbuf_tensor("area", [P, AREA], F32) as area:
            pass
        sb("front", FRONT)

        def sb_rounded(name, cols):
            return ctx.enter_context(nc.sbuf_tensor(name, [P, cols], F32R))


        def par(name, c=0, n=1):
            o, k = PARAMS[name]
            return params[:, bass.ds(c + o, n)]

        def half(name, c=0):
            o, k = PARAMS[name]
            return halves[:, bass.ds(c + o, 1)]

        def con(name):
            o, k = CONSTS[name]
            return consts[:, o:o + k]

        def cut(at, *shape):
            n = 1
            for s in shape:
                n *= s
            v = area[:, at:at + n]
            assert at + n <= AREA, (at, n)
            if len(shape) == 2:
                return v.rearrange("p (a b) -> p a b", b=shape[1])
            if len(shape) == 3:
                return v.rearrange("p (a b c) -> p a b c", b=shape[1], c=shape[2])
            return v

        ident, ones, causal, upto_mask = con("ident"), con("ones"), con("causal"), con("upto")
        xc = x[:, :].rearrange("p (c t) -> p c t", t=T)
        modv = mod[:, :].rearrange("p (c s) -> p c s", s=2)

        def bank(b, lo=0, n=512):
            return ps[:, b, lo:lo + n]

        streams, first = {}, 0
        for name, count, cols in STREAMS:
            streams[name] = Stream(first, count, cols)
            first += count
        landed = [new_sem(f"weights_landed_{s}") for s in range(SLOTS)]
        weights_used = new_sem("weights_used")
        evacuated = {name: new_sem(f"evacuated_{name}") for name, _, _ in STREAMS}
        inputs_loaded = new_sem("inputs_loaded")
        N_INPUTS = 5

        def gemm_block(pe, name, idx, slot, loads, ktiles, rhs, n, out=None):
            pe.wait_ge(landed[slot], loads * 16)
            if not (isinstance(idx, int) and idx < SLOTS):
                pe.wait_ge(evacuated[name], idx - (SLOTS - 1))
            for k in range(ktiles):
                last = nc.tensor.matmul(bank(slot, 0, n) if out is None else out, ring[:, slot, k * P:(k + 1) * P],
                                        rhs(k), start=(k == 0), stop=(k == ktiles - 1))
            return last

        S = {}

        def stage(name, rounds, **names):
            S[name] = Stage(new_sem, name, rounds, **names)
            return S[name]

        def norm_stage(name, rounds, chunks, extra_act=""):
            return stage(name, rounds, act="squares root", pe="sums", dve="inverse " + " ".join(
                f"scaled{c}" for c in range(chunks)))

        def norm_act(act, st, it, src, squares, root, sums, width, scale=1.0):
            do = Do(act, st, "act", it)
            do("squares", nc.scalar.activation(squares, src, ACT.Square))
            do.wait("pe", "sums")
            do("root", nc.scalar.activation(root, sums, ACT.Sqrt, bias=par("eps"), scale=scale))
            do.end()

        def norm_pe(pe, st, it, squares, sums, chunks):
            do = Do(pe, st, "pe", it)
            do.wait("act", "squares")
            for c in range(chunks):
                last = nc.tensor.matmul(sums, ones, squares[:, c, :], start=(c == 0), stop=(c == chunks - 1))
            do("sums", last)
            do.end()

        def norm_dve(dve, st, it, src, dst, root, gain, chunks):
            do = Do(dve, st, "dve", it)
            do.wait("act", "root")
            do("inverse", nc.vector.reciprocal(root, root))
            do.own()
            for c in range(chunks):
                do(f"scaled{c}", nc.vector.scalar_tensor_tensor(
                    out=dst(c), in0=src(c), scalar=gain(c), in1=root, op0=ALU.mult, op1=ALU.mult))
            do.end()

        SP_DVE = "sp_negated sp_plus2 sp_recip sp_s sp_s2 sp_q0 " + " ".join(
            f"sp_q{k}" for k in range(1, SOFTPLUS_TERMS - 1)) + " sp_last sp_top sp_out"
        SP_ACT = "sp_exp"

        def softplus_dve(do, v, t1, t2, t3, out):
            do("sp_negated", nc.vector.scalar_tensor_tensor(out=t1, in0=v, scalar=-1.0, in1=v, op0=ALU.mult, op1=ALU.min))
            do.wait("act", "sp_exp")
            do("sp_plus2", nc.vector.tensor_scalar(t2, t1, 2.0, None, ALU.add))
            do.own()
            do("sp_recip", nc.vector.reciprocal(t2, t2))
            do.own()
            do("sp_s", nc.vector.tensor_tensor(t1, t1, t2, ALU.mult))
            do.own()
            do("sp_s2", nc.vector.tensor_tensor(t2, t1, t1, ALU.mult))
            do.own()
            do("sp_q0", nc.vector.tensor_scalar(t3, t2, 1.0 / (2 * SOFTPLUS_TERMS - 1), None, ALU.mult))
            for k in range(1, SOFTPLUS_TERMS - 1):
                do.own()
                do(f"sp_q{k}", nc.vector.scalar_tensor_tensor(
                    out=t3, in0=t3, scalar=1.0 / (2 * (SOFTPLUS_TERMS - k) - 1), in1=t2, op0=ALU.add, op1=ALU.mult))
            do.own()
            do("sp_last", nc.vector.scalar_tensor_tensor(out=t3, in0=t3, scalar=1.0, in1=t1, op0=ALU.add, op1=ALU.mult))
            do("sp_top", nc.vector.tensor_scalar(out, v, 0.0, None, ALU.max))
            do.own()
            do("sp_out", nc.vector.scalar_tensor_tensor(out=out, in0=t3, scalar=2.0, in1=out, op0=ALU.mult, op1=ALU.add))

        def softplus_act(do, t1):
            do.wait("dve", "sp_negated")
            do("sp_exp", nc.scalar.activation(t1, t1, ACT.Exp))

        HN, ZAT = 0, 4096
        TMP = ZAT + N_Z * T
        hn = cut(HN, DC, T)
        z = cut(ZAT, N_Z, T)

        st_pre = stage("pre", 1, dve="halved cond_silu", act="cond_tanh")
        silu1, junk1 = cut(TMP, 2, D), cut(TMP + 4096, 2, D)
        mod_slots = [ring[:, 2 * k:2 * k + 2, D:] for k in range(2)]
        mod_landed = [new_sem(f"mod_landed_{k}") for k in range(2)]
        mod_used, cond_loaded = new_sem("mod_used"), new_sem("cond_loaded")

        st_n1 = norm_stage("norm_x", 1, DC)
        sq = cut(TMP + 4096, DC, T)
        root = cut(TMP + 4096 + DC * T, T)

        A_AT, M_AT = TMP, TMP + 2048
        lru_a = cut(A_AT, BC, T)
        lru_m = cut(M_AT, BC, T)
        LT = M_AT + 2048
        uc, la, th, den, tx = (cut(LT + k * T, T) for k in range(5))
        lt1, lt2, lt3, lt4, nsp = (cut(LT + 5 * T + 8 * k, 8) for k in range(5))
        st_lam = stage("lam", 1, dve="neg " + SP_DVE + " scaled", act=SP_ACT)
        st_lru = stage("lru", BC, dve="lag0 lag1 lag2 lag3 log_a den inv m gated", act="tanh_a tanh_x a th")
        st_lru2 = stage("lru2", 1, act="root tanh_gate", dve="drive " + " ".join(f"scan{c}" for c in range(BC)) + " silu out")

        st_qk = stage("qk", N_QK // 4, act="squares root", pe="sums0 sums1", dve="inverse " + " ".join(f"scaled{c}" for c in range(4)))
        qk_sq = cut(TMP, 1024)
        qk_root = cut(TMP + 1024, 1024)

        VT_N = 12
        vt = cut(TMP, VT_N * NT, P)
        VT_END = TMP + VT_N * NT * P
        gb = cut(VT_END, NT, P)
        logf = cut(VT_END + 256, NT, BC)
        ft = [cut(VT_END + 256 + 16 * k, NT, BC) for k in range(1, 5)]
        cum = cut(VT_END + 256 + 16 * 5, NT, BC)
        G_END = VT_END + 256 + 96
        st_tr = stage("turn", 1, pe=" ".join(f"turned{k}" for k in range(7)) + " cum0 cum1", act=" ".join(f"kept{k}" for k in range(7))
                      + " gate_tanh " + SP_ACT, dve="gate neg " + SP_DVE + " logf cumkept")

        blk = cut(G_END, 2, 32 * 30)
        C_AT = G_END + 1920
        cth = cut(C_AT, 2, 30)
        chid = cut(C_AT + 60, 2 * 2, 30)
        kc = cut(C_AT + 180, 30)
        kcs = cut(C_AT + 210, 30)
        kcr = cut(C_AT + 240, 30)
        vc = cut(C_AT + 270, 2, P)
        C_END = C_AT + 270 + 256
        st_cmp = stage("cmp", 2, dve="b0 b1 silu halved", act="tanh")
        st_cmp2 = stage("cmp2", 1, pe="kc vc0 vc1 sums", act="copied squares root vck0 vck1", dve="inv out")

        N_AT = C_END
        nq = cut(N_AT, T)
        nst = cut(N_AT + 256, 2, 384)
        nex = cut(N_AT + 1024, 2, 384)
        ncs = cut(N_AT + 1792, 2, 16)
        nce = cut(N_AT + 1824, 2, 16)
        nmx = cut(N_AT + 1856, 2, 3)
        nsm = cut(N_AT + 1862, 2, 3)
        net = nst
        nct = cut(N_AT + 1868, 2, P)
        BR = [(b, t) for t in range(NT) for b in range(3)]
        st_nsa = stage(
            "nsa", BC,
            act="q " + " ".join(f"e{b}{t}" for b, t in BR) + " et0 et1 ctk",
            pe="s turned o",
            dve="ss sw sc max0 max1 maxc guard floor inv gates " + " ".join(f"w{b}{t}" for b, t in BR) + " y")

        fq = cut(N_AT, T)
        fv = cut(N_AT + 256, NT, P)
        fr = cut(N_AT + 512, NT, P)
        fb = cut(N_AT + 768, 384)
        fs = cut(N_AT + 1152, 384)
        fe = cut(N_AT + 1536, 384)
        fet = cut(N_AT + 1920, 384)
        fmx = cut(N_AT + 2304, 2)
        fsm = cut(N_AT + 2306, 2)
        st_fox = stage("fox", BC, act="q v e0 e1 etk", pe="s c turned o",
                       dve="r0 r1 b0 b1 s max0 max1 inv w0 w1 y")
        st_gate = stage("gates1", 2, act="tanh", dve="silu halved")

        merged = cut(TMP, DC, T)
        mth = cut(TMP + 4096, 2, T)
        mtm = cut(TMP + 4096 + 2 * T, 2, T)
        st_merge = stage("merge", 48, act="gate y", dve="scaled summed")
        e_at = ZAT + 512
        e = cut(e_at, DC, T)
        e_sq = cut(e_at + 4096, DC, T)
        e_root = cut(e_at + 8192, T)
        gth = cut(e_at + 8192 + T, SLOTS, T)
        x2 = cut(TMP, DC, T)
        st_e = norm_stage("norm_e", 1, DC)
        st_ple = stage("ple", 2, act="e0 e1", pe="p0")
        st_pg = stage("pg", 16, dve="mixed added")
        st_x2 = stage("x2", 1, dve="moved")

        zg_tanh = cut(LT + 5 * T + 64, BC, T)
        gates_tmp = cut(TMP, BC, T)
        zflat = cut(ZAT, N_Z * T)
        vtf = cut(TMP, VT_N * NT * P)
        blkf = cut(G_END, 2 * 960)
        cthf, chidf = cut(C_AT, 60), cut(C_AT + 60, 120)
        bank45 = ps[:, 4:6, :]
        tick = cut(TMP + 4096 + 6 * T, 1)

        CTX_AT, Y_AT, L_AT, MY_AT, T2 = 4096, 8192, 18432, 23552, 25600
        hcat = cut(0, 2, DC * T)[:, :, :].rearrange("p s (c t) -> p s c t", t=T)
        yv = cut(Y_AT, N_Y, 2 * T)
        lv = cut(L_AT, N_L, T)
        my = cut(MY_AT, BC, T)
        gain1v = gains[:, 0:32].rearrange("p (c s) -> p c s", s=2)
        gain2v = gains[:, 32:48]
        sq2 = cut(T2 + 1024, DC, T)
        root2 = cut(T2 + 5120, T)
        silu2, junk2 = cut(L_AT, 2, D), cut(L_AT + 4096, 2, D)
        st_gain = stage("gain", 1, dve=f"mod0_0 mod0_1 first cond_silu mod{N_Z}_0 mod{N_Z}_1 second", act="cond_tanh")
        st_n2 = [norm_stage(f"norm2_{s}", 1, DC) for s in range(2)]
        st_shift = stage("shift", 1, act=" ".join(f"shift{c}" for c in range(2 * DC)))
        ctx_loaded = new_sem("ctx_loaded")
        st_cq = norm_stage("norm_cq", 1, 4)
        st_ckv = norm_stage("norm_ckv", 1, 2)
        msq = cut(T2, 1024)
        mroot = cut(T2 + 1024, 512)
        krd = cut(T2 + 1536, 2 * T)
        krt = cut(T2 + 2048, T)
        st_kr = stage("kr", 1, pe="dup rot", act="ctx", dve="cos sin sum")
        mq = cut(T2 + 2304, T)
        mqr = cut(T2 + 2560, T)
        mqt = cut(T2 + 2816, T)
        mk = cut(T2 + 3072, 2 * T)
        mv = cut(T2 + 3584, 4, P)
        me = cut(T2 + 4096, 2, 2 * T)
        met = cut(T2 + 5120, 2, 2 * T)
        mmx = cut(T2 + 6144, 2)
        msm = cut(T2 + 6146, 2)
        st_mla = stage("mla", BC, act="qn qr kn v e0 e1 et0 et1", pe="rot s turned0 turned1 o",
                       dve="cos sin sum max neg inv w0 w1 y")
        ctmp, cth2 = cut(T2, 2, T), cut(T2 + 512, 2, T)
        st_ckvv = stage("conv_kv", 16, dve="mid lm2 lm1 lp1 lp2 out", act="tanh")
        st_cvq = stage("conv_q", 8, dve="mid lm2 lm1 lp1 lp2 out", act="tanh")
        st_lk, st_lq = (stage(n, 4, act="squares0 squares1 root0 root1", pe="sums0 sums1", dve="inv0 out0 inv1 out1") for n in ("l2_k", "l2_q"))
        l2_sq, l2_root = ([cut(T2 + 1024 * j + 512 * k, 2 * T) for k in range(2)] for j in range(2))
        dnc_loaded = new_sem("dn_consts_loaded")
        DNC_AT = CTX_AT
        R2 = DNC_AT + N_DN_CONSTS
        dnc = cut(DNC_AT, N_DN_CONSTS)

        def dcon(name, k=0):
            o, _ = DN_CONSTS[name]
            return dnc[:, o + k * P:o + (k + 1) * P]

        gsp, gt1, gt2, gt3, gv = (cut(T2 + 512 * k, 2 * T) for k in range(5))
        ea = cut(T2 + 2560, 1)
        S13 = T2 + 6656
        AB_AT = Y_AT + Y_AB * 512
        gT, bT, gcum, eg, egl = (cut(S13 + 64 * k, 64) for k in range(5))
        beg, egls, gl = cut(AB_AT, 64), cut(AB_AT + 64, 128), cut(AB_AT + 192, 64)
        st_dec = stage("decay", 1, dve="shifted " + SP_DVE + " scale half_b beta sub beg", act=SP_ACT + " ea tanh_b gk bk cumk glk egl_exp eg_exp chunk_exp",
                       pe="turned cums")
        NU = 8
        B = [T2 + 1024 * k for k in range(6)]
        rg = cut(B[0], NU, P)
        pbuf = rg
        dec = cut(B[1], NU, P)
        xb = dec
        ub = dec
        mb = cut(B[2], NU, P)
        kbe = mb
        mt = cut(B[3], NU, P)
        kdec = mt
        xt = cut(B[4], NU, P)
        atl = cut(B[5], NU, P)
        wt = atl
        state = cut(T2 + 6144, 2, P)
        vnew = cut(T2 + 6400, 2, P)
        vb = cut(R2, NU, P)
        att = cut(R2 + 1024, 4, P)
        kst = cut(R2 + 1536, 2 * T)
        vst = cut(R2 + 2048, 2 * T)
        assert R2 + 2560 <= Y_AT + 1024
        qst = cut(L_AT, T)
        ktm = cut(L_AT + 256, 4, P)
        ob0 = cut(L_AT + 768, NT, P)
        vtm = cut(Y_AT + Y_KR * 512, 4, P)
        ob1 = cut(AB_AT + 256, NT, P)
        LV = range(1, 6)
        INNER = range(1, 5)
        st_dn = stage(
            "dn", BC,
            act="k v q ktm vtm relu_t relu dec dec_t mt " + " ".join(f"p{l}0 p{l}1" for l in LV) + " u",
            pe="turned rows gram mt " + " ".join(f"p{l}0 p{l}1 " + " ".join((f"x{l}{d} " if l in INNER else "") + f"xt{l}{d}" for d in range(2)) for l in LV) + " u w "
               + " ".join(f"ws{s}0 ws{s}1 " + " ".join(f"su{s}{d}" + (f" oa{s}{d}" if s >= 4 else "") for d in range(2)) for s in range(8)) + " ot",
            dve="rg0 rg1 diff0 diff1 tmask0 tmask1 att0 att1 smask0 smask1 gb0 gb1 m l00 l01 x l0t0 l0t1 xt "
                + "a10 a11 vb0 vb1 ke0 ke1 s0 " + " ".join((f"a{l + 1}0 a{l + 1}1 " if l in INNER else "kd0 kd1 ")
                           + " ".join((f"x{l}{d} " if l in INNER else "") + f"xt{l}{d}" for d in range(2)) for l in LV) + " w "
                + " ".join(f"vn{s}0 vn{s}1 st{s}0 st{s}1" + (f" oi{s}0 oi{s}1 o{s}0 o{s}1" if s >= 4 else "") for s in range(8)) + " osum ot")
        st_on = stage("dn_out", 2, act="squares root", pe="sums0 sums1", dve="inv " + " ".join(f"scaled{c}" for c in range(4)))
        st_og = stage("dn_gate", 1, act="tanh", dve="silu out")
        osq, oroot = cut(T2, 1024), cut(T2 + 1024, 1024)
        og = cut(T2 + 2048, BC, T)
        merged2 = cut(T2, DC, T)
        m2th, m2tm = cut(T2 + 4096, 2, T), cut(T2 + 4608, 2, T)
        st_merge2 = stage("merge2", 32, act="gate y", dve="scaled summed")

        HP_AT, MTR_AT, W_AT, IDX_AT, PB_AT, PC_AT = 0, 4096, 8192, 24576, 25088, 32256
        hp = cut(HP_AT, DC, T)
        psq, proot = cut(W_AT, DC, T), cut(W_AT + 4096, T)
        pq = cut(MTR_AT, DC, T)
        scores = cut(W_AT, 2 * DC, P)
        topv = cut(W_AT + 4096, 2 * DC, TOPK)
        topi = cut(W_AT + 4608, 2 * DC, TOPK)
        LANES = 4
        TOP_AT, CAND_AT = W_AT + 5120, W_AT + 12800
        krest, krow = cut(TOP_AT, LANES, P), cut(TOP_AT + 512, LANES, P)
        kval, kidx = cut(TOP_AT + 1024, LANES, TOPK), cut(TOP_AT + 1088, LANES * TOPK).bitcast(U32).rearrange("p (l k) -> p l k", k=TOPK)
        gated = cut(TOP_AT + 1152, 1)
        c8, csum = cut(TOP_AT + 1160, LANES, 8), cut(TOP_AT + 1200, 2, LANES)
        cand, crest, cexp = (cut(CAND_AT + 1024 * k, LANES, 256) for k in range(3))

        def lanes(*names):
            return " ".join(f"{n}{l}" for n in names for l in range(LANES)) + " "

        mix = cut(W_AT + 8192, NT, TOPK, P)
        mix5 = mix.rearrange("p t a (h b) -> p t a h b", b=TOPK)
        idxp = cut(W_AT + 12288, 4, P)
        idxt = cut(IDX_AT, 2, T)
        mixt = cut(MTR_AT, TOPK, T)
        st_np = norm_stage("norm_p", 1, DC)
        st_sh2 = stage("shift2", 1, act=" ".join(f"shift{c}" for c in range(DC)))
        st_sc = stage("scores", 1, pe=" ".join(f"s{b}" for b in range(8)), act=" ".join(f"k{b}" for b in range(8)))
        st_top = stage("top", 2 * DC // LANES, dve=lanes("row") + "gate0 " + lanes("m0_") + "gate1 " + lanes("i0_", "rest") + "gate2 "
                       + lanes("m1_") + "gate3 " + lanes("i1_", "values") + lanes("indices"))
        st_cand = stage("cand", DC // LANES, dve=lanes("sum", "m0_", "r0_", "neg", "m1_", "r1_", "chosen", "masked", "total") + "inv " + lanes("out"),
                        act=lanes("exp"))
        st_mt = stage("mix", 1, dve="idx0 idx1", pe="idx " + " ".join(f"m{b}" for b in range(8)), act="idx " + " ".join(f"m{b}" for b in range(8)))
        NB4 = 4
        NR = T // NB4
        hots = [[cut(PB_AT + 512 * (3 * k + j), NB4, P) for j in range(3)] for k in range(4)]
        rbuf = [cut(PB_AT + 512 * (12 + k), NB4, P) for k in range(2)]
        iota, same_head = cut(PC_AT, P), cut(PC_AT + P, P)
        ew = [cut(W_AT + 8192 * k, P, 64) for k in range(2)]
        hot_made, spread_made, spread_kept, weights_made, weights_kept = (new_sem(n) for n in (
            "hot_made", "spread_made", "spread_kept", "weights_made", "weights_kept"))
        peer_loaded, w_stored = new_sem("peer_consts_loaded"), [new_sem(f"expert_weights_stored_{k}") for k in range(2)]
        NG = KEYS // GROUP
        PIECE, NPIECES = 512, 4
        PER_PHASE = GROUP * D // PIECE
        vslots = cut(0, GROUP, D)
        yacc = cut(8192, DC, T)
        wexp = [ring[:, k, D:].rearrange("p (q s t) -> p q s t", q=4, s=GROUP) for k in range(2)]
        gel = ring[:, 2, D:].rearrange("p (s t) -> p s t", t=T)
        hp_parts, gact_parts, pieces = sb_rounded("hp_parts", 2 * DC * T), sb_rounded("gact_parts", 2 * 2 * GROUP * T), sb_rounded("pieces", NPIECES * 2 * PIECE)
        hp2 = hp_parts[:, :].rearrange("p (a c t) -> p a c t", a=2, t=T)
        gact = gact_parts[:, :].rearrange("p (k a s t) -> p k a s t", k=2, a=2, t=T)
        piece = pieces[:, :].rearrange("p (b a n) -> p b a n", b=NPIECES, a=2)
        u_landed = [new_sem(f"u_landed_{k}") for k in range(GROUP)]
        v_landed = [new_sem(f"v_landed_{k}") for k in range(GROUP)]
        wexp_landed = [new_sem(f"expert_weights_landed_{k}") for k in range(2)]
        st_hps = stage("hp_split", 1, act="rounded", dve="rest")
        rounded, remainders, pieces_used, gelu_made, weighted, gact_rounded, gact_split, products_added = (new_sem(n) for n in (
            "pieces_rounded", "piece_remainders", "pieces_used", "gelu_made", "gelu_weighted", "gact_rounded", "gact_split", "products_added"))
        st_res = stage("residual", 1, dve=" ".join(f"r{c}" for c in range(DC)))
        st_nf = norm_stage("norm_f", 1, DC)
        fsq, froot = cut(0, DC, T), cut(4096, T)
        stored = new_sem("stored")

        mixtf = cut(MTR_AT, TOPK * T)
        ewf = [cut(W_AT + 8192 * k, P * 64) for k in range(2)]
        zeroed = new_sem("zeroed")

        def barrier(eng, *names):
            for n in names:
                if n in S:
                    S[n].finished(eng)
                else:
                    eng.wait_ge(evacuated[n], streams[n].count)

        block = ctx.enter_context(nc.Block())

        def evacuate(act, name, out, bias, n=T, func=ACT.Identity, scale=1.0):
            def take(idx, slot, loads, i, u):
                act.wait_ge(weights_used, idx + (streams[name].first + 1))
                nc.scalar.activation(out(idx), bank(slot, 0, n), func, bias=bias(idx), scale=scale).then_inc(evacuated[name], 1)
            streams[name].each(act, take)

        def gemm(pe, name, ktiles, rhs, n=T):
            def product(idx, slot, loads, i, u):
                gemm_block(pe, name, idx, slot, loads, ktiles, rhs, n).then_inc(weights_used, 1)
            streams[name].each(pe, product)

        def load_mod(sp, k, u):
            if not (isinstance(k, int) and k < 2):
                sp.wait_ge(mod_used, k - 1)
            sp.dma_start(mod_slots[u % 2], a["w_mod"][k].rearrange("p (b n) -> p b n", b=2)).then_inc(mod_landed[u % 2], 16)

        def modulation(dve, first, last, silu, junk):
            def chunk(k, u, landings):
                dve.wait_ge(mod_landed[u], landings * 16)
                if not (isinstance(k, int) and k == 0):
                    dve.wait_ge(mod_used, k)
                for c in range(2):
                    half_of = lambda v: v[:, c, :].rearrange("p (b n) -> p b n", b=2)
                    done = nc.vector.scalar_tensor_tensor(out=half_of(junk), in0=mod_slots[u], scalar=1.0, in1=half_of(silu),
                                                          op0=ALU.mult, op1=ALU.mult, accum_out=modv[:, k, c:c + 1])
                done.then_inc(mod_used, 1)
            k = first
            if k % 2:
                chunk(k, 1, k // 2 + 1)
                k += 1
            for u in range(2):
                chunk(k + u, u, k // 2 + 1)
            pairs_ = (last - k) // 2
            with dve.Fori(k // 2 + 1, k // 2 + pairs_) as i:
                for u in range(2):
                    chunk(i * 2 + u, u, i + 1)
            if (last - k) % 2:
                chunk(last - 1, 0, (last - 1) // 2 + 1)
            dve.wait_ge(mod_used, last)

        def mod_biased(do, first, last):
            for c in range(2):
                v = modv[:, first:last, c]
                do(f"mod{first}_{c}", nc.vector.scalar_tensor_tensor(out=v, in0=v, scalar=0.5, in1=par("b_mod", first, last - first), op0=ALU.mult, op1=ALU.add))

        def pre_dve(dve):
            dve.wait_ge(inputs_loaded, N_INPUTS * 16)
            do = Do(dve, st_pre, "dve")
            do("halved", nc.vector.tensor_scalar(halves[:, :], params[:, 0:64], 0.5, None, ALU.mult))
            do.wait("act", "cond_tanh")
            do("cond_silu", nc.vector.scalar_tensor_tensor(out=silu1, in0=junk1, scalar=1.0, in1=silu1, op0=ALU.add, op1=ALU.mult))
            do.end()

        def pre_act(act):
            act.wait_ge(inputs_loaded, N_INPUTS * 16)
            do = Do(act, st_pre, "act")
            act.wait_ge(cond_loaded, 16)
            do("cond_tanh", nc.scalar.activation(junk1, silu1, ACT.Tanh, scale=0.5))
            do.end()

        def pre_pe(pe):
            pe.wait_ge(inputs_loaded, N_INPUTS * 16)
            barrier(pe, "pre")

        def n1_act(act):
            barrier(act, "pre")
            norm_act(act, st_n1, 0, xc, sq, root, bank(4, 0, T), T, 1.0 / D)
            evacuate(act, "z", lambda i: z[:, i, :], lambda i: par("b_in", i))

        def n1_pe(pe):
            norm_pe(pe, st_n1, 0, sq, bank(4, 0, T), DC)
            barrier(pe, "norm_x")
            gemm(pe, "z", DC, lambda k: hn[:, k, :])

        def n1_dve(dve):
            norm_dve(dve, st_n1, 0, lambda c: xc[:, c, :], lambda c: hn[:, c, :], root, lambda c: par("ln_gain", c), DC)
            modulation(dve, 0, N_Z, silu1, junk1)

        def lru_dve(dve):
            do = Do(dve, st_lam, "dve")
            do("neg", nc.vector.tensor_scalar(lt3, par("lam", 0, 8), -1.0, None, ALU.mult))
            do.own()
            softplus_dve(do, lt3, lt1, lt2, lt4, nsp)
            do.own()
            do("scaled", nc.vector.tensor_scalar(nsp, nsp, -4.0, None, ALU.mult))
            do.end()
            barrier(dve, "z")

            def chunk(c):
                do = Do(dve, st_lru, "dve", c)
                u = z[:, Z_LRU + c, :]
                do("lag0", nc.vector.tensor_scalar(uc, u, par("conv_w", c + 24), par("conv_b", c), ALU.mult, ALU.add))
                for lag in range(1, 4):
                    do.own()
                    do(f"lag{lag}", nc.vector.scalar_tensor_tensor(
                        out=uc[:, lag:], in0=u[:, 0:T - lag], scalar=par("conv_w", c + (3 - lag) * 8), in1=uc[:, lag:], op0=ALU.mult, op1=ALU.add))
                do.wait("act", "tanh_a")
                do("log_a", nc.vector.tensor_scalar(la, la, 1.0, nsp[:, bass.ds(c, 1)], ALU.add, ALU.mult))
                do.wait("act", "th")
                do("den", nc.vector.tensor_scalar(den, th, -1.0, 1.0, ALU.mult, ALU.add))
                do.own()
                do("inv", nc.vector.reciprocal(den, den))
                do.own()
                do("m", nc.vector.scalar_tensor_tensor(out=lru_m[:, c, :], in0=th, scalar=-2.0, in1=den, op0=ALU.mult, op1=ALU.mult))
                do("gated", nc.vector.scalar_tensor_tensor(out=z[:, Z_LRU + c, :], in0=tx, scalar=1.0, in1=uc, op0=ALU.add, op1=ALU.mult))
                do.own()
                do.end()

            rounds(dve, BC, chunk)
            do = Do(dve, st_lru2, "dve")
            do.wait("act", "root")
            zu = z[:, Z_LRU:Z_LRU + BC, :]
            zg = z[:, Z_LG:Z_LG + BC, :]
            do("drive", nc.vector.scalar_tensor_tensor(out=zu, in0=lru_m, scalar=0.5, in1=zu, op0=ALU.mult, op1=ALU.mult))
            do.own()
            for c in range(BC):
                do(f"scan{c}", nc.vector.tensor_tensor_scan(
                    out=lru_m[:, c, :], data0=lru_a[:, c, :], data1=z[:, Z_LRU + c, :], initial=0.0, op0=ALU.mult, op1=ALU.add))
            do.wait("act", "tanh_gate")
            do("silu", nc.vector.scalar_tensor_tensor(out=zg, in0=zg_tanh, scalar=1.0, in1=zg, op0=ALU.add, op1=ALU.mult))
            do.own()
            do("out", nc.vector.scalar_tensor_tensor(out=zg, in0=lru_m, scalar=0.5, in1=zg, op0=ALU.mult, op1=ALU.mult))
            do.end()

        def lru_act(act):
            do = Do(act, st_lam, "act")
            softplus_act(do, lt1)

            def chunk(idx, slot, loads, i, u):
                do = Do(act, st_lru, "act", idx)
                act.wait_ge(weights_used, idx + (streams["lru"].first + 1))
                if not (isinstance(idx, int) and idx == 0):
                    do.wait("dve", "gated", idx - 1)
                do("tanh_a", nc.scalar.activation(la, bank(slot, 0, T), ACT.Tanh, bias=half("lru_ba", idx), scale=0.5))
                do("tanh_x", nc.scalar.activation(tx, bank(slot, T, T), ACT.Tanh, bias=half("lru_bx", idx), scale=0.5))
                do.wait("dve", "log_a")
                do("a", nc.scalar.activation(lru_a[:, idx, :], la, ACT.Exp))
                do("th", nc.scalar.activation(th, la, ACT.Tanh))
                do.end()

            streams["lru"].each(act, chunk)
            do = Do(act, st_lru2, "act")
            S["lru"].finished(act)
            do("root", nc.scalar.activation(lru_m, lru_m, ACT.Sqrt))
            do.wait("dve", "drive")
            do("tanh_gate", nc.scalar.activation(zg_tanh, z[:, Z_LG:Z_LG + BC, :], ACT.Tanh, scale=0.5))
            do.end()

        def lru_pe(pe):
            barrier(pe, "z")

            def chunk(idx, slot, loads, i, u):
                pe.wait_ge(landed[slot], loads * 16)
                pe.wait_ge(st_lru.steps["dve"].sem, st_lru.steps["dve"].at("lag3", idx))
                nc.tensor.matmul(bank(slot, 0, T), ring[:, slot, 0:P], uc, start=True, stop=True)
                nc.tensor.matmul(bank(slot, T, T), ring[:, slot, P:2 * P], uc, start=True, stop=True).then_inc(weights_used, 1)

            streams["lru"].each(pe, chunk)

        def qk_act(act):
            barrier(act, "lru2", "gates1")

            def part(it):
                do = Do(act, st_qk, "act", it)
                do("squares", nc.scalar.activation(qk_sq, zflat[:, bass.ds(it * 1024 + Z_NQ * T, 1024)], ACT.Square))
                do.wait("pe", "sums1")
                if not isinstance(it, int) or it > 0:
                    do.wait("dve", "scaled3", it - 1)
                do("root", nc.scalar.activation(qk_root, ps[:, 4:6, :].rearrange("p b n -> p (b n)"), ACT.Sqrt, bias=par("eps"), scale=1.0 / P))
                do.end()
            rounds(act, N_QK // 4, part)

        def qk_pe(pe):
            barrier(pe, "lru2")

            def part(it):
                do = Do(pe, st_qk, "pe", it)
                do.wait("act", "squares")
                do("sums0", nc.tensor.matmul(bank(4), ones, qk_sq[:, 0:512], start=True, stop=True))
                do("sums1", nc.tensor.matmul(bank(5), ones, qk_sq[:, 512:1024], start=True, stop=True))
                do.end()
            rounds(pe, N_QK // 4, part)

        def qk_dve(dve):
            def part(it):
                do = Do(dve, st_qk, "dve", it)
                do.wait("act", "root")
                do("inverse", nc.vector.reciprocal(qk_root, qk_root))
                do.own()
                for c in range(4):
                    v = z[:, it * 4 + (Z_NQ + c), :]
                    do(f"scaled{c}", nc.vector.scalar_tensor_tensor(
                        out=v, in0=v, scalar=par("qk_gain", it * 4 + c), in1=qk_root[:, c * T:(c + 1) * T], op0=ALU.mult, op1=ALU.mult))
                do.end()
            rounds(dve, N_QK // 4, part)

        TURNS = [[(c, t) for c in (2 * k, 2 * k + 1) for t in range(NT)] for k in range(VT_N // 2)] + [[(None, 0), (None, 1)]]

        def turn_pe(pe):
            barrier(pe, "qk")
            do = Do(pe, st_tr, "pe")
            for k, parts in enumerate(TURNS):
                if k >= 2:
                    do.wait("act", f"kept{k - 2}")
                for j, (c, t) in enumerate(parts):
                    src = z[:, Z_GB if c is None else Z_VS + c, t * P:(t + 1) * P]
                    last = nc.tensor.transpose(bank(4 + k % 2, j * P, P), src, ident)
                do(f"turned{k}", last)
            do.wait("dve", "logf")
            do("cum0", nc.tensor.matmul(bank(6, 0, BC), upto_mask, logf[:, 0, :], start=True, stop=True))
            nc.tensor.matmul(bank(7, 0, BC), upto_mask, logf[:, 1, :], start=True, stop=False)
            do("cum1", nc.tensor.matmul(bank(7, 0, BC), ones, logf[:, 0, :], start=False, stop=True))
            do.end()

        def turn_act(act):
            barrier(act, "qk")
            do = Do(act, st_tr, "act")
            for k, parts in enumerate(TURNS):
                do.wait("pe", f"turned{k}")
                dst = vt[:, 4 * k:4 * k + 4, :] if k < len(TURNS) - 1 else gb
                do(f"kept{k}", nc.scalar.activation(dst, bank(4 + k % 2, 0, len(parts) * P).rearrange("p (a b) -> p a b", b=P), ACT.Copy))
            do.own()
            do("gate_tanh", nc.scalar.activation(gb[:, :, 32:56], gb[:, :, 0:24], ACT.Tanh, scale=0.5))
            softplus_act(do, ft[0])
            do.end()

        def turn_dve(dve):
            do = Do(dve, st_tr, "dve")
            do.wait("act", "gate_tanh")
            do("gate", nc.vector.tensor_scalar(gb[:, :, 0:24], gb[:, :, 32:56], 1.0, 0.5, ALU.add, ALU.mult))
            do("neg", nc.vector.tensor_scalar(ft[1], gb[:, :, 24:32], -1.0, None, ALU.mult))
            do.own()
            softplus_dve(do, ft[1], ft[0], ft[2], ft[3], logf)
            do.own()
            do("logf", nc.vector.tensor_scalar(logf, logf, -1.0, None, ALU.mult))
            do.wait("pe", "cum1")
            do("cumkept", nc.vector.tensor_copy(cum, ps[:, 6:8, 0:BC]))
            do.end()

        def cmp_dve(dve):
            barrier(dve, "turn")

            def kv(it):
                do = Do(dve, st_cmp, "dve", it)
                zk = [z[:, it * 2 + (Z_KC + g), :].rearrange("p (n r) -> p r n", r=16) for g in range(2)]
                b4 = blkf[:, bass.ds(it * 960, 960)].rearrange("p (h r g n) -> p h r g n", h=2, r=16, g=2)
                for h in range(2):
                    for g in range(2):
                        last = nc.vector.tensor_tensor(
                            b4[:, h, :, g, :], zk[g][:, :, h:h + NCMP],
                            par("pos", it * 32 + h * 16, 16)[:, :, None].to_broadcast([P, 16, NCMP]), ALU.add)
                        if g == 1:
                            do(f"b{h}", last)
                do.wait("act", "tanh")
                hv = bank45[:, :, 0:30]
                do("silu", nc.vector.scalar_tensor_tensor(out=cth, in0=cth, scalar=1.0, in1=hv, op0=ALU.add, op1=ALU.mult))
                do.own()
                do("halved", nc.vector.tensor_scalar(chidf[:, bass.ds(it * 60, 60)], cthf, 0.5, None, ALU.mult))
                do.own()
                do.end()
            rounds(dve, 2, kv)
            do = Do(dve, st_cmp2, "dve")
            do.wait("act", "root")
            do("inv", nc.vector.reciprocal(kcr, kcr))
            do.own()
            do("out", nc.vector.scalar_tensor_tensor(out=kc, in0=kc, scalar=par("cmp_gain"), in1=kcr, op0=ALU.mult, op1=ALU.mult))
            do.end()

        def cmp_pe(pe):
            barrier(pe, "turn")

            def part(idx, slot, loads, i, u):
                pe.wait_ge(landed[slot], loads * 16)
                if u == 0:
                    pe.wait_ge(st_cmp.steps["dve"].sem, st_cmp.steps["dve"].at("b1", i))
                bk = blkf[:, bass.ds(i * 960, 960)].rearrange("p (r n) -> p r n", n=30)
                for r in range(8):
                    for h in range(2):
                        last = nc.tensor.matmul(bank(4 + h, 0, 30), ring[:, slot, r * T + h * P:r * T + (h + 1) * P], bk[:, u * 8 + r, :],
                                                start=(u == 0 and r == 0), stop=(u == 3 and r == 7))
                last.then_inc(weights_used, 1)

            streams["cmp"].each(pe, part)
            do = Do(pe, st_cmp2, "pe")
            S["cmp"].finished(pe)
            w2 = misc[:, 0:512].rearrange("p (a n) -> p a n", n=P)
            for h in range(2):
                last = nc.tensor.matmul(bank(6, 0, 30), w2[:, h, :], chid[:, h, :], start=(h == 0), stop=(h == 1))
            do("kc", last)
            for g in range(2):
                for h in range(2):
                    last = nc.tensor.matmul(bank(4 + g, 0, P)[0:NCMP, :], chid[:, 2 + h, g * NCMP:(g + 1) * NCMP], w2[:, 2 + h, :],
                                            start=(h == 0), stop=(h == 1))
                do(f"vc{g}", last)
            do.wait("act", "squares")
            do("sums", nc.tensor.matmul(bank(7, 0, 30), ones, kcs, start=True, stop=True))
            do.end()

        def cmp_act(act):
            barrier(act, "turn")

            def kv(it):
                do = Do(act, st_cmp, "act", it)
                act.wait_ge(weights_used, it * 4 + (streams["cmp"].first + 4))
                do("tanh", nc.scalar.activation(cth, bank45[:, :, 0:30], ACT.Tanh, scale=0.5))
                do.end()
            rounds(act, 2, kv)
            do = Do(act, st_cmp2, "act")
            do.wait("pe", "kc")
            do("copied", nc.scalar.activation(kc, bank(6, 0, 30), ACT.Copy))
            do("squares", nc.scalar.activation(kcs, bank(6, 0, 30), ACT.Square))
            do.wait("pe", "sums")
            do("root", nc.scalar.activation(kcr, bank(7, 0, 30), ACT.Sqrt, bias=par("eps"), scale=1.0 / P))
            for g in range(2):
                do(f"vck{g}", nc.scalar.activation(vc[0:NCMP, g, :], bank(4 + g, 0, P)[0:NCMP, :], ACT.Copy))
            do.end()

        SPAN = ((0, 128), (128, 256))

        def nsa_head(g, fn):
            def run(eng):
                with eng.Fori(4 * g, 4 * g + 4) as h:
                    fn(h, g)
            return run

        def nsa_act(act):
            barrier(act, "cmp2")

            def head(h, g):
                do = Do(act, st_nsa, "act", h)
                do("q", nc.scalar.activation(nq, z[:, h + Z_NQ, :], ACT.Copy))
                do.wait("dve", "guard")
                for b, t in BR:
                    lo, n = SPAN[t]
                    src, dst = (ncs[:, t, 0:NCMP], nce[:, t, 0:NCMP]) if b == 2 else (nst[:, b, lo:lo + n], nex[:, b, lo:lo + n])
                    do(f"e{b}{t}", nc.scalar.activation(dst, src, ACT.Exp, bias=nmx[:, t, b:b + 1], accum_out=nsm[:, t, b:b + 1]))
                do.wait("pe", "turned")
                do("et0", nc.scalar.activation(net[:, 0, :], bank(5, 0, 384), ACT.Copy))
                do("et1", nc.scalar.activation(net[:, 1, :], bank(6, 0, 384), ACT.Copy))
                do("ctk", nc.scalar.activation(nct[0:NCMP, :, :], bank(7, 0, 256)[0:NCMP, :].rearrange("p (a b) -> p a b", b=P), ACT.Copy))
                do.end()
            for g in range(2):
                nsa_head(g, head)(act)

        def nsa_pe(pe):
            barrier(pe, "cmp2")

            def head(h, g):
                do = Do(pe, st_nsa, "pe", h)
                do.wait("act", "q")
                for t in range(NT):
                    lo, n = SPAN[t]
                    q = nq[:, t * P:(t + 1) * P]
                    nc.tensor.matmul(bank(0, lo, n), q, z[:, Z_KS + g, 0:n], start=True, stop=True)
                    nc.tensor.matmul(bank(1, lo, n), q, z[:, Z_KW + g, 0:n], start=True, stop=True)
                    last = nc.tensor.matmul(bank(2, t * 16, NCMP), q, kc[:, g * NCMP:(g + 1) * NCMP], start=True, stop=True)
                do("s", last)
                do.wait("dve", "w21")
                for b in range(2):
                    for j in range(3):
                        nc.tensor.transpose(bank(5 + b, j * P, P), nex[:, b, j * P:(j + 1) * P], ident)
                for t in range(NT):
                    last = nc.tensor.transpose(bank(7, t * P, P)[0:NCMP, :], nce[:, t, 0:NCMP], ident)
                do("turned", last)
                do.wait("act", "ctk")
                for t in range(NT):
                    out = bank(4, t * P, P)
                    keys = (0,) if t == 0 else (1, 2)
                    for b in range(2):
                        for n, j in enumerate(keys):
                            nc.tensor.matmul(out, vt[:, (2 * b + g) * NT + n, :], net[:, b, j * P:(j + 1) * P],
                                             start=(b == 0 and n == 0), stop=False)
                    last = nc.tensor.matmul(out, vc[0:NCMP, g, :], nct[0:NCMP, t, :], start=False, stop=True)
                do("o", last)
                do.end()
            for g in range(2):
                nsa_head(g, head)(pe)

        def nsa_dve(dve):
            barrier(dve, "cmp2", "gates1")

            def head(h, g):
                do = Do(dve, st_nsa, "dve", h)
                do.wait("pe", "s")
                for b, name in enumerate(("ss", "sw")):
                    do(name, nc.vector.scalar_tensor_tensor(out=nst[:, b, :], in0=bank(b, 0, 384), scalar=SCALE, in1=causal,
                                                            op0=ALU.mult, op1=ALU.subtract))
                cm = con("cmp_mask").rearrange("p (t n) -> p t n", n=16)[:, :, 0:NCMP]
                do("sc", nc.vector.scalar_tensor_tensor(out=ncs[:, :, 0:NCMP], in0=bank(2, 0, 32).rearrange("p (t n) -> p t n", n=16)[:, :, 0:NCMP],
                                                        scalar=SCALE, in1=cm, op0=ALU.mult, op1=ALU.subtract))
                do.own()
                for t in range(NT):
                    lo, n = SPAN[t]
                    do(f"max{t}", nc.vector.tensor_reduce(nmx[:, t, 0:2], nst[:, :, lo:lo + n], AX_X, ALU.max, negate=True))
                do("maxc", nc.vector.tensor_reduce(nmx[:, :, 2], ncs[:, :, 0:NCMP], AX_X, ALU.max, negate=True))
                do.own()
                do("guard", nc.vector.tensor_scalar(nmx, nmx, GUARD, None, ALU.min))
                do.wait("act", "e21")
                do("floor", nc.vector.tensor_scalar(nsm, nsm, 1e-30, None, ALU.max))
                do.own()
                do("inv", nc.vector.reciprocal(nsm, nsm))
                do.own()
                do("gates", nc.vector.tensor_tensor(nsm, nsm, gb[:, :, bass.ds(h * 3, 3)], ALU.mult))
                do.own()
                for b, t in BR:
                    lo, n = SPAN[t]
                    v = nce[:, t, 0:NCMP] if b == 2 else nex[:, b, lo:lo + n]
                    do(f"w{b}{t}", nc.vector.tensor_scalar(v, v, nsm[:, t, b:b + 1], None, ALU.mult))
                do.wait("pe", "o")
                y = z[:, h + Z_NG, :]
                do("y", nc.vector.tensor_tensor(y, y, bank(4, 0, T), ALU.mult))
                do.end()
            for g in range(2):
                nsa_head(g, head)(dve)

        GATES = (Z_NG, Z_FG)

        def gates_act(act):
            barrier(act, "lru2")
            for it, c in enumerate(GATES):
                do = Do(act, st_gate, "act", it)
                if it:
                    do.wait("dve", "silu", it - 1)
                do("tanh", nc.scalar.activation(gates_tmp, z[:, c:c + BC, :], ACT.Tanh, scale=0.5))
                do.end()

        def gates_dve(dve):
            for it, c in enumerate(GATES):
                do = Do(dve, st_gate, "dve", it)
                do.wait("act", "tanh")
                v = z[:, c:c + BC, :]
                do("silu", nc.vector.scalar_tensor_tensor(out=v, in0=gates_tmp, scalar=1.0, in1=v, op0=ALU.add, op1=ALU.mult))
                do.own()
                do("halved", nc.vector.tensor_scalar(v, v, 0.5, None, ALU.mult))
                do.end()

        def fox_act(act):
            barrier(act, "nsa")

            def head(h):
                do = Do(act, st_fox, "act", h)
                do("q", nc.scalar.activation(fq, z[:, h + Z_FQ, :], ACT.Copy))
                if not isinstance(h, int) or h > 0:
                    do.wait("pe", "o", h - 1)
                do("v", nc.scalar.activation(fv, vtf[:, bass.ds(h * (NT * P) + 4 * NT * P, NT * P)].rearrange("p (a b) -> p a b", b=P), ACT.Copy))
                for t in range(NT):
                    lo, n = SPAN[t]
                    do.wait("dve", f"max{t}")
                    do(f"e{t}", nc.scalar.activation(fe[:, lo:lo + n], fs[:, lo:lo + n], ACT.Exp, bias=fmx[:, t:t + 1], accum_out=fsm[:, t:t + 1]))
                do.wait("pe", "turned")
                do("etk", nc.scalar.activation(fet, bank(2, 0, 384), ACT.Copy))
                do.end()
            rounds(act, BC, head)

        def fox_pe(pe):
            barrier(pe, "nsa")

            def head(h):
                do = Do(pe, st_fox, "pe", h)
                do.wait("act", "q")
                if not isinstance(h, int) or h > 0:
                    do.wait("dve", "y", h - 1)
                for t in range(NT):
                    lo, n = SPAN[t]
                    last = nc.tensor.matmul(bank(0, lo, n), fq[:, t * P:(t + 1) * P], z[:, h + Z_FK, 0:n], start=True, stop=True)
                do("s", last)
                do.wait("dve", "r1")
                nc.tensor.matmul(bank(1, 0, P), ones, fr[:, 0, :], start=True, stop=True)
                nc.tensor.matmul(bank(1, P, P), ones, fr[:, 1, :], start=True, stop=False)
                do("c", nc.tensor.matmul(bank(1, P, P), ones, logf[:, 0, bass.ds(h, 1)].to_broadcast([P, P]), start=False, stop=True))
                do.wait("dve", "w1")
                for j in range(3):
                    last = nc.tensor.transpose(bank(2, j * P, P), fe[:, j * P:(j + 1) * P], ident)
                do("turned", last)
                do.wait("act", "etk")
                nc.tensor.matmul(bank(3, 0, P), fv[:, 0, :], fet[:, 0:P], start=True, stop=True)
                nc.tensor.matmul(bank(3, P, P), fv[:, 0, :], fet[:, P:2 * P], start=True, stop=False)
                do("o", nc.tensor.matmul(bank(3, P, P), fv[:, 1, :], fet[:, 2 * P:3 * P], start=False, stop=True))
                do.end()
            rounds(pe, BC, head)

        def fox_dve(dve):
            barrier(dve, "nsa")

            def head(h):
                do = Do(dve, st_fox, "dve", h)
                for t in range(NT):
                    do(f"r{t}", nc.vector.tensor_scalar(fr[:, t, :], upto_mask, logf[:, t, bass.ds(h, 1)], None, ALU.mult))
                do.wait("pe", "c")
                for t in range(NT):
                    lo, n = SPAN[t]
                    do(f"b{t}", nc.vector.scalar_tensor_tensor(out=fb[:, lo:lo + n], in0=bank(1, 0, n), scalar=cum[:, t, bass.ds(h, 1)],
                                                               in1=causal[:, lo:lo + n], op0=ALU.subtract, op1=ALU.add))
                do.own()
                do.wait("pe", "s")
                do("s", nc.vector.scalar_tensor_tensor(out=fs, in0=bank(0, 0, 384), scalar=SCALE, in1=fb, op0=ALU.mult, op1=ALU.subtract))
                do.own()
                for t in range(NT):
                    lo, n = SPAN[t]
                    do(f"max{t}", nc.vector.tensor_reduce(fmx[:, t:t + 1], fs[:, lo:lo + n], AX_X, ALU.max, negate=True))
                do.wait("act", "e1")
                do("inv", nc.vector.reciprocal(fsm, fsm))
                do.own()
                for t in range(NT):
                    lo, n = SPAN[t]
                    do(f"w{t}", nc.vector.tensor_scalar(fe[:, lo:lo + n], fe[:, lo:lo + n], fsm[:, t:t + 1], None, ALU.mult))
                do.wait("pe", "o")
                y = z[:, h + Z_FG, :]
                do("y", nc.vector.tensor_tensor(y, y, bank(3, 0, T), ALU.mult))
                do.end()
            rounds(dve, BC, head)

        YAT = (Z_LG, Z_NG, Z_FG)

        def merge_pe(pe):
            barrier(pe, "fox")

            def part(idx, slot, loads, i, u):
                y = YAT[u % 3]
                pe.wait_ge(landed[slot], loads * 16)
                if not (isinstance(idx, int) and idx < SLOTS):
                    pe.wait_ge(st_merge.steps["act"].sem, st_merge.steps["act"].at("y", idx - SLOTS))
                for k in range(DC):
                    nc.tensor.matmul(bank(slot, 0, T), ring[:, slot, k * P:(k + 1) * P], hn[:, k, :], start=(k == 0), stop=(k == DC - 1))
                for k in range(BC):
                    last = nc.tensor.matmul(bank(4 + slot, 0, T), ring[:, slot, D + k * P:D + (k + 1) * P], z[:, y + k, :],
                                            start=(k == 0), stop=(k == BC - 1))
                last.then_inc(weights_used, 1)
            streams["merge"].each(pe, part, step=12)

        def merge_act(act):
            def part(idx, slot, loads, i, u):
                do = Do(act, st_merge, "act", idx)
                act.wait_ge(weights_used, idx + (streams["merge"].first + 1))
                if not (isinstance(idx, int) and idx < 2):
                    do.wait("dve", "summed", idx - 2)
                do("gate", nc.scalar.activation(mth[:, u % 2, :], bank(slot, 0, T), ACT.Tanh, bias=half("b_merge", idx), scale=0.5))
                do("y", nc.scalar.activation(mtm[:, u % 2, :], bank(4 + slot, 0, T), ACT.Copy, scale=0.5))
                do.end()
            streams["merge"].each(act, part, step=12)

        def merge_dve(dve):
            barrier(dve, "fox")

            def part(idx, slot, loads, i, u):
                do = Do(dve, st_merge, "dve", idx)
                do.wait("act", "y")
                d = merged[:, i * 4 + u // 3, :]
                dst = d if u % 3 == 0 else mtm[:, u % 2, :]
                do("scaled", nc.vector.scalar_tensor_tensor(out=dst, in0=mth[:, u % 2, :], scalar=1.0, in1=mtm[:, u % 2, :], op0=ALU.add, op1=ALU.mult))
                do.own()
                if u % 3 == 0:
                    ins = nc.vector.tensor_copy(tick, par("eps"))
                else:
                    ins = nc.vector.tensor_tensor(d, d, dst, ALU.add)
                do("summed", ins)
                do.end()
            streams["merge"].each(dve, part, step=12)

        def add_block(dve, name, out, scalar=None):
            def take(idx, slot, loads, i, u):
                dve.wait_ge(weights_used, idx + (streams[name].first + 1))
                o = out(idx)
                if scalar is None:
                    ins = nc.vector.tensor_tensor(o, o, bank(slot, 0, T), ALU.add)
                else:
                    ins = nc.vector.scalar_tensor_tensor(out=o, in0=bank(slot, 0, T), scalar=scalar(idx), in1=o, op0=ALU.mult, op1=ALU.add)
                ins.then_inc(evacuated[name], 1)
            streams[name].each(dve, take)

        def out_pe(pe):
            barrier(pe, "merge")
            gemm(pe, "out", DC, lambda k: merged[:, k, :])

            def ple(idx, slot, loads, i, u):
                pe.wait_ge(landed[slot], loads * 16)
                do = Do(pe, st_ple, "pe", idx)
                for half_ in range(2):
                    if idx or half_:
                        do.wait("act", "e0" if half_ else "e1", idx if half_ else idx - 1)
                    for c in range(4):
                        n = half_ * 4 + c
                        for k in range(2):
                            last = nc.tensor.matmul(bank(4 + c // 2, (c % 2) * T, T), ring[:, slot, k * 1024 + n * P:k * 1024 + (n + 1) * P],
                                                    pT[:, k, :], start=(k == 0), stop=(k == 1))
                    if half_ == 0:
                        do("p0", last)
                    else:
                        last.then_inc(weights_used, 1)
                do.end()
            streams["ple"].each(pe, ple)
            barrier(pe, "ple")
            norm_pe(pe, st_e, 0, e_sq, bank(6, 0, T), DC)
            barrier(pe, "out", "norm_e")
            gemm(pe, "ple_gate", DC, lambda k: xc[:, k, :])

        def out_act(act):
            barrier(act, "fox", "merge")
            for idx in range(2):
                do = Do(act, st_ple, "act", idx)
                for half_ in range(2):
                    if half_ == 0:
                        do.wait("pe", "p0")
                    else:
                        act.wait_ge(weights_used, streams["ple"].first + idx + 1)
                    do(f"e{half_}", nc.scalar.activation(e[:, idx * 8 + half_ * 4:idx * 8 + half_ * 4 + 4, :],
                                                         ps[:, 4:6, :].rearrange("p b (c t) -> p (b c) t", t=T), ACT.Copy))
                do.own()
            norm_act(act, st_e, 0, e, e_sq, e_root, bank(6, 0, T), T, 1.0 / D)

            def gate(idx, slot, loads, i, u):
                do = Do(act, st_pg, "dve", idx)
                act.wait_ge(weights_used, idx + (streams["ple_gate"].first + 1))
                if not (isinstance(idx, int) and idx < SLOTS):
                    do.wait("dve", "mixed", idx - SLOTS)
                nc.scalar.activation(gth[:, u, :], bank(slot, 0, T), ACT.Tanh, scale=0.5).then_inc(evacuated["ple_gate"], 1)
            streams["ple_gate"].each(act, gate)

        def out_dve(dve):
            add_block(dve, "out", lambda i: xc[:, i, :])
            norm_dve(dve, st_e, 0, lambda c: e[:, c, :], lambda c: e[:, c, :], e_root, lambda c: par("ple_gain", c), DC)
            barrier(dve, "norm_e", "out")

            def gate(idx, slot, loads, i, u):
                do = Do(dve, st_pg, "dve", idx)
                dve.wait_ge(evacuated["ple_gate"], idx + 1)
                v = e[:, idx, :]
                do("mixed", nc.vector.scalar_tensor_tensor(out=v, in0=gth[:, u, :], scalar=1.0, in1=v, op0=ALU.add, op1=ALU.mult))
                do.own()
                do("added", nc.vector.scalar_tensor_tensor(out=x2[:, idx, :], in0=v, scalar=0.5, in1=xc[:, idx, :], op0=ALU.mult, op1=ALU.add))
                do.end()
            streams["ple_gate"].each(dve, gate)
            barrier(dve, "ple_gate", "pg")
            do = Do(dve, st_x2, "dve")
            do("moved", nc.vector.tensor_copy(xc, x2))
            do.end()

        def n2_act(act):
            barrier(act, "x2")
            do = Do(act, st_gain, "act")
            act.wait_ge(cond_loaded, 32)
            do("cond_tanh", nc.scalar.activation(junk2, silu2, ACT.Tanh, scale=0.5))
            do.end()
            norm_act(act, st_n2[0], 0, xc, sq2, root2, bank(4, 0, T), T, 1.0 / D)
            act.wait_ge(ctx_loaded, 16)
            barrier(act, "norm2_0")
            norm_act(act, st_n2[1], 0, hcat[:, 1, :, :], sq2, root2, bank(5, 0, T), T, 1.0 / D)
            barrier(act, "norm2_1")
            do = Do(act, st_shift, "act")
            for c in range(2 * DC):
                s, k = c // DC, c % DC
                v = hcat[:, s, k, :]
                do(f"shift{c}", nc.scalar.activation(v, v, ACT.Identity, bias=modv[:, k, s:s + 1]))
            do.end()
            copy_out(act, "y", lambda i: yv[:, i, :], 2 * T)
            act.wait_ge(mod_used, N_MOD)
            s = streams["l"]
            for at, count, with_conv in ((0, 16, True), (16, 4, False)):
                def take(idx, slot, loads, i, u, at=at, with_conv=with_conv):
                    act.wait_ge(weights_used, idx + (s.first + at + 1))
                    nc.scalar.activation(lv[:, idx + at, :], bank(slot, 0, T), ACT.Copy).then_inc(evacuated["l"], 1)
                    if with_conv:
                        conv_tanh(act, st_ckvv, idx, 2)
                Stream(s.first + at, count, s.cols).each(act, take)

        def copy_out(act, name, out, n):
            def take(idx, slot, loads, i, u):
                act.wait_ge(weights_used, idx + (streams[name].first + 1))
                nc.scalar.activation(out(idx), bank(slot, 0, n), ACT.Copy).then_inc(evacuated[name], 1)
            streams[name].each(act, take)

        def n2_pe(pe):
            barrier(pe, "x2")
            norm_pe(pe, st_n2[0], 0, sq2, bank(4, 0, T), DC)
            norm_pe(pe, st_n2[1], 0, sq2, bank(5, 0, T), DC)
            barrier(pe, "norm2_1", "shift")

            def product(idx, slot, loads, i, u):
                gemm_block(pe, "y", idx, slot, loads, DC, lambda k: hcat[:, :, k, :], 2 * T,
                           out=bank(slot).rearrange("p (s t) -> p s t", s=2)).then_inc(weights_used, 1)
            streams["y"].each(pe, product)
            barrier(pe, "y")
            gemm(pe, "l", DC, lambda k: hcat[:, 0, k, :])

        def n2_dve(dve):
            do = Do(dve, st_gain, "dve")
            mod_biased(do, 0, N_Z)
            do.own()
            do("first", nc.vector.scalar_tensor_tensor(
                out=gain1v, in0=modv[:, DC:2 * DC, :], scalar=1.0, in1=par("norm1", 0, DC)[:, :, None].to_broadcast([P, DC, 2]),
                op0=ALU.add, op1=ALU.mult))
            do.own()
            norm_dve(dve, st_n2[0], 0, lambda c: xc[:, c, :], lambda c: hcat[:, 0, c, :], root2, lambda c: gain1v[:, c, 0:1], DC)
            dve.wait_ge(ctx_loaded, 16)
            norm_dve(dve, st_n2[1], 0, lambda c: hcat[:, 1, c, :], lambda c: hcat[:, 1, c, :], root2, lambda c: gain1v[:, c, 1:2], DC)
            do.wait("act", "cond_tanh")
            do("cond_silu", nc.vector.scalar_tensor_tensor(out=silu2, in0=junk2, scalar=1.0, in1=silu2, op0=ALU.add, op1=ALU.mult))
            do.own()
            modulation(dve, N_Z, N_MOD, silu2, junk2)
            mod_biased(do, N_Z, N_MOD)
            do.own()
            do("second", nc.vector.scalar_tensor_tensor(
                out=gain2v, in0=modv[:, 4 * DC:5 * DC, 0], scalar=1.0, in1=par("norm2", 0, DC), op0=ALU.add, op1=ALU.mult))
            do.own()
            do.end()
            barrier(dve, "y")

            def conv_kv(c):
                do, u = Do(dve, st_ckvv, "dve", c), yv[:, c + Y_K, :].rearrange("p (s t) -> p s t", t=T)
                conv_taps(do, c, u, 8, 2)
                conv_out(do, u, 2)
            rounds(dve, 16, conv_kv)

        def mla_act(act):
            barrier(act, "y", "l", "conv_kv")
            sq4 = msq.rearrange("p (c t) -> p c t", t=T)
            norm_act(act, st_cq, 0, lv[:, L_CQ:L_CQ + 4, :], sq4, mroot[:, 0:T], bank(4, 0, T), T, 1.0 / 512)
            barrier(act, "norm_cq")
            norm_act(act, st_ckv, 0, yv[:, Y_KV:Y_KV + 2, :], msq.rearrange("p (c t) -> p c t", t=2 * T), mroot, bank(5), 2 * T, 1.0 / 256)
            do = Do(act, st_kr, "act")
            do.wait("pe", "dup")
            do("ctx", nc.scalar.activation(krd[:, T:2 * T], bank(6, T, T), ACT.Copy))
            do.end()

            def head(idx, slot, loads, i, u):
                do = Do(act, st_mla, "act", idx)
                act.wait_ge(weights_used, idx + (streams["mla"].first + 1))
                do("qn", nc.scalar.activation(mq, bank(0, 0, T), ACT.Copy))
                do("qr", nc.scalar.activation(mqr[0:64, :], bank(0, T, T)[0:64, :], ACT.Copy))
                do("kn", nc.scalar.activation(mk, bank(1), ACT.Copy))
                do("v", nc.scalar.activation(mv, bank(2).rearrange("p (a b) -> p a b", b=P), ACT.Copy))
                conv_tanh(act, st_cvq, idx, 1)
                do.wait("dve", "neg")
                for t in range(NT):
                    do(f"e{t}", nc.scalar.activation(me[:, t, :], bank(4 + t), ACT.Exp, bias=mmx[:, t:t + 1], scale=MLA_SCALE, accum_out=msm[:, t:t + 1]))
                for t in range(NT):
                    do.wait("pe", f"turned{t}")
                    do(f"et{t}", nc.scalar.activation(met[:, t, :], bank(6 + t), ACT.Copy))
                do.end()
            streams["mla"].each(act, head)

        def mla_pe(pe):
            barrier(pe, "y", "l")
            norm_pe(pe, st_cq, 0, msq.rearrange("p (c t) -> p c t", t=T), bank(4, 0, T), 4)
            norm_pe(pe, st_ckv, 0, msq.rearrange("p (c t) -> p c t", t=2 * T), bank(5), 2)
            do = Do(pe, st_kr, "pe")
            do("dup", nc.tensor.matmul(bank(6), con("dup"), yv[:, Y_KR, :], start=True, stop=True))
            do("rot", nc.tensor.matmul(bank(7, 0, T), con("duprot"), yv[:, Y_KR, 0:T], start=True, stop=True))
            do.end()
            barrier(pe, "norm_cq", "norm_ckv", "kr")

            def head(idx, slot, loads, i, u):
                do = Do(pe, st_mla, "pe", idx)
                pe.wait_ge(landed[slot], loads * 16)
                if not (isinstance(idx, int) and idx == 0):
                    do.wait("dve", "y", idx - 1)
                w = ring[:, slot, :]
                for k in range(4):
                    nc.tensor.matmul(bank(0, 0, T), w[:, k * 192:k * 192 + P], lv[:, L_CQ + k, :], start=(k == 0), stop=(k == 3))
                for k in range(4):
                    nc.tensor.matmul(bank(0, T, T)[0:64, :], w[:, k * 192 + P:k * 192 + 192], lv[:, L_CQ + k, :], start=(k == 0), stop=(k == 3))
                for k in range(2):
                    nc.tensor.matmul(bank(1), w[:, 768 + k * 256:768 + k * 256 + P], yv[:, Y_KV + k, :], start=(k == 0), stop=(k == 1))
                for j in range(4):
                    for k in range(2):
                        last = nc.tensor.matmul(bank(2, j * P, P), yv[:, Y_KV + k, j * P:(j + 1) * P],
                                                w[:, 768 + k * 256 + P:768 + (k + 1) * 256], start=(k == 0), stop=(k == 1))
                last.then_inc(weights_used, 1)
                do.wait("act", "qr")
                do("rot", nc.tensor.matmul(bank(3, 0, T)[0:64, :], con("rot")[0:64, 0:64], mqr[0:64, :], start=True, stop=True))
                do.wait("act", "kn")
                do.wait("dve", "sum")
                for t in range(NT):
                    nc.tensor.matmul(bank(4 + t), mq[:, t * P:(t + 1) * P], mk, start=True, stop=False)
                    last = nc.tensor.matmul(bank(4 + t), mqt[0:64, t * P:(t + 1) * P], krd[0:64, :], start=False, stop=True)
                do("s", last)
                for t in range(NT):
                    do.wait("dve", f"w{t}")
                    for j in range(4):
                        last = nc.tensor.transpose(bank(6 + t, j * P, P), me[:, t, j * P:(j + 1) * P], ident)
                    do(f"turned{t}", last)
                do.wait("act", "et1")
                for t in range(NT):
                    for j in range(4):
                        last = nc.tensor.matmul(bank(3, T + t * P, P), mv[:, j, :], met[:, t, j * P:(j + 1) * P], start=(j == 0), stop=(j == 3))
                do("o", last)
                do.end()
            streams["mla"].each(pe, head)

        def mla_dve(dve):
            norm_dve(dve, st_cq, 0, lambda c: lv[:, L_CQ + c, :], lambda c: lv[:, L_CQ + c, :], mroot[:, 0:T], lambda c: par("q_norm", c), 4)
            norm_dve(dve, st_ckv, 0, lambda c: yv[:, Y_KV + c, :], lambda c: yv[:, Y_KV + c, :], mroot, lambda c: par("kv_norm", c), 2)
            do = Do(dve, st_kr, "dve")
            do.wait("pe", "rot")
            do.wait("act", "ctx")
            do("cos", nc.vector.tensor_tensor(krd[:, 0:T], bank(6, 0, T), con("cos"), ALU.mult))
            do("sin", nc.vector.tensor_tensor(krt, bank(7, 0, T), con("sin"), ALU.mult))
            do.own()
            do("sum", nc.vector.tensor_tensor(krd[:, 0:T], krd[:, 0:T], krt, ALU.add))
            do.end()

            def head(idx, slot, loads, i, u):
                do = Do(dve, st_mla, "dve", idx)
                conv, q = Do(dve, st_cvq, "dve", idx), lv[:, idx + L_Q, :].rearrange("p (s t) -> p s t", s=1)
                conv_taps(conv, idx, q, 0, 1)
                do.wait("act", "qr")
                do("cos", nc.vector.tensor_tensor(mqt[0:64, :], mqr[0:64, :], con("cos")[0:64, :], ALU.mult))
                do.wait("pe", "rot")
                do.own()
                do("sin", nc.vector.tensor_tensor(mqr[0:64, :], bank(3, 0, T)[0:64, :], con("sin")[0:64, :], ALU.mult))
                do.own()
                do("sum", nc.vector.tensor_tensor(mqt[0:64, :], mqt[0:64, :], mqr[0:64, :], ALU.add))
                do.wait("pe", "s")
                do("max", nc.vector.tensor_reduce(mmx, ps[:, 4:6, :], AX_X, ALU.max, negate=True))
                do.own()
                do("neg", nc.vector.tensor_scalar(mmx, mmx, MLA_SCALE, None, ALU.mult))
                conv_out(conv, q, 1)
                do.wait("act", "e1")
                do("inv", nc.vector.reciprocal(msm, msm))
                do.own()
                for t in range(NT):
                    do(f"w{t}", nc.vector.tensor_scalar(me[:, t, :], me[:, t, :], msm[:, t:t + 1], None, ALU.mult))
                do.wait("pe", "o")
                do("y", nc.vector.tensor_copy(my[:, idx, :], bank(3, T, T)))
                do.end()
            streams["mla"].each(dve, head)

        def conv_taps(do, c, u, first_w, seqs):
            out = ctmp[:, 0:seqs, :]
            do("mid", nc.vector.tensor_scalar(out, u, par("conv2_w", c + (2 * 24 + first_w)), None, ALU.mult))
            for name, k in (("lm2", -2), ("lm1", -1), ("lp1", 1), ("lp2", 2)):
                do.own()
                lo, hi = max(0, -k), T - max(0, k)
                o = out[:, :, lo:hi]
                do(name, nc.vector.scalar_tensor_tensor(out=o, in0=u[:, :, lo + k:hi + k], scalar=par("conv2_w", c + ((2 + k) * 24 + first_w)),
                                                        in1=o, op0=ALU.mult, op1=ALU.add))

        def conv_out(do, u, seqs):
            do.wait("act", "tanh")
            do("out", nc.vector.scalar_tensor_tensor(out=u, in0=cth2[:, 0:seqs, :], scalar=1.0, in1=ctmp[:, 0:seqs, :], op0=ALU.add, op1=ALU.mult))
            do.own()
            do.end()

        def conv_tanh(act, st, c, seqs):
            do = Do(act, st, "act", c)
            do.wait("dve", "lp2")
            do("tanh", nc.scalar.activation(cth2[:, 0:seqs, :], ctmp[:, 0:seqs, :], ACT.Tanh, scale=0.5))
            do.end()

        def l2_stages():
            return ((st_lk, lambda c: yv[:, c + Y_K, :], 2 * T), (st_lq, lambda c: lv[:, c + L_Q, :], T))

        def conv_dve(dve):
            for st, chunk, w in l2_stages():
                def norm(it, st=st, chunk=chunk, w=w):
                    do = Do(dve, st, "dve", it)
                    for k in range(2):
                        v, r = chunk(it * 2 + k), l2_root[k][:, 0:w]
                        do.wait("act", f"root{k}")
                        do(f"inv{k}", nc.vector.reciprocal(r, r))
                        do.own()
                        do(f"out{k}", nc.vector.scalar_tensor_tensor(out=v, in0=v, scalar=0.5 if w == 2 * T else 0.5 * SCALE, in1=r, op0=ALU.mult, op1=ALU.mult))
                    do.end()
                rounds(dve, 4, norm)

        def conv_act(act):
            barrier(act, "mla", "conv_q")
            for st, chunk, w in l2_stages():
                def norm(it, st=st, chunk=chunk, w=w):
                    do = Do(act, st, "act", it)
                    for k in range(2):
                        do(f"squares{k}", nc.scalar.activation(l2_sq[k][:, 0:w], chunk(it * 2 + k), ACT.Square, scale=0.5))
                    for k in range(2):
                        do.wait("pe", f"sums{k}")
                        if not (isinstance(it, int) and it == 0):
                            do.wait("dve", f"out{k}", it - 1)
                        do(f"root{k}", nc.scalar.activation(l2_root[k][:, 0:w], bank(4 + k, 0, w), ACT.Sqrt, bias=par("eps")))
                    do.end()
                rounds(act, 4, norm)
                S["l2_k"].finished(act)

        def conv_pe(pe):
            for st, chunk, w in l2_stages():
                def norm(it, st=st, w=w):
                    do = Do(pe, st, "pe", it)
                    for k in range(2):
                        do.wait("act", f"squares{k}")
                        if not (isinstance(it, int) and it == 0):
                            do.wait("act", f"root{k}", it - 1)
                        do(f"sums{k}", nc.tensor.matmul(bank(4 + k, 0, w), ones, l2_sq[k][:, 0:w], start=True, stop=True))
                    do.end()
                rounds(pe, 4, norm)
                S["l2_k"].finished(pe)

        ab = yv[:, Y_AB, :]
        LO, HI = slice(64, 96), slice(96, 128)

        def decay_dve(dve):
            barrier(dve, "l2_q")
            dve.wait_ge(dnc_loaded, 16)
            do = Do(dve, st_dec, "dve")
            do("shifted", nc.vector.tensor_scalar(gv, ab, par("dt_bias"), None, ALU.add))
            do.own()
            softplus_dve(do, gv, gt1, gt2, gt3, gsp)
            do.own()
            do.wait("act", "ea")
            do("scale", nc.vector.tensor_scalar(gsp, gsp, ea, -1.0, ALU.mult, ALU.mult))
            do.wait("act", "tanh_b")
            do.own()
            do("half_b", nc.vector.tensor_scalar(gt3[HI, :], gt3[HI, :], 1.0, 0.5, ALU.add, ALU.mult))
            do.own()
            do("beta", nc.vector.tensor_copy(gsp[HI, :], gt3[HI, :]))
            do.wait("act", "glk")
            d4 = lambda v: v.rearrange("p (t d h) -> p d t h", t=4, d=2)
            c4 = lambda v: v.rearrange("p (d t h) -> p d t h", t=4, d=2)
            do("sub", nc.vector.tensor_tensor(c4(egl), d4(gl), c4(gcum), ALU.subtract))
            do.wait("act", "eg_exp")
            do("beg", nc.vector.tensor_tensor(c4(beg), d4(bT), c4(eg), ALU.mult))
            do.end()

        def decay_act(act):
            barrier(act, "l2_q")
            do = Do(act, st_dec, "act")
            softplus_act(do, gt1)
            do("ea", nc.scalar.activation(ea, par("a_log"), ACT.Exp))
            do.wait("dve", "sp_out")
            do("tanh_b", nc.scalar.activation(gt3[HI, :], ab[HI, :], ACT.Tanh, scale=0.5))
            do.wait("pe", "turned")
            tv = bank(4).rearrange("p (t n) -> p t n", n=P)
            g16 = lambda v: v.rearrange("p (t n) -> p t n", n=16)
            do("gk", nc.scalar.activation(g16(gT), tv[:, :, 64:80], ACT.Copy))
            do("bk", nc.scalar.activation(g16(bT), tv[:, :, 96:112], ACT.Copy))
            do.wait("pe", "cums")
            do("cumk", nc.scalar.activation(gcum, bank(5, 0, 64), ACT.Copy))
            do("glk", nc.scalar.activation(gl, bank(5, 64, 64), ACT.Copy))
            do.wait("dve", "sub")
            do("egl_exp", nc.scalar.activation(egl, egl, ACT.Exp))
            do("eg_exp", nc.scalar.activation(eg, bank(5, 0, 64), ACT.Exp))
            do("chunk_exp", nc.scalar.activation(egls, bank(5, 128, 128), ACT.Exp))
            do.end()

        def decay_pe(pe):
            do = Do(pe, st_dec, "pe")
            do.wait("dve", "beta")
            for t in range(4):
                last = nc.tensor.transpose(bank(4, t * P, P), gsp[:, t * P:(t + 1) * P], ident)
            do("turned", last)
            do.wait("act", "gk")
            g4 = gT.rearrange("p (t d h) -> p d t h", t=4, d=2)
            for d, m in enumerate(("le", "ge")):
                nc.tensor.matmul(bank(5, 32 * d, 32).rearrange("p (t h) -> p t h", t=4), dcon(m), g4[:, d, :, :], start=True, stop=True)
            nc.tensor.matmul(bank(5, 64, 64), dcon("chunk"), gT, start=True, stop=True)
            nc.tensor.matmul(bank(5, 128, 64), dcon("half0"), gT, start=True, stop=True)
            do("cums", nc.tensor.matmul(bank(5, 192, 64), dcon("half1"), gT, start=True, stop=True))
            do.end()

        def of_head(v, h):
            return v.rearrange("p (u h) -> p u h", h=BC)[:, :, bass.ds(h, 1)]

        def spread(v, d, n=4):
            return v[:, d * n:(d + 1) * n, :].to_broadcast([P, n, P])

        def over_tiles(m, n=4):
            return m[:, None, :].to_broadcast([P, n, P])

        def where(s, d):
            base, r = (2, s) if s < 4 else (0, s - 4)
            r = r if d == 0 else 3 - r
            t = base + r // 2
            return d * 4 + t, t, 64 * (r % 2)

        def two(b):
            return ps[:, b:b + 2, :].rearrange("p b (u n) -> p (b u) n", n=P)

        def dn_dve(dve):
            barrier(dve, "decay")

            def head(h):
                do = Do(dve, st_dn, "dve", h)
                g3 = gT.rearrange("p (t n) -> p t n", n=16)
                b3 = bT.rearrange("p (t n) -> p t n", n=16)
                gsel = lambda v, d: v[:, :, bass.ds(h + d * 8, 1)].to_broadcast([P, 4, P])
                gc = of_head(gcum, h)
                for d, m in enumerate(("le", "ge")):
                    do(f"rg{d}", nc.vector.tensor_tensor(rg[:, 4 * d:4 * d + 4, :], over_tiles(dcon(m)), gsel(g3, d), ALU.mult))
                do.wait("pe", "rows")
                for d in range(2):
                    do(f"diff{d}", nc.vector.tensor_tensor(dec[:, 4 * d:4 * d + 4, :], bank(2 + d).rearrange("p (t n) -> p t n", n=P), spread(gc, d), ALU.subtract))
                do.wait("act", "dec_t")
                for d, m in enumerate(("le", "ge")):
                    do(f"tmask{d}", nc.vector.tensor_tensor(att[:, 2 * d:2 * d + 2, :], att[:, 2 * d:2 * d + 2, :], over_tiles(dcon(m), 2), ALU.mult))
                do.wait("pe", "gram")
                do.own()
                for d in range(2):
                    do(f"att{d}", nc.vector.tensor_tensor(att[:, 2 * d:2 * d + 2, :], att[:, 2 * d:2 * d + 2, :],
                                                          bank(5, 0, 256).rearrange("p (t n) -> p t n", n=P), ALU.mult))
                do.wait("act", "dec")
                for d, m in enumerate(("gt", "lt")):
                    do(f"smask{d}", nc.vector.tensor_tensor(dec[:, 4 * d:4 * d + 4, :], dec[:, 4 * d:4 * d + 4, :], over_tiles(dcon(m)), ALU.mult))
                for d in range(2):
                    do(f"gb{d}", nc.vector.tensor_tensor(mb[:, 4 * d:4 * d + 4, :], bank(4).rearrange("p (t n) -> p t n", n=P), gsel(b3, d), ALU.mult))
                do.own()
                do("m", nc.vector.tensor_tensor(mb, mb, dec, ALU.mult))
                do.own()
                for d, m in enumerate(("level", "level_t")):
                    do(f"l0{d}", nc.vector.tensor_tensor(xb[:, 4 * d:4 * d + 4, :], mb[:, 4 * d:4 * d + 4, :], over_tiles(dcon(m)), ALU.mult))
                do.own()
                do("x", nc.vector.scalar_tensor_tensor(out=xb, in0=xb, scalar=-1.0, in1=over_tiles(ident, NU), op0=ALU.mult, op1=ALU.add))
                do.wait("act", "mt")
                for d, m in enumerate(("level_t", "level")):
                    do(f"l0t{d}", nc.vector.tensor_tensor(xt[:, 4 * d:4 * d + 4, :], mt[:, 4 * d:4 * d + 4, :], over_tiles(dcon(m)), ALU.mult))
                do.own()
                do("xt", nc.vector.scalar_tensor_tensor(out=xt, in0=xt, scalar=-1.0, in1=over_tiles(ident, NU), op0=ALU.mult, op1=ALU.add))

                def paired(l, d):
                    do(f"a{l}{d}", nc.vector.tensor_tensor(atl[:, 4 * d:4 * d + 4, :], mt[:, 4 * d:4 * d + 4, :], over_tiles(dcon(("level_t", "level")[d], l)), ALU.mult))

                for d in range(2):
                    paired(1, d)
                for d in range(2):
                    do(f"vb{d}", nc.vector.tensor_tensor(vb[:, 4 * d:4 * d + 4, :], vtm, gsel(b3, d), ALU.mult))
                for d in range(2):
                    do(f"ke{d}", nc.vector.tensor_tensor(kbe[:, 4 * d:4 * d + 4, :], ktm, spread(of_head(beg, h), d), ALU.mult))
                do("s0", nc.vector.memset(state, 0.0))
                for l in LV:
                    if l in INNER:
                        for d in range(2):
                            do.wait("pe", f"p{l}{d}")
                            paired(l + 1, d)
                    else:
                        do.own()
                        for d in range(2):
                            do(f"kd{d}", nc.vector.tensor_tensor(kdec[:, 4 * d:4 * d + 4, :], ktm, spread(of_head(egl, h), d), ALU.mult))
                    for d in range(2):
                        units = slice(4 * d, 4 * d + 4)
                        if l in INNER:
                            do.wait("pe", f"x{l}{d}")
                            do(f"x{l}{d}", nc.vector.tensor_tensor(xb[:, units, :], xb[:, units, :], two(2)[:, units, :], ALU.subtract))
                        do.wait("pe", f"xt{l}{d}")
                        do(f"xt{l}{d}", nc.vector.tensor_tensor(xt[:, units, :], xt[:, units, :], two(6)[:, units, :], ALU.subtract))
                do.wait("pe", "w")
                do("w", nc.vector.tensor_copy(wt, two(6)))
                do.wait("act", "u")
                ego = of_head(eg, h)
                e5 = egls.rearrange("p (f t d h) -> p f t d h", f=2, t=4, d=2)
                for s in range(8):
                    at = [where(s, d) for d in range(2)]
                    for d, (u, t, p0) in enumerate(at):
                        rows = slice(p0, p0 + 64)
                        do.wait("pe", f"ws{s}{d}")
                        do(f"vn{s}{d}", nc.vector.tensor_tensor(vnew[rows, d, :], ub[rows, u, :], ps[rows, 2 + d, 0:P], ALU.subtract))
                    for d, (u, t, p0) in enumerate(at):
                        do.wait("pe", f"su{s}{d}")
                        do(f"st{s}{d}", nc.vector.scalar_tensor_tensor(
                            out=state[:, d, :], in0=state[:, d, :], scalar=e5[:, p0 // 64, t, d, bass.ds(h, 1)], in1=bank(4 + d, 0, P), op0=ALU.mult, op1=ALU.add))
                    if s < 4:
                        continue
                    for d, (u, t, p0) in enumerate(at):
                        rows = slice(p0, p0 + 64)
                        do.wait("pe", f"oa{s}{d}")
                        do(f"oi{s}{d}", nc.vector.tensor_scalar((ob0, ob1)[d][rows, t, :], ps[rows, 6 + d, 0:P], ego[rows, u, :], None, ALU.mult))
                    do.own()
                    for d, (u, t, p0) in enumerate(at):
                        rows = slice(p0, p0 + 64)
                        ob = (ob0, ob1)[d]
                        do(f"o{s}{d}", nc.vector.tensor_tensor(ob[rows, t, :], ob[rows, t, :], ps[rows, 6 + d, P:2 * P], ALU.add))
                do.own()
                do("osum", nc.vector.tensor_tensor(ob0, ob0, ob1, ALU.add))
                do.wait("pe", "ot")
                do("ot", nc.vector.tensor_scalar(lv[:, h + L_Q, :], bank(6, 0, T), 1.0, None, ALU.mult))
                do.end()
            rounds(dve, BC, head)

        def dn_act(act):
            barrier(act, "decay")

            def head(h):
                do = Do(act, st_dn, "act", h)
                if not (isinstance(h, int) and h == 0):
                    do.wait("pe", "ot", h - 1)
                do("k", nc.scalar.activation(kst, yv[:, h + Y_K, :], ACT.Copy))
                do("v", nc.scalar.activation(vst, yv[:, h + Y_V, :], ACT.Copy, scale=0.5))
                do("q", nc.scalar.activation(qst, lv[:, h + L_Q, :], ACT.Copy))
                do.wait("pe", "turned")
                do("ktm", nc.scalar.activation(ktm, bank(0).rearrange("p (t n) -> p t n", n=P), ACT.Copy))
                do("vtm", nc.scalar.activation(vtm, bank(1).rearrange("p (t n) -> p t n", n=P), ACT.Copy))
                do.wait("dve", "diff1")
                att4 = att.rearrange("p (d t) n -> p d t n", d=2)
                lat = dec.rearrange("p (d t) n -> p d t n", d=2)[:, :, 0:2, :]
                do("relu_t", nc.scalar.activation(att4, lat, ACT.Relu, scale=-1.0))
                do("relu", nc.scalar.activation(mt, dec, ACT.Relu))
                do.own()
                do("dec", nc.scalar.activation(dec, mt, ACT.Exp, scale=-1.0))
                do("dec_t", nc.scalar.activation(att, att, ACT.Exp, scale=-1.0))
                do.wait("pe", "mt")
                do("mt", nc.scalar.activation(mt, two(6), ACT.Copy))
                for l in LV:
                    for d in range(2):
                        units = slice(4 * d, 4 * d + 4)
                        do.wait("pe", f"p{l}{d}")
                        do(f"p{l}{d}", nc.scalar.activation(pbuf[:, units, :], two(0)[:, units, :], ACT.Copy))
                do.wait("pe", "u")
                do("u", nc.scalar.activation(ub, two(0), ACT.Copy))
                do.end()
            rounds(act, BC, head)

        def dn_pe(pe):
            barrier(pe, "decay")

            def head(h):
                do = Do(pe, st_dn, "pe", h)
                do.wait("act", "q")
                for t in range(4):
                    nc.tensor.transpose(bank(0, t * P, P), kst[:, t * P:(t + 1) * P], ident)
                for t in range(4):
                    last = nc.tensor.transpose(bank(1, t * P, P), vst[:, t * P:(t + 1) * P], ident)
                do("turned", last)
                do.wait("dve", "rg1")
                for d in range(2):
                    last = nc.tensor.matmul(bank(2 + d), ones, rg[:, 4 * d:4 * d + 4, :].rearrange("p u n -> p (u n)"), start=True, stop=True)
                do("rows", last)
                for t in range(4):
                    nc.tensor.matmul(bank(4, t * P, P), kst[:, t * P:(t + 1) * P], kst[:, t * P:(t + 1) * P], start=True, stop=True)
                for t in range(2):
                    last = nc.tensor.matmul(bank(5, t * P, P), kst[:, t * P:(t + 1) * P], qst[:, t * P:(t + 1) * P], start=True, stop=True)
                do("gram", last)
                do.wait("dve", "m")
                for u in range(NU):
                    last = nc.tensor.transpose(two(6)[:, u, :], mb[:, u, :], ident)
                do("mt", last)
                for l in LV:
                    for d in range(2):
                        do.wait("dve", f"a{l}{d}")
                        if l > 1:
                            do.wait("dve", f"xt{l - 1}{d}")
                        for u in range(4 * d, 4 * d + 4):
                            last = nc.tensor.matmul(two(0)[:, u, :], atl[:, u, :], xb[:, u, :], start=True, stop=True)
                        do(f"p{l}{d}", last)
                    for d in range(2):
                        do.wait("act", f"p{l}{d}")
                        if l in INNER:
                            for u in range(4 * d, 4 * d + 4):
                                last = nc.tensor.matmul(two(2)[:, u, :], xt[:, u, :], pbuf[:, u, :], start=True, stop=True)
                            do(f"x{l}{d}", last)
                        for u in range(4 * d, 4 * d + 4):
                            last = nc.tensor.matmul(two(6)[:, u, :], pbuf[:, u, :], xt[:, u, :], start=True, stop=True)
                        do(f"xt{l}{d}", last)
                do.wait("dve", f"xt{LV[-1]}1")
                for u in range(NU):
                    last = nc.tensor.matmul(two(0)[:, u, :], xt[:, u, :], vb[:, u, :], start=True, stop=True)
                do("u", last)
                for u in range(NU):
                    last = nc.tensor.matmul(two(6)[:, u, :], kbe[:, u, :], xt[:, u, :], start=True, stop=True)
                do("w", last)
                do.wait("dve", "w")
                do.wait("act", "u")

                def reads_state(s, d):
                    u, t, p0 = where(s, d)
                    rows = slice(p0, p0 + 64)
                    if s:
                        do.wait("dve", f"st{s - 1}{d}")
                    do(f"ws{s}{d}", nc.tensor.matmul(ps[rows, 2 + d, 0:P], wt[:, u, rows], state[:, d, :], start=True, stop=True))
                    if s >= 4:
                        if s > 4:
                            do.wait("dve", f"o{s - 1}{d}")
                        nc.tensor.matmul(ps[rows, 6 + d, 0:P], qst[:, t * P + p0:t * P + p0 + 64], state[:, d, :], start=True, stop=True)

                def from_new(s, d):
                    u, t, p0 = where(s, d)
                    rows = slice(p0, p0 + 64)
                    do.wait("dve", f"vn{s}{d}")
                    do(f"su{s}{d}", nc.tensor.matmul(bank(4 + d, 0, P), kdec[rows, u, :], vnew[rows, d, :], start=True, stop=True))
                    if s >= 4:
                        do(f"oa{s}{d}", nc.tensor.matmul(ps[rows, 6 + d, P:2 * P], att[rows, 2 * d + t, rows], vnew[rows, d, :], start=True, stop=True))
                for s in range(8):
                    for d in range(2):
                        reads_state(s, d)
                    for d in range(2):
                        from_new(s, d)
                do.wait("dve", "osum")
                for t in range(NT):
                    last = nc.tensor.transpose(bank(6, t * P, P), ob0[:, t, :], ident)
                do("ot", last)
                do.end()
            rounds(pe, BC, head)

        oflat = cut(L_AT + L_Q * T, BC * T)
        ov = lv[:, L_Q:L_Q + BC, :]
        zv = lv[:, L_Z:L_Z + BC, :]

        def dno_act(act):
            barrier(act, "dn")
            for it in range(2):
                do = Do(act, st_on, "act", it)
                do("squares", nc.scalar.activation(osq, oflat[:, it * 1024:(it + 1) * 1024], ACT.Square))
                do.wait("pe", "sums1")
                if it:
                    do.wait("dve", "scaled3", it - 1)
                do("root", nc.scalar.activation(oroot, ps[:, 4:6, :].rearrange("p b n -> p (b n)"), ACT.Sqrt, bias=par("eps"), scale=1.0 / P))
                do.end()
            do = Do(act, st_og, "act")
            do("tanh", nc.scalar.activation(og, zv, ACT.Tanh, scale=0.5))
            do.end()

        def dno_pe(pe):
            for it in range(2):
                do = Do(pe, st_on, "pe", it)
                do.wait("act", "squares")
                do("sums0", nc.tensor.matmul(bank(4), ones, osq[:, 0:512], start=True, stop=True))
                do("sums1", nc.tensor.matmul(bank(5), ones, osq[:, 512:1024], start=True, stop=True))
                do.end()

        def dno_dve(dve):
            for it in range(2):
                do = Do(dve, st_on, "dve", it)
                do.wait("act", "root")
                do("inv", nc.vector.reciprocal(oroot, oroot))
                do.own()
                for c in range(4):
                    v = ov[:, it * 4 + c, :]
                    do(f"scaled{c}", nc.vector.scalar_tensor_tensor(out=v, in0=v, scalar=par("dn_norm"), in1=oroot[:, c * T:(c + 1) * T], op0=ALU.mult, op1=ALU.mult))
                do.end()
            do = Do(dve, st_og, "dve")
            do.wait("act", "tanh")
            do("silu", nc.vector.scalar_tensor_tensor(out=og, in0=og, scalar=1.0, in1=zv, op0=ALU.add, op1=ALU.mult))
            do.own()
            barrier(dve, "dn_out")
            do("out", nc.vector.scalar_tensor_tensor(out=ov, in0=og, scalar=0.5, in1=ov, op0=ALU.mult, op1=ALU.mult))
            do.end()

        def merge2_pe(pe):
            barrier(pe, "dn_gate")

            def part(idx, slot, loads, i, u):
                y = (my, ov)[u % 2]
                pe.wait_ge(landed[slot], loads * 16)
                if not (isinstance(idx, int) and idx < SLOTS):
                    pe.wait_ge(st_merge2.steps["act"].sem, st_merge2.steps["act"].at("y", idx - SLOTS))
                for k in range(DC):
                    nc.tensor.matmul(bank(slot, 0, T), ring[:, slot, k * P:(k + 1) * P], hcat[:, 0, k, :], start=(k == 0), stop=(k == DC - 1))
                for k in range(BC):
                    last = nc.tensor.matmul(bank(4 + slot, 0, T), ring[:, slot, D + k * P:D + (k + 1) * P], y[:, k, :],
                                            start=(k == 0), stop=(k == BC - 1))
                last.then_inc(weights_used, 1)
            streams["merge2"].each(pe, part)
            barrier(pe, "merge2")
            gemm(pe, "out2", DC, lambda k: merged2[:, k, :])

        def merge2_act(act):
            barrier(act, "dn_gate")

            def part(idx, slot, loads, i, u):
                do = Do(act, st_merge2, "act", idx)
                act.wait_ge(weights_used, idx + (streams["merge2"].first + 1))
                if not (isinstance(idx, int) and idx < 2):
                    do.wait("dve", "summed", idx - 2)
                do("gate", nc.scalar.activation(m2th[:, u % 2, :], bank(slot, 0, T), ACT.Tanh, scale=0.5))
                do("y", nc.scalar.activation(m2tm[:, u % 2, :], bank(4 + slot, 0, T), ACT.Copy, scale=0.5))
                do.end()
            streams["merge2"].each(act, part)

        def merge2_dve(dve):
            barrier(dve, "dn_gate")

            def part(idx, slot, loads, i, u):
                do = Do(dve, st_merge2, "dve", idx)
                do.wait("act", "y")
                d = merged2[:, i * 2 + u // 2, :]
                dst = d if u % 2 == 0 else m2tm[:, 1, :]
                do("scaled", nc.vector.scalar_tensor_tensor(out=dst, in0=m2th[:, u % 2, :], scalar=1.0, in1=m2tm[:, u % 2, :], op0=ALU.add, op1=ALU.mult))
                do.own()
                do("summed", nc.vector.tensor_copy(gains[:, 48:49], par("eps")) if u % 2 == 0 else nc.vector.tensor_tensor(d, d, dst, ALU.add))
                do.end()
            streams["merge2"].each(dve, part)
            add_block(dve, "out2", lambda i: xc[:, i, :], scalar=lambda i: modv[:, i + 2 * DC, 0:1])

        def choose_act(act):
            barrier(act, "out2")
            norm_act(act, st_np, 0, xc, psq, proot, bank(4, 0, T), T, 1.0 / D)
            barrier(act, "norm_p")
            do = Do(act, st_sh2, "act")
            for c in range(DC):
                do(f"shift{c}", nc.scalar.activation(hp[:, c, :], hp[:, c, :], ACT.Identity, bias=modv[:, 3 * DC + c, 0:1]))
            do.end()
            copy_out(act, "peer_q", lambda i: pq[:, i, :], T)
            do = Do(act, st_sc, "act")
            for b in range(8):
                do.wait("pe", f"s{b}")
                do(f"k{b}", nc.scalar.activation(scores[:, 4 * b:4 * b + 4, :], bank(b).rearrange("p (r n) -> p r n", n=P), ACT.Copy))
            do.end()

            for r in range(DC // LANES):
                do = Do(act, st_cand, "act", r)
                do.wait("dve", f"neg{LANES - 1}")
                for l in range(LANES):
                    do(f"exp{l}", nc.scalar.activation(cexp[:, l, :], cand[:, l, :], ACT.Exp, bias=csum[:, 0, l:l + 1]))
                do.end()
            do = Do(act, st_mt, "act")
            do.wait("pe", "idx")
            do("idx", nc.scalar.activation(idxt, bank(0).rearrange("p (a b) -> p a b", b=T), ACT.Copy))
            for b in range(8):
                do.wait("pe", f"m{b}")
                do(f"m{b}", nc.scalar.activation(mixt[:, 2 * b:2 * b + 2, :], bank((b + 1) % 8).rearrange("p (a t) -> p a t", t=T), ACT.Copy))
            do.end()

        def choose_pe(pe):
            barrier(pe, "out2")
            norm_pe(pe, st_np, 0, psq, bank(4, 0, T), DC)
            barrier(pe, "norm_p", "shift2")
            gemm(pe, "peer_q", DC, lambda k: hp[:, k, :])
            barrier(pe, "peer_q")
            do = Do(pe, st_sc, "pe")
            for b in range(8):
                for j in range(4):
                    t, c = divmod(4 * b + j, DC)
                    last = nc.tensor.matmul(bank(b, j * P, P), pq[:, c, t * P:(t + 1) * P], misc[:, 512 + (c % 2) * P:512 + (c % 2 + 1) * P],
                                            start=True, stop=True)
                do(f"s{b}", last)
            do.end()
            barrier(pe, "scores", "cand")
            do = Do(pe, st_mt, "pe")
            do.wait("dve", "idx1")
            for half_ in range(2):
                for t in range(NT):
                    last = nc.tensor.transpose(bank(0, half_ * T + t * P, P), idxp[:, 2 * t + half_, :], ident)
            do("idx", last)
            for b in range(8):
                if b == 7:
                    do.wait("act", "idx")
                for j in range(2):
                    for t in range(NT):
                        last = nc.tensor.transpose(bank((b + 1) % 8, j * T + t * P, P), mix[:, t, 2 * b + j, :], ident)
                do(f"m{b}", last)
            do.end()

        def choose_dve(dve):
            barrier(dve, "out2")
            norm_dve(dve, st_np, 0, lambda c: xc[:, c, :], lambda c: hp[:, c, :], proot, lambda c: gain2v[:, c:c + 1], DC)
            barrier(dve, "scores")

            each_lane = range(LANES)

            def top(r):
                do = Do(dve, st_top, "dve", r)

                def gate(k):
                    do.own()
                    do(f"gate{k}", nc.vector.memset(gated, 0.0))
                for l in each_lane:
                    do(f"row{l}", nc.vector.tensor_copy(krow[:, l, :], scores[:, r * LANES + l, :]))
                gate(0)
                for l in each_lane:
                    do(f"m0_{l}", nc.vector.max(kval[:, l, 0:8], krow[:, l, :]))
                gate(1)
                for l in each_lane:
                    do(f"i0_{l}", nc.vector.max_index(kidx[:, l, 0:8], kval[:, l, 0:8], krow[:, l, :]))
                for l in each_lane:
                    do(f"rest{l}", nc.vector.match_replace(krest[:, l, :], kval[:, l, 0:8], krow[:, l, :], -BIG))
                gate(2)
                for l in each_lane:
                    do(f"m1_{l}", nc.vector.max(kval[:, l, 8:16], krest[:, l, :]))
                gate(3)
                for l in each_lane:
                    do(f"i1_{l}", nc.vector.max_index(kidx[:, l, 8:16], kval[:, l, 8:16], krest[:, l, :]))
                for l in each_lane:
                    do(f"values{l}", nc.vector.tensor_copy(topv[:, r * LANES + l, :], kval[:, l, :]))
                do.own()
                for l in each_lane:
                    do(f"indices{l}", nc.vector.tensor_copy(topi[:, r * LANES + l, :], kidx[:, l, :]))
                do.own()
                do.end()
            rounds(dve, 2 * DC // LANES, top)
            S["top"].finished(dve)

            for r in range(DC // LANES):
                do = Do(dve, st_cand, "dve", r)
                head = [r * LANES + l for l in each_lane]
                for l in each_lane:
                    do(f"sum{l}", nc.vector.tensor_tensor(
                        cand[:, l, :].rearrange("p (a b) -> p a b", b=TOPK), topv[:, 2 * head[l], :][:, :, None].to_broadcast([P, TOPK, TOPK]),
                        topv[:, 2 * head[l] + 1, :][:, None, :].to_broadcast([P, TOPK, TOPK]), ALU.add))
                do.own()
                for l in each_lane:
                    do(f"m0_{l}", nc.vector.max(c8[:, l, :], cand[:, l, :]))
                do.own()
                for l in each_lane:
                    do(f"r0_{l}", nc.vector.match_replace(crest[:, l, :], c8[:, l, :], cand[:, l, :], -BIG))
                for l in each_lane:
                    do(f"neg{l}", nc.vector.tensor_scalar(csum[:, 0, l:l + 1], c8[:, l, 0:1], -1.0, None, ALU.mult))
                do.own()
                for l in each_lane:
                    do(f"m1_{l}", nc.vector.max(c8[:, l, :], crest[:, l, :]))
                do.own()
                for l in each_lane:
                    do(f"r1_{l}", nc.vector.match_replace(crest[:, l, :], c8[:, l, :], crest[:, l, :], -BIG))
                do.own()
                for l in each_lane:
                    do(f"chosen{l}", nc.vector.tensor_tensor(crest[:, l, :], crest[:, l, :], cand[:, l, :], ALU.is_lt))
                do.wait("act", f"exp{LANES - 1}")
                do.own()
                for l in each_lane:
                    do(f"masked{l}", nc.vector.tensor_tensor(cexp[:, l, :], cexp[:, l, :], crest[:, l, :], ALU.mult))
                do.own()
                for l in each_lane:
                    do(f"total{l}", nc.vector.tensor_reduce(csum[:, 1, l:l + 1], cexp[:, l, :], AX_X, ALU.add))
                do.own()
                do("inv", nc.vector.reciprocal(csum[:, 1, :], csum[:, 1, :]))
                do.own()
                for l in each_lane:
                    t, h = divmod(head[l], 8)
                    do(f"out{l}", nc.vector.tensor_scalar(mix5[:, t, :, h, :], cexp[:, l, :].rearrange("p (a b) -> p a b", b=TOPK), csum[:, 1, l:l + 1], None, ALU.mult))
                do.own()
                do.end()
            do = Do(dve, st_mt, "dve")
            for t in range(NT):
                do(f"idx{t}", nc.vector.tensor_copy(
                    idxp[:, 2 * t:2 * t + 2, :].rearrange("p q (h k) -> p q h k", k=TOPK),
                    topi[:, DC * t:DC * t + DC, :].rearrange("p (h q) k -> p q h k", q=2)))
            do.end()

        def by_groups(eng, q, body):
            if q == 0:
                body(0)
            with eng.Fori(4 * q + (q == 0), 4 * q + 4) as g:
                body(g)

        def later(r, n):
            return not (isinstance(r, int) and r < n)

        def expw_dve(dve):
            barrier(dve, "mix")
            dve.wait_ge(peer_loaded, 16)

            def group(g):
                for u in range(4):
                    r = g * 4 + u
                    bd, hot1, hot2 = hots[u]
                    if later(r, 4):
                        dve.wait_ge(weights_made, r - 3)
                    mt4 = mixtf.rearrange("p (a t) -> p t a", t=T)[:, bass.ds(r * NB4, NB4), :]
                    nc.vector.tensor_tensor(
                        bd.rearrange("p t (h a) -> p t h a", a=TOPK), same_head.rearrange("p (h a) -> p h a", a=TOPK)[:, None, :, :].to_broadcast([P, NB4, 8, TOPK]),
                        mt4[:, :, None, :].to_broadcast([P, NB4, 8, TOPK]), ALU.mult)
                    for k, hot in enumerate((hot1, hot2)):
                        last = nc.vector.tensor_tensor(hot, iota[:, None, :].to_broadcast([P, NB4, P]),
                                                       idxt[:, k, bass.ds(r * NB4, NB4)].rearrange("p (t o) -> p t o", o=1).to_broadcast([P, NB4, P]), ALU.is_equal)
                    last.then_inc(hot_made, 1)
            for q in range(4):
                by_groups(dve, q, group)

        def expw_pe(pe):
            barrier(pe, "mix")

            def group(g):
                for pair in range(2):
                    for u in (2 * pair, 2 * pair + 1):
                        r = g * 4 + u
                        pe.wait_ge(hot_made, r + 1)
                        if later(r, 2):
                            pe.wait_ge(spread_kept, r - 1)
                        bd, hot1, hot2 = hots[u]
                        for n in range(NB4):
                            last = nc.tensor.matmul(bank(u % 2, n * P, P), bd[:, n, :], hot2[:, n, :], start=True, stop=True)
                        last.then_inc(spread_made, 1)
                    for u in (2 * pair, 2 * pair + 1):
                        r = g * 4 + u
                        pe.wait_ge(spread_kept, r + 1)
                        if later(r, 2):
                            pe.wait_ge(weights_kept, r - 1)
                        for n in range(NB4):
                            last = nc.tensor.matmul(bank(2 + u % 2, n * P, P), rbuf[u % 2][:, n, :], hots[u][1][:, n, :], start=True, stop=True)
                        last.then_inc(weights_made, 1)
            for q in range(4):
                by_groups(pe, q, group)

        def expw_act(act):
            for q in range(4):
                if q >= 2:
                    act.wait_ge(w_stored[q % 2], 16)

                def group(g, q=q):
                    for pair in range(2):
                        for u in (2 * pair, 2 * pair + 1):
                            r = g * 4 + u
                            act.wait_ge(spread_made, r + 1)
                            if later(r, 2):
                                act.wait_ge(weights_made, r - 1)
                            nc.scalar.activation(rbuf[u % 2], bank(u % 2).rearrange("p (t n) -> p t n", n=P), ACT.Copy).then_inc(spread_kept, 1)
                        for u in (2 * pair, 2 * pair + 1):
                            r = g * 4 + u
                            act.wait_ge(weights_made, r + 1)
                            kept_to = ewf[q % 2].rearrange("p (i t) -> p t i", t=64)[:, bass.ds(r * NB4 - 64 * q, NB4), :]
                            quarter_copy(act, kept_to, bank(2 + u % 2).rearrange("p (t i) -> p t i", i=P))
                by_groups(act, q, group)

        def quarter_copy(act, out, src):
            nc.scalar.activation(out, src, ACT.Copy).then_inc(weights_kept, 1)

        def pairs(eng, body):
            for g in range(2):
                body(g, g)
            with eng.Fori(1, NG // 2 - 1) as i:
                for k in range(2):
                    body(i * 2 + k, k)
            for g in range(NG - 2, NG):
                body(g, g % 2)

        def is_last(g, n=1):
            return isinstance(g, int) and g >= NG - n

        def base(g):
            return g * (2 * PER_PHASE) + PER_PHASE

        def v_base(g):
            return base(g) + (0 if is_last(g) else PER_PHASE)

        def three_products(out, weights, moving, k, n):
            for a, (wa, ma) in enumerate(((0, 0), (1, 0), (0, 1))):
                last = nc.tensor.matmul(out, weights(wa), moving(ma), start=(k == 0 and a == 0), stop=(k == n - 1 and a == 2))
            return last

        def take_piece(pe, p):
            pe.wait_ge(remainders, p + 1)

        def u_pe(pe, g, at):
            for s in range(GROUP):
                for j in range(4):
                    n = 4 * s + j
                    take_piece(pe, at + n)
                    if n == 0 and not (isinstance(g, int) and g == 0):
                        pe.wait_ge(gelu_made, g)
                    b = n % NPIECES
                    for k in range(4):
                        last = three_products(bank(s, 0, T), lambda a: piece[:, b, a, k * P:(k + 1) * P], lambda a: hp2[:, a, 4 * j + k, :], 4 * j + k, DC)
                    last.then_inc(pieces_used, 1)

        def experts_pe(pe):
            barrier(pe, "hp_split")
            u_pe(pe, 0, 0)

            def group(g, k):
                if not is_last(g):
                    u_pe(pe, g + 1, base(g))
                pe.wait_ge(gact_split, g + 1)
                for c in range(DC):
                    take_piece(pe, v_base(g) + c)
                    if not (isinstance(g, int) and g == 0 and c < 4):
                        pe.wait_ge(products_added, g * DC + (c - 3))
                    for s in range(GROUP):
                        last = three_products(bank(4 + c % 4, 0, T), lambda a: piece[:, c % NPIECES, a, s * P:(s + 1) * P],
                                              lambda a: gact[:, k, a, s, :], s, GROUP)
                    last.then_inc(pieces_used, 1)
            pairs(pe, group)

        def u_source(n):
            s, j = divmod(n, 4)
            return ring[:, s, j * PIECE:(j + 1) * PIECE]

        def v_source(c):
            return vslots[:, :, c * P:(c + 1) * P]

        def part_of(b, a, like_v):
            v = piece[:, b, a, :]
            return v.rearrange("p (s n) -> p s n", n=P) if like_v else v

        def round_piece(act, p, n, source, like_v=False):
            if not (isinstance(p, int) and p < NPIECES):
                act.wait_ge(pieces_used, p - (NPIECES - 1))
            nc.scalar.activation(part_of(n % NPIECES, 0, like_v), source, ACT.Copy).then_inc(rounded, 1)

        def u_act(act, g, at):
            for n in range(PER_PHASE):
                if n % 4 == 0:
                    act.wait_ge(u_landed[n // 4], g * 16 + 16)
                round_piece(act, at + n, n, u_source(n))

        def gelu_act(act, g, end):
            act.wait_ge(pieces_used, end)
            if not (isinstance(g, int) and g == 0):
                act.wait_ge(gact_split, g)
            nc.scalar.activation(gel, ps[:, 0:4, 0:T], ACT.Gelu).then_inc(gelu_made, 1)

        def round_gact(act, g, k):
            act.wait_ge(weighted, g + 1)
            nc.scalar.activation(gact[:, k, 0, :, :], gel, ACT.Copy).then_inc(gact_rounded, 1)

        def experts_act(act):
            act.wait_ge(weights_kept, NR)
            for k in range(2):
                act.wait_ge(w_stored[k], 32)
            do = Do(act, st_hps, "act")
            do("rounded", nc.scalar.activation(hp2[:, 0, :, :], hp, ACT.Copy))
            do.end()
            u_act(act, 0, 0)
            gelu_act(act, 0, PER_PHASE)
            round_gact(act, 0, 0)

            def group(g, k):
                if not is_last(g):
                    u_act(act, g + 1, base(g))
                for c in range(DC):
                    if c == 0:
                        for s in range(GROUP):
                            act.wait_ge(v_landed[s], g * 16 + 16)
                    round_piece(act, v_base(g) + c, c, v_source(c), like_v=True)
                    if c == 3 and not is_last(g):
                        gelu_act(act, g + 1, v_base(g))
                    if c == 8 and not is_last(g):
                        round_gact(act, g + 1, 1 - k)
            pairs(act, group)

        def remainder(dve, p, n, source, like_v=False):
            dve.wait_ge(rounded, p + 1)
            b = n % NPIECES
            nc.vector.tensor_tensor(part_of(b, 1, like_v), source, part_of(b, 0, like_v).bitcast(F32), ALU.subtract).then_inc(remainders, 1)

        def weigh(dve, g, k):
            dve.wait_ge(wexp_landed[k], (g // 2) * 16 + 16 if isinstance(g, int) else (g - k) * 8 + 16)
            dve.wait_ge(gelu_made, g + 1)
            g4 = gel.rearrange("p s (q t) -> p q s t", t=64)
            nc.vector.tensor_tensor(g4, g4, wexp[k], ALU.mult).then_inc(weighted, 1)

        def split_gact(dve, g, k):
            dve.wait_ge(gact_rounded, g + 1)
            nc.vector.tensor_tensor(gact[:, k, 1, :, :], gel, gact[:, k, 0, :, :].bitcast(F32), ALU.subtract).then_inc(gact_split, 1)

        def add(dve, g, c, p):
            dve.wait_ge(pieces_used, p + 1)
            if not (isinstance(g, int) and g == 0):
                dve.wait_ge(products_added, g * DC + (c - DC + 1))
            nc.vector.tensor_tensor(yacc[:, c, :], yacc[:, c, :], bank(4 + c % 4, 0, T), ALU.add).then_inc(products_added, 1)

        LAG = 3

        def experts_dve(dve):
            dve.wait_ge(weights_kept, NR)
            for k in range(2):
                dve.wait_ge(w_stored[k], 32)
            do = Do(dve, st_hps, "dve")
            do.wait("act", "rounded")
            do("rest", nc.vector.tensor_tensor(hp2[:, 1, :, :], hp, hp2[:, 0, :, :].bitcast(F32), ALU.subtract))
            do.end()
            nc.vector.memset(yacc, 0.0).then_inc(zeroed, 1)
            for n in range(PER_PHASE):
                remainder(dve, n, n, u_source(n))
            weigh(dve, 0, 0)
            split_gact(dve, 0, 0)
            dve.wait_ge(zeroed, 1)

            def group(g, k):
                for n in range(0 if is_last(g) else PER_PHASE):
                    remainder(dve, base(g) + n, n, u_source(n))
                    if n < LAG and not (isinstance(g, int) and g == 0):
                        add(dve, g - 1, DC - LAG + n, v_base(g - 1) + (DC - LAG + n))
                for c in range(DC):
                    remainder(dve, v_base(g) + c, c, v_source(c), like_v=True)
                    if is_last(g) and c < LAG:
                        add(dve, g - 1, DC - LAG + c, v_base(g - 1) + (DC - LAG + c))
                    if c >= LAG:
                        add(dve, g, c - LAG, v_base(g) + (c - LAG))
                    if c == 6 and not is_last(g):
                        weigh(dve, g + 1, 1 - k)
                    if c == 11 and not is_last(g):
                        split_gact(dve, g + 1, 1 - k)
            pairs(dve, group)
            for c in range(DC - LAG, DC):
                add(dve, NG - 1, c, v_base(NG - 1) + c)

        def last_dve(dve):
            dve.wait_ge(products_added, NG * DC)
            do = Do(dve, st_res, "dve")
            for c in range(DC):
                do(f"r{c}", nc.vector.scalar_tensor_tensor(out=xc[:, c, :], in0=yacc[:, c, :], scalar=modv[:, 5 * DC + c, 0:1], in1=xc[:, c, :], op0=ALU.mult, op1=ALU.add))
            do.end()
            norm_dve(dve, st_nf, 0, lambda c: xc[:, c, :], lambda c: xc[:, c, :], froot, lambda c: par("final_norm", c), DC)

        def last_act(act):
            barrier(act, "residual")
            norm_act(act, st_nf, 0, xc, fsq, froot, bank(0, 0, T), T, 1.0 / D)

        def last_pe(pe):
            norm_pe(pe, st_nf, 0, fsq, bank(0, 0, T), DC)

        def experts_sp(sp):
            barrier(sp, "out2")
            sp.dma_start(cut(PC_AT, N_PEER_CONSTS), a["peer_consts"]).then_inc(peer_loaded, 16)

            def load_u(g, at=None):
                for s in range(GROUP):
                    if at is not None:
                        sp.wait_ge(remainders, at + (4 * s + 4))
                    sp.dma_start(ring[:, s, 0:D], a["u"][g * GROUP + s]).then_inc(u_landed[s], 16)

            def load_w(g, k):
                if not (isinstance(g, int) and g < 2):
                    sp.wait_ge(weighted, g - 1)
                sp.dma_start(wexp[k].rearrange("p q s t -> p q (s t)"),
                             a["experts"].rearrange("q j i t -> j q (i t)")[:, :, bass.ds(g * (GROUP * 64), GROUP * 64)]).then_inc(wexp_landed[k], 16)

            def load_v(g):
                for s in range(GROUP):
                    sp.dma_start(vslots[:, s, :], a["v"][g * GROUP + s]).then_inc(v_landed[s], 16)

            sp.wait_ge(weights_used, sum(n for _, n, _ in STREAMS))
            load_u(0)
            for q in range(4):
                sp.wait_ge(weights_kept, 16 * q + 16)
                sp.dma_start(a["experts"][q].rearrange("j i t -> j (i t)"), ewf[q % 2]).then_inc(w_stored[q % 2], 16)
            for k in range(2):
                sp.wait_ge(w_stored[k], 32)
            for g in range(2):
                load_w(g, g)
            barrier(sp, "hp_split")
            load_v(0)
            load_u(1, 0)

            def group(g, k):
                if not is_last(g, 2):
                    load_u(g + 2, base(g))
                    load_w(g + 2, k)
                if not is_last(g):
                    sp.wait_ge(remainders, v_base(g) + PER_PHASE)
                    load_v(g + 1)
            pairs(sp, group)

        def store_sp(sp):
            barrier(sp, "norm_f")
            sp.dma_start(a["out"], x[:, :]).then_inc(stored, 16)
            sp.wait_ge(stored, 16)

        @block.sync
        def _(sp):
            for dst, src in ((params[:, :], a["params"]), (consts[:, :], a["consts"]), (misc[:, :], a["misc"]),
                             (x[:, :], a["x"]), (pT, a["p"].rearrange("p (k t) -> p k t", t=T))):
                sp.dma_start(dst, src).then_inc(inputs_loaded, 16)
            sp.dma_start(silu1, a["cond"].rearrange("p (c n) -> p c n", c=2)).then_inc(cond_loaded, 16)
            for name, count, cols in STREAMS:
                s = streams[name]
                if name == "y":
                    barrier(sp, "x2")
                    sp.dma_start(hcat[:, 1, :, :], a["ctx"].rearrange("p (c t) -> p c t", t=T)).then_inc(ctx_loaded, 16)
                    sp.dma_start(silu2, a["cond"].rearrange("p (c n) -> p c n", c=2)).then_inc(cond_loaded, 16)
                if name in ("merge", "merge2"):
                    sp.wait_ge(mod_used, N_Z if name == "merge" else N_MOD)
                if name == "merge2":
                    barrier(sp, "y")
                    sp.dma_start(dnc, a["dn_consts"]).then_inc(dnc_loaded, 16)

                for at, n in ((0, count),) if name != "y" else ((0, count - SLOTS), (count - SLOTS, SLOTS)):
                    def load(idx, slot, loads, i, u, name=name, s=s, cols=cols, at=at):
                        idx = idx + at
                        if not (isinstance(idx, int) and s.first + idx < SLOTS):
                            sp.wait_ge(weights_used, idx + (s.first - SLOTS + 1))
                        sp.dma_start(ring[:, slot, 0:cols], a["w_" + name][idx]).then_inc(landed[slot], 16)
                        if name == "z":
                            load_mod(sp, idx, u)
                        if name == "y" and not (isinstance(idx, int) and idx >= N_MOD - N_Z):
                            load_mod(sp, idx + N_Z, u + N_Z)
                    Stream(s.first + at, n, cols).each(sp, load)
            experts_sp(sp)
            store_sp(sp)

        @block.tensor
        def _(pe):
            pre_pe(pe)
            n1_pe(pe)
            lru_pe(pe)
            qk_pe(pe)
            turn_pe(pe)
            cmp_pe(pe)
            nsa_pe(pe)
            fox_pe(pe)
            merge_pe(pe)
            out_pe(pe)
            n2_pe(pe)
            mla_pe(pe)
            conv_pe(pe)
            decay_pe(pe)
            dn_pe(pe)
            dno_pe(pe)
            merge2_pe(pe)
            choose_pe(pe)
            expw_pe(pe)
            experts_pe(pe)
            last_pe(pe)

        @block.scalar
        def _(act):
            pre_act(act)
            n1_act(act)
            lru_act(act)
            gates_act(act)
            qk_act(act)
            turn_act(act)
            cmp_act(act)
            nsa_act(act)
            fox_act(act)
            merge_act(act)
            out_act(act)
            n2_act(act)
            mla_act(act)
            conv_act(act)
            decay_act(act)
            dn_act(act)
            dno_act(act)
            merge2_act(act)
            choose_act(act)
            expw_act(act)
            experts_act(act)
            last_act(act)

        @block.vector
        def _(dve):
            pre_dve(dve)
            n1_dve(dve)
            lru_dve(dve)
            gates_dve(dve)
            qk_dve(dve)
            turn_dve(dve)
            cmp_dve(dve)
            nsa_dve(dve)
            fox_dve(dve)
            merge_dve(dve)
            out_dve(dve)
            n2_dve(dve)
            mla_dve(dve)
            conv_dve(dve)
            decay_dve(dve)
            dn_dve(dve)
            dno_dve(dve)
            merge2_dve(dve)
            choose_dve(dve)
            expw_dve(dve)
            experts_dve(dve)
            last_dve(dve)


def blocks(w):
    k, n = w.shape
    return w.reshape(k // P, P, n // P, P).transpose(2, 1, 0, 3).reshape(n // P, P, k)


def columns(v):
    return v.reshape(-1, P).T


def tokens_last(v):
    t, n = v.shape
    return v.T.reshape(n // P, P, t).transpose(1, 0, 2).reshape(P, -1)


def pad_to(v, n):
    out = np.zeros(v.shape[:-1] + (n,), np.float32)
    out[..., :v.shape[-1]] = v
    return out


def constants():
    i = np.arange(P)
    eye = np.eye(P)
    masked = BIG * (i[None, :] > i[:, None])
    t = np.arange(T)
    end = np.arange(NCMP) * 16 + 31
    cmp_mask = np.zeros((P, NT, 16))
    for tile in range(NT):
        cmp_mask[:, tile, :NCMP] = BIG * (end[None, :] > (i + tile * P)[:, None])
    freq = (10000.0 ** (-np.arange(0, 32, 2, dtype=np.float32) / np.float32(32))).astype(np.float32)
    rows, cols = (t // 64).astype(np.float32), (t % 64).astype(np.float32)
    ang = np.zeros((64, T), np.float32)
    for f in range(64):
        ang[f] = (rows if f < 32 else cols) * freq[f % 16]
    ang = np.concatenate([ang, ang])
    rot = np.zeros((P, P))
    for f in range(P):
        if f % 32 < 16:
            rot[f + 16, f] = -1
        else:
            rot[f - 16, f] = 1
    dup = np.zeros((P, P))
    dup[:64, :64] = dup[:64, 64:] = np.eye(64)
    duprot = np.zeros((P, P))
    duprot[:64, :64] = duprot[:64, 64:] = rot[:64, :64]
    c = np.concatenate([eye, np.ones((P, P)), masked, np.zeros((P, P)), masked, cmp_mask.reshape(P, -1),
                        i[:, None] <= i[None, :], np.cos(ang), np.sin(ang), rot, dup, duprot], 1)
    same = (i[:, None] // 64) == (i[None, :] // 64)
    r, s = i[:, None], i[None, :]
    level = [((r // (2 * b)) == (s // (2 * b))) & ((r // b) % 2 == 1) & ((s // b) % 2 == 0) for b in (1, 2, 4, 8, 16, 32)]
    dn = np.concatenate([same & (r <= s), same & (r >= s), same & (r < s), same & (r > s), same,
                         np.broadcast_to(r < 64, (P, P)), np.broadcast_to(r >= 64, (P, P))] + level + [m.T for m in level], 1)
    peer = np.concatenate([np.broadcast_to(s, (P, P)), (r // 16) == (s // 16)], 1)
    out = [v.astype(np.float32) for v in (c, dn, peer)]
    assert [v.shape[1] for v in out] == [N_CONSTS, N_DN_CONSTS, N_PEER_CONSTS]
    return out


def lay_out(v):
    v = {k: np.asarray(x) for k, x in v.items()}
    out = {}
    w, b = v["w_in"][0], v["b_in"][0]
    order = ("lru_x lru_gate nsa_q k_cmp v_cmp k_slc v_slc k_win v_win bgate nsa_gate fox_q fox_k fox_v fox_f fox_gate merge").split()
    size = (1024, 1024, 1024, 256, 256, 256, 256, 256, 256, 24, 1024, 1024, 1024, 1024, 8, 1024, 6144)
    at = dict(zip(order, np.concatenate([[0], np.cumsum(size)[:-1]]).tolist()))
    size = dict(zip(order, size))

    def col(m, name):
        return m[..., at[name]:at[name] + size[name]]
    z_order = "lru_x nsa_q k_slc k_win fox_q fox_k v_slc v_win fox_v k_cmp v_cmp".split()

    def z_columns(m):
        by_head = col(m, "bgate").reshape(m.shape[:-1] + (8, 3))[..., [1, 2, 0]].reshape(m.shape[:-1] + (24,))
        gates = pad_to(np.concatenate([by_head, col(m, "fox_f")], -1), P)
        return np.concatenate([col(m, n) for n in z_order] + [gates] + [col(m, n) for n in ("lru_gate", "nsa_gate", "fox_gate")], -1)
    out["w_z"] = blocks(z_columns(w))
    out["w_mod"] = v["w_mod_2"][0].T.reshape(N_MOD, P, D)
    out["cond"] = np.broadcast_to(np.concatenate([v["c_2"][0], v["c_ctx_2"]]), (P, 2 * D))
    bz = z_columns(b)
    mg = blocks(col(w, "merge")).reshape(3, DC, P, D)
    wb = np.stack([blocks(v["w_branch"][0, j]) for j in range(3)])
    out["w_merge"] = np.concatenate([mg, wb], -1).transpose(1, 0, 2, 3).reshape(48, P, 3072)
    b_merge = col(b, "merge").reshape(3, DC, P).transpose(2, 1, 0).reshape(P, 48)
    pair = np.zeros((2, 8, P, P), np.float32)
    for j, name in enumerate(("lru_wa", "lru_wx")):
        m = v[name][0].reshape(8, 2, 64, 64)
        pair[j, :, :64, :64], pair[j, :, 64:, 64:] = m[:, 0], m[:, 1]
    out["w_lru"] = pair.transpose(1, 2, 0, 3).reshape(8, P, 256)
    out["w_cmp"] = v["cmp_w1"][0].reshape(2, 4, 8, P, 256).transpose(0, 1, 3, 2, 4).reshape(8, P, 2048)
    out["w_out"] = blocks(v["w_out"][0])
    out["w_ple"] = v["w_ple"][0].reshape(2, P, 2, 1024).transpose(2, 1, 0, 3).reshape(2, P, 2048)
    out["w_ple_gate"] = blocks(v["w_ple_gate"][0])
    out["misc"] = np.concatenate([v["cmp_w2"][0].reshape(4, P, P).transpose(1, 0, 2).reshape(P, 512),
                                  v["peer_sub_keys_2"][0].transpose(2, 0, 1).reshape(P, 256)], 1)
    out["x"], out["ctx"], out["p"] = tokens_last(v["x"][0]), tokens_last(v["ctx_2"][0]), tokens_last(v["p"][0, 0])

    w = v["w_in_2"][0]
    sizes = (512, 256, 64, 3072, 1024, 8, 8, 8, 8, 2048, 2048)
    cq, ckv, kr, qkv, zz, af, ab, bf, bb, ga, gate_b = np.split(w, np.cumsum(sizes)[:-1], axis=1)
    small = np.zeros((D, P), np.float32)
    small[:, 64:72], small[:, 72:80], small[:, 96:104], small[:, 104:112] = af, ab, bf, bb
    out["w_y"] = blocks(np.concatenate([ckv, qkv[:, 1024:], pad_to(kr, P), small], 1))
    out["w_l"] = blocks(np.concatenate([cq, qkv[:, :1024], zz], 1))
    uq = v["w_uq_2"][0].reshape(4, P, 8, 192).transpose(2, 1, 0, 3).reshape(8, P, 768)
    ukv = v["w_ukv_2"][0].reshape(2, P, 8, 256).transpose(2, 1, 0, 3).reshape(8, P, 512)
    out["w_mla"] = np.concatenate([uq, ukv], -1)
    g2 = np.stack([blocks(ga), blocks(gate_b)])
    b2 = np.stack([blocks(v["w_branch_a_2"][0]), blocks(v["w_branch_b_2"][0])])
    out["w_merge2"] = np.concatenate([g2, b2], -1).transpose(1, 0, 2, 3).reshape(32, P, 3072)
    out["w_out2"] = blocks(v["w_out_2"][0])
    out["w_peer_q"] = blocks(v["peer_w_q_2"][0])
    out["u"] = blocks(v["peer_u_2"][0].T)
    out["v"] = v["peer_v_2"][0].reshape(KEYS, P, D)

    ab_rows = np.zeros((2, P, 1), np.float32)
    ab_rows[0, 64:80, 0] = v["dn_a_log_2"][0].reshape(16)
    ab_rows[1, 64:80, 0] = v["dn_dt_bias_2"][0].reshape(16)
    conv = v["conv_w"][0].reshape(4, 8, P).transpose(2, 0, 1).reshape(P, 32)
    conv2 = v["dn_conv_w_2"][0].reshape(5, 24, P).transpose(2, 0, 1).reshape(P, 120)
    gains = np.concatenate([np.repeat(v[n][0][:, None], c, 1) for n, c in
                            (("nsa_q_gain", 8), ("nsa_k_gain", 4), ("fox_q_gain", 8), ("fox_k_gain", 8))], 1)
    p = {"b_merge": b_merge, "lru_ba": columns(v["lru_ba"][0]), "lru_bx": columns(v["lru_bx"][0]),
         "eps": np.full((P, 1), EPS, np.float32), "ln_gain": columns(v["ln_gain"][0]), "b_in": columns(bz),
         "conv_w": conv, "conv_b": columns(v["conv_b"][0]), "lam": columns(v["lru_lambda"][0]),
         "pos": v["cmp_pos"][0].transpose(2, 0, 1).reshape(P, 64), "qk_gain": gains,
         "cmp_gain": v["nsa_k_gain"][0][:, None], "ple_gain": columns(v["ple_gain"][0]), "b_mod": columns(v["b_mod_2"][0]),
         "norm1": columns(v["norm1_w_2"][0]), "q_norm": columns(v["mla_q_norm_w_2"][0]),
         "kv_norm": columns(v["mla_kv_norm_w_2"][0]), "conv2_w": conv2, "a_log": ab_rows[0], "dt_bias": ab_rows[1],
         "dn_norm": v["dn_norm_w_2"][0][:, None], "norm2": columns(v["norm2_w_2"][0]),
         "final_norm": columns(v["final_norm_w_2"])}
    out["params"] = np.concatenate([p[n] for n in PARAMS], 1)
    out["consts"], out["dn_consts"], out["peer_consts"] = constants()
    return {k: np.ascontiguousarray(x) for k, x in out.items()}


def kernel(**inputs):
    import concourse.bacc as bacc
    from concourse.bass_utils import run_bass_kernel_spmd

    nc = bacc.Bacc("TRN2", target_bir_lowering=False, num_devices=1)
    arrays = lay_out(inputs)
    args = {k: nc.dram_tensor(f"{k}_dram", x.shape, F32, kind="ExternalInput").ap() for k, x in arrays.items()}
    args["out"] = nc.dram_tensor("out_dram", (P, DC * T), F32, kind="ExternalOutput").ap()
    args["experts"] = nc.dram_tensor("experts_dram", (4, P, KEYS, 64), F32, kind="Internal").ap()
    build(nc, args)
    r = run_bass_kernel_spmd(nc, [{f"{k}_dram": x for k, x in arrays.items()}], core_ids=[0])
    out = r.results[0]["out_dram"]
    return out.reshape(P, DC, T).transpose(2, 1, 0).reshape(1, T, D)
```
